# Optimizing a Trainium2 kernel written in Bass

```python
import math
import jax, jax.numpy as jnp
from jax import lax
import numpy as np

D_MODEL = 1024
BATCH = 1
SEQ = 256
DEPTH = 2

MIX_WIDTH = D_MODEL
DN_HEAD_DIM = 128
DN_WIDTH = D_MODEL // 2
DN_HEADS = DN_WIDTH // DN_HEAD_DIM
SB_HEAD_DIM = 64
SB_WIDTH = MIX_WIDTH - DN_WIDTH
SB_HEADS = SB_WIDTH // SB_HEAD_DIM
CONV_K = 4
CHUNK = 64
SB_BLOCK = 128
D_FF = 2816
N_EXPERTS = 8
TOP_K = 2
D_FF_EXPERT = 3584
N_DENSE = (DEPTH + 1) // 2
N_MOE = DEPTH // 2
EPS = 1e-6
IN_SPLITS = (DN_WIDTH, DN_WIDTH, DN_WIDTH, DN_WIDTH, DN_HEADS, DN_HEADS, SB_WIDTH, SB_WIDTH, SB_WIDTH)
P_IN = sum(IN_SPLITS)

kernel_name = "hybrid_deltanet_stickbreaking_moe"

def rms_norm(x, w):
    xf = x.astype(jnp.float32)
    y = xf * lax.rsqrt(jnp.mean(xf * xf, axis=-1, keepdims=True) + EPS)
    return (y * w.astype(jnp.float32)).astype(x.dtype)

def l2_normalize(x):
    return x * lax.rsqrt(jnp.sum(x * x, axis=-1, keepdims=True) + EPS)

def causal_depthwise_conv(x, w):
    return lax.conv_general_dilated(
        x, w[:, None, :].astype(x.dtype), window_strides=(1,), padding=((CONV_K - 1, 0),),
        dimension_numbers=("NWC", "WIO", "NWC"), feature_group_count=x.shape[-1])

def chunk_gated_delta_rule(q, k, v, beta, g):
    B, T, H, dk = q.shape
    dv = v.shape[-1]
    N = T // CHUNK
    q = l2_normalize(q) * (dk ** -0.5)
    k = l2_normalize(k)

    def to_chunks(a):
        return a.reshape(B, N, CHUNK, H, a.shape[-1]).transpose(0, 3, 1, 2, 4)

    q, k, v = to_chunks(q), to_chunks(k), to_chunks(v)
    beta = beta.reshape(B, N, CHUNK, H).transpose(0, 3, 1, 2)
    g = jnp.cumsum(g.reshape(B, N, CHUNK, H).transpose(0, 3, 1, 2), axis=-1)

    tril = jnp.tril(jnp.ones((CHUNK, CHUNK), dtype=bool))
    strict = jnp.tril(jnp.ones((CHUNK, CHUNK), dtype=bool), -1)
    decay = jnp.exp(jnp.where(tril, g[..., :, None] - g[..., None, :], -jnp.inf))

    k_beta = k * beta[..., None]
    v_beta = v * beta[..., None]
    L = jnp.where(strict, jnp.einsum("bhncd,bhnsd->bhncs", k_beta, k) * decay, 0.0)
    eye = jnp.eye(CHUNK, dtype=q.dtype)
    rhs = jnp.concatenate([v_beta, k_beta * jnp.exp(g)[..., None]], axis=-1)
    sol = lax.linalg.triangular_solve(L + eye, rhs, left_side=True, lower=True, unit_diagonal=True)
    u, w = sol[..., :dv], sol[..., dv:]

    attn = jnp.einsum("bhncd,bhnsd->bhncs", q, k) * decay
    g_last = g[..., -1]
    q_decay = q * jnp.exp(g)[..., None]
    k_to_end = k * jnp.exp(g_last[..., None] - g)[..., None]

    def step(S, inp):
        qd, kd, u_i, w_i, a_i, gl = inp
        v_new = u_i - jnp.einsum("bhcd,bhde->bhce", w_i, S)
        o = jnp.einsum("bhcd,bhde->bhce", qd, S) + jnp.einsum("bhcs,bhse->bhce", a_i, v_new)
        S = S * jnp.exp(gl)[..., None, None] + jnp.einsum("bhcd,bhce->bhde", kd, v_new)
        return S, o

    xs = tuple(jnp.moveaxis(a, 2, 0) for a in (q_decay, k_to_end, u, w, attn, g_last))
    S0 = jnp.zeros((B, H, dk, dv), dtype=q.dtype)
    _, o = lax.scan(step, S0, xs)
    return o.transpose(1, 0, 3, 2, 4).reshape(B, T, H, dv)

def gated_deltanet(dq, dk_, dv_, dz, db, da, conv_w, a_log, dt_bias, norm_w):
    B, T, _ = dq.shape
    qkv = jax.nn.silu(causal_depthwise_conv(jnp.concatenate([dq, dk_, dv_], axis=-1), conv_w))
    qkv = qkv.astype(jnp.float32)
    q, k, v = jnp.split(qkv, 3, axis=-1)
    q = q.reshape(B, T, DN_HEADS, DN_HEAD_DIM)
    k = k.reshape(B, T, DN_HEADS, DN_HEAD_DIM)
    v = v.reshape(B, T, DN_HEADS, DN_HEAD_DIM)
    beta = jax.nn.sigmoid(db.astype(jnp.float32))
    g = -jnp.exp(a_log.astype(jnp.float32)) * jax.nn.softplus(
        da.astype(jnp.float32) + dt_bias.astype(jnp.float32))
    o = chunk_gated_delta_rule(q, k, v, beta, g)
    z = dz.astype(jnp.float32).reshape(B, T, DN_HEADS, DN_HEAD_DIM)
    o = rms_norm(o, norm_w) * jax.nn.silu(z)
    return o.reshape(B, T, DN_WIDTH).astype(dq.dtype)

def stick_breaking_attention(q, k, v):
    B, T, H, d = q.shape
    nb = T // SB_BLOCK
    qb = q.astype(jnp.float32).reshape(B, nb, SB_BLOCK, H, d).transpose(1, 0, 3, 2, 4)
    kh = k.astype(jnp.float32).transpose(0, 2, 1, 3)
    vh = v.astype(jnp.float32).transpose(0, 2, 1, 3)
    k_pos = jnp.arange(T, dtype=jnp.int32)
    scale = d ** -0.5

    def block(args):
        q_blk, start = args
        z = jnp.einsum("bhqd,bhkd->bhqk", q_blk, kh) * scale
        q_pos = start + jnp.arange(SB_BLOCK, dtype=jnp.int32)
        mask = k_pos[None, :] < q_pos[:, None]
        log_keep = jnp.where(mask, jax.nn.log_sigmoid(-z), 0.0)
        between = lax.cumsum(log_keep, axis=3, reverse=True) - log_keep
        weight = jnp.where(mask, jnp.exp(jax.nn.log_sigmoid(z) + between), 0.0)
        return jnp.einsum("bhqk,bhkd->bhqd", weight, vh)

    starts = jnp.arange(nb, dtype=jnp.int32) * SB_BLOCK
    o = lax.map(block, (qb, starts))
    return o.transpose(1, 0, 3, 2, 4).reshape(B, T, H, d)

def hybrid_mixer(h, w_in, conv_w, a_log, dt_bias, dn_norm_w, sb_norm_w, w_out):
    B, T, _ = h.shape
    proj = jnp.einsum("btd,dp->btp", h, w_in)
    split_points = [int(s) for s in np.cumsum(IN_SPLITS)[:-1]]
    dq, dk_, dv_, dz, db, da, sq, sk, sv = jnp.split(proj, split_points, axis=-1)
    dn_out = gated_deltanet(dq, dk_, dv_, dz, db, da, conv_w, a_log, dt_bias, dn_norm_w)
    sb = stick_breaking_attention(sq.reshape(B, T, SB_HEADS, SB_HEAD_DIM),
                                  sk.reshape(B, T, SB_HEADS, SB_HEAD_DIM),
                                  sv.reshape(B, T, SB_HEADS, SB_HEAD_DIM))
    sb_out = rms_norm(sb, sb_norm_w).reshape(B, T, SB_WIDTH).astype(h.dtype)
    mixed = jnp.concatenate([dn_out, sb_out], axis=-1)
    return jnp.einsum("btm,md->btd", mixed, w_out)

def swiglu(x, w_gate, w_up, w_down):
    return (jax.nn.silu(x @ w_gate) * (x @ w_up)) @ w_down

def moe_swiglu(h, router_w, w_gate, w_up, w_down):
    B, T, D = h.shape
    xt = h.reshape(B * T, D)
    logits = (xt @ router_w).astype(jnp.float32)
    top_val, top_idx = lax.top_k(logits, TOP_K)
    gates = jax.nn.softmax(top_val, axis=-1)
    combine = jnp.einsum("nk,nke->ne", gates, jax.nn.one_hot(top_idx, N_EXPERTS, dtype=jnp.float32))
    y = jnp.zeros((B * T, D), dtype=jnp.float32)
    for e in range(N_EXPERTS):
        y = y + combine[:, e:e + 1] * swiglu(xt, w_gate[e], w_up[e], w_down[e]).astype(jnp.float32)
    return y.reshape(B, T, D).astype(h.dtype)

def setup_inputs(seed: int = 0) -> dict:
    key = jax.random.key(seed)
    ks = jax.random.split(key, 19)

    def normal(k, shape, scale):
        return jax.random.normal(k, shape, jnp.float32) * scale

    def gain(k, shape):
        return 1.0 + 0.05 * jax.random.normal(k, shape, jnp.float32)

    x = normal(ks[0], (BATCH, SEQ, D_MODEL), 1.0)
    norm_mix_pre = gain(ks[1], (DEPTH, D_MODEL))
    norm_mix_post = gain(ks[2], (DEPTH, D_MODEL))
    norm_ffn_pre = gain(ks[3], (DEPTH, D_MODEL))
    norm_ffn_post = gain(ks[4], (DEPTH, D_MODEL))
    w_in = normal(ks[5], (DEPTH, D_MODEL, P_IN), D_MODEL ** -0.5)
    conv_w = normal(ks[6], (DEPTH, CONV_K, 3 * DN_WIDTH), CONV_K ** -0.5)
    dn_a_log = jnp.log(jax.random.uniform(ks[7], (DEPTH, DN_HEADS), jnp.float32, 1.0, 16.0))
    dt = jnp.exp(jax.random.uniform(ks[8], (DEPTH, DN_HEADS), jnp.float32, math.log(1e-3), math.log(1e-1)))
    dn_dt_bias = dt + jnp.log(-jnp.expm1(-dt))
    dn_norm_w = gain(ks[9], (DEPTH, DN_HEAD_DIM))
    sb_norm_w = gain(ks[10], (DEPTH, SB_HEAD_DIM))
    w_out = normal(ks[11], (DEPTH, MIX_WIDTH, D_MODEL), MIX_WIDTH ** -0.5)
    ffn_w_gate = normal(ks[12], (N_DENSE, D_MODEL, D_FF), D_MODEL ** -0.5)
    ffn_w_up = normal(ks[13], (N_DENSE, D_MODEL, D_FF), D_MODEL ** -0.5)
    ffn_w_down = normal(ks[14], (N_DENSE, D_FF, D_MODEL), D_FF ** -0.5)
    router_w = normal(ks[15], (N_MOE, D_MODEL, N_EXPERTS), D_MODEL ** -0.5)
    moe_w_gate = normal(ks[16], (N_MOE, N_EXPERTS, D_MODEL, D_FF_EXPERT), D_MODEL ** -0.5)
    moe_w_up = normal(ks[17], (N_MOE, N_EXPERTS, D_MODEL, D_FF_EXPERT), D_MODEL ** -0.5)
    moe_w_down = normal(ks[18], (N_MOE, N_EXPERTS, D_FF_EXPERT, D_MODEL), D_FF_EXPERT ** -0.5)
    return {"x": x, "norm_mix_pre": norm_mix_pre, "norm_mix_post": norm_mix_post,
            "norm_ffn_pre": norm_ffn_pre, "norm_ffn_post": norm_ffn_post, "w_in": w_in,
            "conv_w": conv_w, "dn_a_log": dn_a_log, "dn_dt_bias": dn_dt_bias, "dn_norm_w": dn_norm_w,
            "sb_norm_w": sb_norm_w, "w_out": w_out, "ffn_w_gate": ffn_w_gate, "ffn_w_up": ffn_w_up,
            "ffn_w_down": ffn_w_down, "router_w": router_w, "moe_w_gate": moe_w_gate,
            "moe_w_up": moe_w_up, "moe_w_down": moe_w_down}

def reference(x, norm_mix_pre, norm_mix_post, norm_ffn_pre, norm_ffn_post, w_in, conv_w,
              dn_a_log, dn_dt_bias, dn_norm_w, sb_norm_w, w_out, ffn_w_gate, ffn_w_up, ffn_w_down,
              router_w, moe_w_gate, moe_w_up, moe_w_down):
    for layer in range(DEPTH):
        h = rms_norm(x, norm_mix_pre[layer])
        h = hybrid_mixer(h, w_in[layer], conv_w[layer], dn_a_log[layer], dn_dt_bias[layer],
                         dn_norm_w[layer], sb_norm_w[layer], w_out[layer])
        x = x + rms_norm(h, norm_mix_post[layer])
        h = rms_norm(x, norm_ffn_pre[layer])
        if layer % 2 == 0:
            i = layer // 2
            h = swiglu(h, ffn_w_gate[i], ffn_w_up[i], ffn_w_down[i])
        else:
            i = layer // 2
            h = moe_swiglu(h, router_w[i], moe_w_gate[i], moe_w_up[i], moe_w_down[i])
        x = x + rms_norm(h, norm_ffn_post[layer])
    return x


_drawn_inputs = setup_inputs


def setup_inputs(seed=0):
    import zlib

    import numpy as np

    out = dict(_drawn_inputs(seed))
    spreads = {}
    factors = {}
    for name, (base, spread) in spreads.items():
        noise = np.random.default_rng([zlib.crc32(name.encode()), seed]).standard_normal(out[name].shape)
        drawn = base * np.exp(spread * noise) if base else spread * noise
        out[name] = __import__('jax').numpy.asarray(drawn.astype(out[name].dtype))
    for name, factor in factors.items():
        out[name] = (out[name] * factor).astype(out[name].dtype)
    return out
```

```python
from contextlib import ExitStack

import numpy as np

import concourse.bass as bass
from concourse import mybir

F32 = mybir.dt.float32
I32 = mybir.dt.int32
ALU = mybir.AluOpType
ACT = mybir.ActivationFunctionType
AX_X = mybir.AxisListType.X

P = 128
D = 1024
KD = D // P
T = 256
TT = T // P
DEPTH = 2
DN_H, DN_D = 4, 128
DN_W = DN_H * DN_D
SB_H, SB_D = 8, 64
NPR = TT * DN_H
D_FF = 2816
N_EXP = 8
FF_E = 3584
EPS = 1e-6
SLOTS = 96
ROUND_LIMITS = (SLOTS, 2 * SLOTS)

FC = 256
SLOT = 2 * KD * FC + (FC // P) * D
NSLOT = 4
PARTS = 3
LANDED = 16 * PARTS
FFN_CH = D_FF // FC
MOE_CH = FF_E // FC
IN_CUTS = (0, 768, 1536, 2056, 2568, 3080, 3592)
N_IN = len(IN_CUTS) - 1
N_MIX = N_IN + 2
FIRST_FFN = N_MIX
FIRST_MIX = (0, N_MIX + FFN_CH)
FIRST_MOE = 2 * N_MIX + FFN_CH
N_STEPS = 25
LEVELS = 7

C_ID = 0
C_UINC = C_ID + P
C_TRI = C_UINC + P
C_SB = C_TRI + P
C_LVL = C_SB + 3 * P
C_IOTA = C_LVL + LEVELS * P
C_W8 = C_IOTA + SLOTS
C_ALL = C_W8 + N_EXP

CONV_K = 4
CONV_T = 3 * DN_W // P
CONV_ROWS = DEPTH * CONV_K * CONV_T
R_MIX, R_FFN, R_DN, R_SB = 0, DEPTH * KD, 2 * DEPTH * KD, 2 * DEPTH * KD + DEPTH
NORM_ROWS = 2 * DEPTH * KD + 2 * DEPTH


def proj_steps():
    s = []
    for m in range(CONV_T):
        s.append(("conv", m, m // 6, (m % 6) * P))
    s += [("z", 0, 2, 0), ("z", 1, 2, 0), ("ba", 0, 2, DN_W)]
    s += [("sq", i, 3, i * P) for i in range(4)]
    s += [("sk", i, 4, i * P) for i in range(4)]
    s += [("sv", 0, 5, 0), ("sv", 1, 5, 0)]
    return s


STEPS = proj_steps()
LAST_STEP = {max(n for n, s in enumerate(STEPS) if s[2] == c): c for c in range(N_IN)}


def build(nc, x_in, consts, norm_mix_pre, norm_mix_post, norm_ffn_pre, norm_ffn_post, w_in, conv_w,
          dn_a_log, dn_dt_bias, dn_norm_w, sb_norm_w, w_out, ffn_gate, ffn_up, ffn_down, router_w,
          moe_gate, moe_up, moe_down, out):
    with ExitStack() as ctx:
        def sb(name, cols, dt=F32):
            return ctx.enter_context(nc.sbuf_tensor(name, [P, cols], dt))

        def sem(name):
            return ctx.enter_context(nc.semaphore(name))

        ps = ctx.enter_context(nc.psum_tensor("ps", [P, 8, 512], F32))

        def bank(b, n=1):
            return ps[:, b:b + n, :].rearrange("p b c -> p (b c)")

        ring = sb("ring", NSLOT * SLOT)
        cst = sb("cst", C_ALL)
        prm = sb("prm", CONV_ROWS + NORM_ROWS)
        headp = sb("headp", 2 * DEPTH * DN_H)
        routw = sb("routw", KD * N_EXP)
        x_sb = sb("x_sb", TT * D)
        h_sb = sb("h_sb", TT * D)
        wt_hT = sb("wt_hT", D + TT * D)
        wpost = sb("wpost", D)
        qk_sb = sb("qk_sb", DN_H * 2 * T)
        bv_sb = sb("bv_sb", NPR * P)
        kend_sb = sb("kend_sb", DN_H * P)
        sbq = sb("sbq", 4 * T)
        sbk = sb("sbk", 4 * T)
        DR_sb = sb("DR_sb", NPR * P)
        LT_sb = sb("LT_sb", NPR * P)
        AT_sb = sb("AT_sb", NPR * P)
        X_sb = sb("X_sb", NPR * P)
        XT_sb = sb("XT_sb", NPR * P)
        BM = sb("BM", 2 * NPR * P)
        Vn_sb = sb("Vn_sb", 2 * DN_H * P)
        SR = sb("SR", 2 * DN_H * P)
        sbz = sb("sbz", 2 * 3 * P)
        sbe = sb("sbe", 3 * P)
        sbp = sb("sbp", 2 * 3 * P)
        small = sb("small", 416)
        rounds_i = sb("rounds_i", 1, I32)

        def v3(t, a, lo=0, n=None):
            n = n or t.shape[1] - lo
            return t[:, lo:lo + n].rearrange("p (a b) -> p a b", a=a)

        ident = cst[:, C_ID:C_ID + P]
        uinc = cst[:, C_UINC:C_UINC + P]
        tri = cst[:, C_TRI:C_TRI + P]
        sbmask = cst[:, C_SB:C_SB + 3 * P]
        ustrict = cst[:, C_SB:C_SB + P]
        ones = cst[:, C_SB + P:C_SB + 2 * P]
        iota = cst[:, C_IOTA:C_IOTA + SLOTS]
        w8 = cst[:, C_W8:C_W8 + N_EXP]
        xv = v3(x_sb, TT)
        hv = v3(h_sb, TT)
        hT = v3(wt_hT, KD, D)
        mixT = hT
        wT = v3(wt_hT, SB_H)
        qk = qk_sb[:, :].rearrange("p (h k t) -> p h k t", h=DN_H, k=2)
        vT = v3(X_sb, DN_H)
        bv = v3(bv_sb, NPR)
        kend = v3(kend_sb, DN_H)
        sq_v, sk_v = v3(sbq, 4), v3(sbk, 4)
        DR, LT, AT, X, XT = (v3(t, NPR) for t in (DR_sb, LT_sb, AT_sb, X_sb, XT_sb))
        DF = XT
        diag_g, diag_b = LT, AT
        BT = v3(BM, NPR, 0, NPR * P)
        M1 = v3(BM, NPR, NPR * P, NPR * P)
        squares = v3(BM, 8)
        Vn = v3(Vn_sb, NPR)
        S = v3(SR, DN_H, 0, DN_H * P)
        RH1 = v3(SR, DN_H, DN_H * P, DN_H * P)
        zm = v3(sbz, 2)
        sp = v3(sbp, 2)
        dn_o = v3(LT_sb, TT)
        dn_sq = v3(AT_sb, TT)
        post_tmp = DR_sb[:, :]
        act_junk = (XT_sb[:, :], X_sb[:, :])
        rows = BM
        wpost_ffn = sbq[:, :]

        at = [0]

        def cols(n):
            at[0] += n
            return small[:, at[0] - n:at[0]]

        ssx, rsx = cols(TT), cols(TT)
        mhalf = cols(16)
        negA = cols(2 * DN_H)
        nsum, rn = cols(16), cols(16)
        ba = cols(16)
        aa, sabs, sln, spl, g_log = cols(8), cols(8), cols(8), cols(8), cols(8)
        eb, beta = cols(8), cols(8)
        gsum = cols(16)
        gdiff, egl, kcoef = cols(4), cols(4), cols(4)
        eg, scoef, coefq, br = cols(8), cols(4), cols(8), cols(8)
        dss, drs = cols(8), cols(8)
        sss, srs = cols(16), cols(16)
        lg, sel1, sel2, lg2, cand, sel, gate, rank = (cols(16) for _ in range(8))
        m1, m2, mx, ge, gd, g1, g2 = (cols(2) for _ in range(7))
        cmax, cgt, ctwo = cols(1), cols(1), cols(1)
        cur_rank, cur_gate = cols(2 * TT), cols(2 * TT)
        assert at[0] <= 416
        rk, rq = rn[:, 0:8], rn[:, 8:16]

        ffn_hid = v3(LT_sb, 4)
        ffn_sg = v3(AT_sb, 4)
        moe_y = qk_sb
        moe_yv = v3(qk_sb, TT)
        xgT = v3(bv_sb, KD, 0, KD * SLOTS)
        onehot = [v3(AT_sb, TT, j * TT * SLOTS, TT * SLOTS) for j in range(2)]
        onehotT = [X_sb[0:SLOTS, j * T:(j + 1) * T] for j in range(2)]
        moe_sg = [v3(LT_sb, 2, j * 2 * SLOTS, 2 * SLOTS) for j in range(2)]
        moe_hid = [v3(LT_sb, 2, (2 + j) * 2 * SLOTS, 2 * SLOTS) for j in range(2)]
        yT = v3(BM, KD, 0, KD * SLOTS)
        y_tok = BM[0:SLOTS, D:2 * D]

        ring_landed = [sem(f"ring_landed{i}") for i in range(NSLOT)]
        ring_used = sem("ring_used")
        x_landed, consts_landed, rows_landed, heads_landed, router_landed = (
            sem(n) for n in ("x_landed", "consts_landed", "rows_landed", "heads_landed", "router_landed"))
        wpost_landed, wpostf_landed, out_landed = (sem(n) for n in ("wpost_landed", "wpostf_landed", "out_landed"))
        params_ps, params_ready, half_ready, expA, negA_ready = (
            sem(n) for n in ("params_ps", "params_ready", "half_ready", "expA", "negA_ready"))
        ss_ready, rstd_mean, rstd_ready, h_ready = (
            sem(n) for n in ("ss_ready", "rstd_mean", "rstd_ready", "h_ready"))
        hT_ps, hT_dve, hT_act = (sem(n) for n in ("hT_ps", "hT_dve", "hT_act"))
        proj_done, conv_base, conv_taps, conv_silu, qk_squares, z_gate, ba_copied, sb_copied = (
            sem(n) for n in ("proj_done", "conv_base", "conv_taps", "conv_silu", "qk_squares", "z_gate",
                             "ba_copied", "sb_copied"))
        norms_ps, norms_sum, norms_ready, v_ps, kT_ps = (
            sem(n) for n in ("norms_ps", "norms_sum", "norms_ready", "v_ps", "kT_ps"))
        gate_in, gate_exp, gates_ready, gcum_ps, gcum_ready, gexp_ready, coef_ready, bv_ready, kend_ready = (
            sem(n) for n in ("gate_in", "gate_exp", "gates_ready", "gcum_ps", "gcum_ready", "gexp_ready",
                             "coef_ready", "bv_ready", "kend_ready"))
        diag_ready, bc_ps, decay_in, decay_exp, decay_ready, betadecay_ready, kk_ps, LT_ready, AT_ready = (
            sem(n) for n in ("diag_ready", "bc_ps", "decay_in", "decay_exp", "decay_ready",
                             "betadecay_ready", "kk_ps", "LT_ready", "AT_ready"))
        BT_ready, M1_ps, M1_ready, XM_ps, XTM_ps, X_ready, XT_ready = (
            sem(n) for n in ("BT_ready", "M1_ps", "M1_ready", "XM_ps", "XTM_ps", "X_ready", "XT_ready"))
        vnew_ps, vnew_ready, state_ps, state_ready, ks_ps, rhs1_ready, dno_ps = (
            sem(n) for n in ("vnew_ps", "vnew_ready", "state_ps", "state_ready", "ks_ps", "rhs1_ready", "dno_ps"))
        dn_out, dn_rstd_in, dn_rstd, mixed_dn = (sem(n) for n in ("dn_out", "dn_rstd_in", "dn_rstd", "mixed_dn"))
        sbz_ps, sbz_ready, sb_soft, sb_softplus, sb_keep, sbc_ps, sb_expo, sb_weight, sb_wmask, sbo_ps = (
            sem(n) for n in ("sbz_ps", "sbz_ready", "sb_soft", "sb_softplus", "sb_keep", "sbc_ps", "sb_expo",
                             "sb_weight", "sb_wmask", "sbo_ps"))
        sb_sq, sb_ss, sb_rstd_in, sb_rstd, mixed_sb = (
            sem(n) for n in ("sb_sq", "sb_ss", "sb_rstd_in", "sb_rstd", "mixed_sb"))
        mixT_ps, mixT_dve, mixT_act, out_t0 = (sem(n) for n in ("mixT_ps", "mixT_dve", "mixT_act", "out_t0"))
        post_ss, post_mean, post_rstd, post_scaled, x_ready = (
            sem(n) for n in ("post_ss", "post_mean", "post_rstd", "post_scaled", "x_ready"))
        gu_ps, sg_ready, hid_ready, down_done = (sem(n) for n in ("gu_ps", "sg_ready", "hid_ready", "down_done"))
        router_ps, route_step, route_exp, sel_ready, rank_ps, rounds_ready, moe_zero = (
            sem(n) for n in ("router_ps", "route_step", "route_exp", "sel_ready", "rank_ps", "rounds_ready",
                             "moe_zero"))
        cur_ready, onehot_ready, gather_ps, xg_ready, ohT_ps, ohT_ready = (
            sem(n) for n in ("cur_ready", "onehot_ready", "gather_ps", "xg_ready", "ohT_ps", "ohT_ready"))
        mgu_ps, msg_ready, mhid_ready, yT_ready, y_ps, y_act, y_dve, scatter_ps, moe_acc = (
            sem(n) for n in ("mgu_ps", "msg_ready", "mhid_ready", "yT_ready", "y_ps", "y_act", "y_dve",
                             "scatter_ps", "moe_acc"))

        def bcl(ap, n):
            return ap.unsqueeze(2).broadcast_to([ap.shape[0], ap.shape[1], n])

        def bcm(ap, n):
            return ap.unsqueeze(1).broadcast_to([ap.shape[0], n, ap.shape[1]])

        def slot_of(n):
            return ring[:, (n % NSLOT) * SLOT:(n % NSLOT + 1) * SLOT]

        def chunk_landed(eng, n, extra=0):
            eng.wait_ge(ring_landed[n % NSLOT], extra + LANDED * (n // NSLOT + 1))

        def gate_up_down(n):
            s = slot_of(n)
            g = s[:, 0:KD * FC].rearrange("p (k f) -> p k f", k=KD)
            u = s[:, KD * FC:2 * KD * FC].rearrange("p (k f) -> p k f", k=KD)
            d = s[:, 2 * KD * FC:SLOT].rearrange("p (i d) -> p i d", i=FC // P)
            return g, u, d

        def in_cols(n, width):
            return slot_of(n)[:, 0:KD * width].rearrange("p (k c) -> p k c", k=KD)

        def step_sem(L, n):
            if n in LAST_STEP:
                return ring_used, FIRST_MIX[L] + LAST_STEP[n] + 1
            before = sum(1 for m in range(n) if m not in LAST_STEP)
            return proj_done, (N_STEPS - N_IN) * L + before + 1

        def post_source(u):
            return (out_t0, ring_used)

        block = ctx.enter_context(nc.Block())

        @block.sync
        def _(sp_):
            sp_.dma_start(xv, x_in[0].rearrange("(t p) d -> p t d", p=P)).then_inc(x_landed, 16)
            sp_.dma_start(cst[:, :], consts).then_inc(consts_landed, 16)

            def free_slot(n):
                if n >= NSLOT:
                    sp_.wait_ge(ring_used, n - NSLOT + 1)

            def load_rows(n, src, width):
                free_slot(n)
                dst = in_cols(n, width)
                src = src.rearrange("(k p) c -> p k c", p=P)
                for a, b in ((0, 3), (3, 6), (6, 8)):
                    sp_.dma_start(dst[:, a:b, :], src[:, a:b, :]).then_inc(ring_landed[n % NSLOT], 16)

            def load_mixer(L):
                for c in range(N_IN):
                    load_rows(FIRST_MIX[L] + c, w_in[L][:, IN_CUTS[c]:IN_CUTS[c + 1]], IN_CUTS[c + 1] - IN_CUTS[c])
                for h in range(2):
                    load_rows(FIRST_MIX[L] + N_IN + h, w_out[L][:, h * 512:(h + 1) * 512], 512)

            def load_ffn(n, wg, wu, wd):
                g, u, d = gate_up_down(n)
                s = ring_landed[n % NSLOT]
                sp_.dma_start(g, wg.rearrange("(k p) f -> p k f", p=P)).then_inc(s, 16)
                sp_.dma_start(u, wu.rearrange("(k p) f -> p k f", p=P)).then_inc(s, 16)
                sp_.dma_start(d, wd.rearrange("(i p) d -> p i d", p=P)).then_inc(s, 16)

            load_mixer(0)
            for c in range(FFN_CH):
                free_slot(FIRST_FFN + c)
                f = slice(c * FC, (c + 1) * FC)
                load_ffn(FIRST_FFN + c, ffn_gate[0][:, f], ffn_up[0][:, f], ffn_down[0][f, :])
            load_mixer(1)

            def moe_pair(pair, it):
                for j in range(2):
                    for c in range(MOE_CH):
                        n = FIRST_MOE + j * MOE_CH + c
                        sp_.wait_ge(ring_used, it * (2 * MOE_CH) + (n - NSLOT + 1))
                        f = slice(c * FC, (c + 1) * FC)
                        e = pair * 2 + j
                        load_ffn(n, moe_gate[0, e][:, f], moe_up[0, e][:, f], moe_down[0, e][f, :])

            with sp_.Fori(0, N_EXP // 2) as pair:
                moe_pair(pair, pair)
            sp_.wait_ge(rounds_ready, 1)
            rounds = sp_.value_load(rounds_i[0:1, 0:1], min_val=1, max_val=3)
            with sp_.If(rounds > 1):
                with sp_.Fori(1, rounds) as r:
                    with sp_.Fori(0, N_EXP // 2) as pair:
                        moe_pair(pair, r * (N_EXP // 2) + pair)
            for t in range(TT):
                sp_.wait_ge(x_ready, 3 * TT + t + 1)
                sp_.dma_start(out[0].rearrange("(t p) d -> p t d", p=P)[:, t, :], xv[:, t, :]).then_inc(out_landed, 16)
            sp_.wait_ge(out_landed, 32)

        @block.tensor
        def _(pe):
            mm = nc.tensor.matmul

            pe.wait_ge(consts_landed, 16)
            pe.wait_ge(rows_landed, 16 * 6)
            nc.tensor.transpose(bank(4)[:, 0:CONV_ROWS], rows[0:CONV_ROWS, 0:P],
                                ident[0:CONV_ROWS, 0:CONV_ROWS])
            nc.tensor.transpose(bank(4)[:, CONV_ROWS:CONV_ROWS + NORM_ROWS], rows[0:NORM_ROWS, P:2 * P],
                                ident[0:NORM_ROWS, 0:NORM_ROWS]).then_inc(params_ps, 1)

            def transpose_h(u):
                pe.wait_ge(h_ready, TT * (u + 1))
                for b in range(4):
                    for k in (2 * b, 2 * b + 1):
                        for t in range(TT):
                            o = (k % 2) * T + t * P
                            i = nc.tensor.transpose(bank(b)[:, o:o + P], hv[:, t, k * P:(k + 1) * P], ident)
                    i.then_inc(hT_ps, 1)

            def hT_wait(u, k):
                pe.wait_ge(hT_act if k // 2 % 2 else hT_dve, 4 * u + 2 * (k // 4) + k % 2 + 1)

            def project(L, n):
                kind, i, c, col = STEPS[n]
                m = n - 4
                if m >= 0:
                    if m < CONV_T:
                        pe.wait_ge(conv_taps, 3 * (CONV_T * L + m + 1))
                    elif m < 14:
                        pe.wait_ge(z_gate, 2 * L + m - 11)
                    elif m == 14:
                        pe.wait_ge(ba_copied, L + 1)
                    else:
                        pe.wait_ge(sb_copied, 10 * L + m - 14)
                chunk = FIRST_MIX[L] + c
                chunk_landed(pe, chunk)
                w = in_cols(chunk, IN_CUTS[c + 1] - IN_CUTS[c])
                o = bank(4 + n % 4)
                if kind in ("conv", "sq", "sk"):
                    for k in range(KD):
                        if n == 0:
                            hT_wait(2 * L, k)
                        ins = mm(o[:, 0:T], w[:, k, col:col + P], hT[:, k, :], start=(k == 0), stop=(k == KD - 1))
                elif kind == "ba":
                    for t in range(TT):
                        for k in range(KD):
                            ins = mm(o[:, t * 8:(t + 1) * 8], hT[:, k, t * P:(t + 1) * P], w[:, k, col:col + 8],
                                     start=(k == 0), stop=(k == KD - 1))
                else:
                    for k in range(KD):
                        ins = mm(o, hT[:, k, i * P:(i + 1) * P], w[:, k, col:col + 512],
                                 start=(k == 0), stop=(k == KD - 1))
                ins.then_inc(step_sem(L, n)[0], 1)

            def sb_scores(L, h):
                if h >= 2:
                    pe.wait_ge(sb_expo, SB_H * L + h - 1)
                if h == 0:
                    pe.wait_ge(sb_copied, 10 * L + 10)
                r = (h % 2) * SB_D
                kh, qh = sk_v[r:r + SB_D, h // 2, :], sq_v[r:r + SB_D, h // 2, :]
                o = bank(6 + h % 2)
                mm(o[:, 0:T], kh[:, 0:P], qh[:, 0:T], start=True, stop=True)
                mm(o[:, T:T + P], kh[:, P:T], qh[:, P:T], start=True, stop=True).then_inc(sbz_ps, 1)

            def sb_cumsum(L, h):
                pe.wait_ge(sb_keep, SB_H * L + h + 1)
                o = bank(6 + h % 2)
                mm(o[:, 0:3 * P], tri, sp[:, h % 2, :], start=True, stop=True)
                mm(o[:, P:2 * P], ones, sp[:, h % 2, 2 * P:3 * P], start=False, stop=True,
                   skip_group_check=True).then_inc(sbc_ps, 1)

            def sb_output(L):
                pe.wait_ge(sb_wmask, SB_H * (L + 1))
                pe.wait_ge(sb_expo, SB_H * (L + 1))
                for t in range(TT):
                    for h in range(SB_H):
                        o = bank(6 + t)[:, h * SB_D:(h + 1) * SB_D]
                        v = [hv[:, s, DN_W + h * SB_D:DN_W + (h + 1) * SB_D] for s in range(TT)]
                        ins = mm(o, wT[:, h, t * P:(t + 1) * P], v[0], start=True, stop=(t == 0))
                        if t == 1:
                            ins = mm(o, wT[:, h, 2 * P:3 * P], v[1], start=False, stop=True)
                    ins.then_inc(sbo_ps, 1)

            def qk_norms(L):
                pe.wait_ge(qk_squares, 8 * (L + 1))
                for kind in range(2):
                    for t in range(TT):
                        for h in range(DN_H):
                            c = kind * 8 + t * DN_H + h
                            ins = mm(bank(0)[:, c:c + 1], squares[:, (1 - kind) * 4 + h, t * P:(t + 1) * P],
                                     ones[:, 0:1], start=True, stop=True)
                ins.then_inc(norms_ps, 1)

            def v_k_transposes(L):
                pe.wait_ge(conv_silu, CONV_T * (L + 1))
                for t in range(TT):
                    for h in range(DN_H):
                        ins = nc.tensor.transpose(bank(1 + t)[:, h * P:(h + 1) * P], vT[:, h, t * P:(t + 1) * P],
                                                  ident)
                    ins.then_inc(v_ps, 1)
                for h in range(DN_H):
                    ins = nc.tensor.transpose(bank(3)[:, h * P:(h + 1) * P], qk[:, h, 0, 0:P], ident)
                ins.then_inc(kT_ps, 1)

            def decay_sums(L):
                pe.wait_ge(gates_ready, 5 * (L + 1))
                pe.wait_ge(norms_sum, L + 1)
                mm(bank(0)[:, 16:24], uinc, g_log, start=True, stop=True)
                mm(bank(0)[:, 24:32], ones, g_log, start=True, stop=True).then_inc(gcum_ps, 1)

            def broadcasts(L):
                pe.wait_ge(gcum_ready, L + 1)
                pe.wait_ge(bv_ready, 2 * (L + 1))
                pe.wait_ge(kend_ready, L + 1)
                for n, dg in enumerate((diag_g, diag_b)):
                    pe.wait_ge(diag_ready, 2 * L + n + 1)
                    for b in range(2):
                        ins = mm(bank(2 * n + b), ones, dg[:, 4 * b:4 * b + 4, :], start=True, stop=True)
                    ins.then_inc(bc_ps, 1)

            def key_products(L):
                pe.wait_ge(decay_in, 8 * (L + 1))
                pe.wait_ge(betadecay_ready, 2 * (L + 1))
                for pr in range(NPR):
                    t, h = pr // DN_H, pr % DN_H
                    o = bank(pr // 2)[:, (pr % 2) * T:(pr % 2 + 1) * T]
                    ins = mm(o, qk[:, h, 0, t * P:(t + 1) * P], qk[:, h, :, t * P:(t + 1) * P],
                             start=True, stop=True)
                    if pr % 4 == 3:
                        ins.then_inc(kk_ps, 1)

            def level_product(L, l, g):
                pe.wait_ge(BT_ready, 2 * (LEVELS * L + l) + g + 1)
                if l == 0:
                    pe.wait_ge(AT_ready, 2 * (L + 1))
                    pe.wait_ge(LT_ready, 2 * (L + 1))
                else:
                    pe.wait_ge(X_ready, 2 * (6 * L + l - 1) + g + 1)
                    if l >= 2:
                        pe.wait_ge(M1_ready, 2 * (6 * L + l - 2) + g + 1)
                for pr in range(4 * g, 4 * g + 4):
                    rhs = ident if l == 0 else X[:, pr, :]
                    ins = mm(bank(g)[:, (pr % 4) * P:(pr % 4 + 1) * P], BT[:, pr, :], rhs, start=True, stop=True)
                ins.then_inc(M1_ps, 1)

            def level_update(L, l, g):
                pe.wait_ge(M1_ready, 2 * (6 * L + l - 1) + g + 1)
                pe.wait_ge(XT_ready, 2 * (LEVELS * L + l - 1) + g + 1)
                if l < LEVELS - 1:
                    for pr in range(4 * g, 4 * g + 4):
                        ins = mm(bank(2 + g)[:, (pr % 4) * P:(pr % 4 + 1) * P], XT[:, pr, :], M1[:, pr, :],
                                 start=True, stop=True)
                    ins.then_inc(XM_ps, 1)
                for pr in range(4 * g, 4 * g + 4):
                    ins = mm(bank(4 + g)[:, (pr % 4) * P:(pr % 4 + 1) * P], M1[:, pr, :], XT[:, pr, :],
                             start=True, stop=True)
                ins.then_inc(XTM_ps, 1)

            def per_head(b, lhs, rhs, signal):
                for h in range(DN_H):
                    ins = mm(bank(b)[:, h * P:(h + 1) * P], lhs(h), rhs(h), start=True, stop=True)
                if signal is not None:
                    ins.then_inc(signal, 1)

            def mixer(L):
                transpose_h(2 * L)
                for n in range(15):
                    project(L, n)
                qk_norms(L)
                v_k_transposes(L)
                for n in range(15, 19):
                    project(L, n)
                decay_sums(L)
                for n in range(19, 23):
                    project(L, n)
                broadcasts(L)
                for n in range(23, 25):
                    project(L, n)
                sb_scores(L, 0)
                key_products(L)
                sb_scores(L, 1)
                for l in range(LEVELS):
                    for g in range(2):
                        level_product(L, l, g)
                        if l and g == 0:
                            sb_cumsum(L, l - 1)
                    if l:
                        level_update(L, l, 0)
                        sb_scores(L, l + 1)
                        level_update(L, l, 1)
                sb_cumsum(L, SB_H - 2)
                pe.wait_ge(XT_ready, 2 * LEVELS * (L + 1))
                per_head(0, lambda h: XT[:, h, :], lambda h: bv[:, h, :], vnew_ps)
                sb_cumsum(L, SB_H - 1)
                pe.wait_ge(vnew_ready, 2 * L + 1)
                per_head(1, lambda h: kend[:, h, :], lambda h: Vn[:, h, :], state_ps)
                per_head(4, lambda h: AT[:, h, :], lambda h: Vn[:, h, :], None)
                pe.wait_ge(state_ready, L + 1)
                per_head(2, lambda h: qk[:, h, 0, P:T], lambda h: S[:, h, :], ks_ps)
                per_head(3, lambda h: qk[:, h, 1, P:T], lambda h: S[:, h, :], None)
                sb_output(L)
                pe.wait_ge(rhs1_ready, 2 * (L + 1))
                per_head(0, lambda h: XT[:, 4 + h, :], lambda h: RH1[:, h, :], vnew_ps)
                pe.wait_ge(vnew_ready, 2 * L + 2)
                per_head(5, lambda h: AT[:, 4 + h, :], lambda h: Vn[:, 4 + h, :], dno_ps)
                for n, b in enumerate((2, 3, 0, 1)):
                    if n == 0:
                        pe.wait_ge(mixed_sb, TT * (L + 1))
                        pe.wait_ge(dn_out, 5 * (L + 1))
                    if n == 2:
                        pe.wait_ge(mixed_dn, TT * (L + 1))
                    for k in (2 * b, 2 * b + 1):
                        for t in range(TT):
                            o = (k % 2) * T + t * P
                            ins = nc.tensor.transpose(bank(b)[:, o:o + P], hv[:, t, k * P:(k + 1) * P], ident)
                    ins.then_inc(mixT_ps, 1)
                c = FIRST_MIX[L] + N_IN
                chunk_landed(pe, c)
                chunk_landed(pe, c + 1)
                for t in range(TT):
                    for half in range(2):
                        w = in_cols(c + half, 512)
                        for n, k in enumerate((4, 5, 6, 7, 0, 1, 2, 3)):
                            if t == 0 and half == 0:
                                pe.wait_ge(mixT_act if n // 2 % 2 else mixT_dve, 2 * L + n // 4 + 1)
                            ins = mm(bank(4 + 2 * t + half), mixT[:, k, t * P:(t + 1) * P], w[:, k, :],
                                     start=(n == 0), stop=(n == KD - 1))
                    ins.then_inc(*((out_t0, 1) if t == 0 else (ring_used, 2)))

            def dense_ffn():
                transpose_h(1)
                n_mt = D_FF // P

                def gate_up(mt):
                    c, i = FIRST_FFN + mt // 2, mt % 2
                    chunk_landed(pe, c)
                    g, u, _ = gate_up_down(c)
                    if mt >= 4:
                        pe.wait_ge(hid_ready, mt - 3)
                    for which, w in enumerate((g, u)):
                        for k in range(KD):
                            if mt == 0 and which == 0:
                                hT_wait(1, max(k, 1))
                            ins = mm(bank(mt % 4)[:, which * T:(which + 1) * T], w[:, k, i * P:(i + 1) * P],
                                     hT[:, k, :], start=(k == 0), stop=(k == KD - 1))
                    ins.then_inc(gu_ps, 1)

                def down(mt):
                    c, i = FIRST_FFN + mt // 2, mt % 2
                    d = gate_up_down(c)[2]
                    pe.wait_ge(hid_ready, mt + 1)
                    for t in range(TT):
                        for half in range(2):
                            ins = mm(bank(4 + 2 * t + half), ffn_hid[:, mt % 4, t * P:(t + 1) * P],
                                     d[:, i, half * 512:(half + 1) * 512], start=(mt == 0), stop=(mt == n_mt - 1))
                    ins.then_inc(ring_used if i else down_done, 1)

                for mt in range(n_mt):
                    gate_up(mt)
                    if mt >= 2:
                        down(mt - 2)
                down(n_mt - 2)
                down(n_mt - 1)

            mixer(0)
            dense_ffn()
            mixer(1)

            transpose_h(3)
            pe.wait_ge(router_landed, 16)
            rw = v3(routw, KD)
            for t in range(TT):
                for k in range(KD):
                    if t == 0:
                        hT_wait(3, k)
                    ins = mm(bank(4)[:, t * 8:(t + 1) * 8], hT[:, k, t * P:(t + 1) * P], rw[:, k, :],
                             start=(k == 0), stop=(k == KD - 1))
            ins.then_inc(router_ps, 1)
            pe.wait_ge(sel_ready, 1)
            r5 = bank(5)
            mm(r5[:, 0:8], ustrict, sel[:, 0:8], start=True, stop=True)
            mm(r5[:, 8:16], ustrict, sel[:, 8:16], start=True, stop=False)
            mm(r5[:, 8:16], ones, sel[:, 0:8], start=False, stop=True)
            mm(r5[:, 16:24], ones, sel[:, 0:8], start=True, stop=False)
            mm(r5[:, 16:24], ones, sel[:, 8:16], start=False, stop=True).then_inc(rank_ps, 1)
            pe.wait_ge(rounds_ready, 1)
            rounds = pe.value_load(rounds_i[0:1, 0:1], min_val=1, max_val=3)

            def gather(it, j):
                pe.wait_ge(onehot_ready, it * (2 * TT) + TT * (j + 1))
                for k in range(KD):
                    for t in range(TT):
                        ins = mm(bank(4 + k // 4)[:, (k % 4) * SLOTS:(k % 4 + 1) * SLOTS],
                                 hv[:, t, k * P:(k + 1) * P], onehot[j][:, t, :], start=(t == 0), stop=(t == 1))
                    if k % 4 == 3:
                        ins.then_inc(gather_ps, 1)
                for t in range(TT):
                    ins = nc.tensor.transpose(bank(6)[0:SLOTS, t * P:(t + 1) * P], onehot[j][:, t, :], ident)
                ins.then_inc(ohT_ps, 1)

            def m_gate_up(it, j, c):
                n = FIRST_MOE + j * MOE_CH + c
                chunk_landed(pe, n, it * (LANDED * 2 * MOE_CH // NSLOT))
                if c == 0:
                    pe.wait_ge(xg_ready, it * 4 + 2 * (j + 1))
                if c >= 2:
                    pe.wait_ge(mhid_ready, it * (2 * MOE_CH) + (j * MOE_CH + c - 1))
                g, u, _ = gate_up_down(n)
                for i in range(FC // P):
                    for which, w in enumerate((g, u)):
                        o = bank(c % 2)[:, (2 * which + i) * SLOTS:(2 * which + i + 1) * SLOTS]
                        for k in range(KD):
                            ins = mm(o, w[:, k, i * P:(i + 1) * P], xgT[:, k, :], start=(k == 0), stop=(k == KD - 1))
                ins.then_inc(mgu_ps, 1)

            def m_down(it, j, c):
                d = gate_up_down(FIRST_MOE + j * MOE_CH + c)[2]
                pe.wait_ge(mhid_ready, it * (2 * MOE_CH) + (j * MOE_CH + c + 1))
                if j == 1 and c == 0:
                    pe.wait_ge(yT_ready, it * 4 + 2)
                for i in range(FC // P):
                    for k in range(KD):
                        ins = mm(bank(2 + k // 4)[:, (k % 4) * SLOTS:(k % 4 + 1) * SLOTS],
                                 d[:, i, k * P:(k + 1) * P], moe_hid[c % 2][:, i, :],
                                 start=(c == 0 and i == 0 and k % 4 == 0),
                                 stop=(c == MOE_CH - 1 and i == 1), skip_group_check=True)
                ins.then_inc(ring_used, 1)

            def y_transposes(it, j):
                pe.wait_ge(yT_ready, it * 4 + 2 * (j + 1))
                for k in range(KD):
                    ins = nc.tensor.transpose(bank(4 + k // 4)[0:SLOTS, (k % 4) * P:(k % 4 + 1) * P],
                                              yT[:, k, :], ident)
                    if k % 4 == 3:
                        ins.then_inc(y_ps, 1)

            def scatter(it, j):
                pe.wait_ge(ohT_ready, it * 2 + (j + 1))
                pe.wait_ge(y_act, it * 2 + (j + 1))
                pe.wait_ge(y_dve, it * 2 + (j + 1))
                for t in range(TT):
                    for half in range(2):
                        ins = mm(bank((6, 4)[t] + half), onehotT[j][:, t * P:(t + 1) * P],
                                 y_tok[:, half * 512:(half + 1) * 512], start=True, stop=True)
                    ins.then_inc(scatter_ps, 1)

            with pe.Fori(0, rounds) as r:
                with pe.Fori(0, N_EXP // 2) as pair:
                    it = r * (N_EXP // 2) + pair
                    for j in range(2):
                        gather(it, j)
                        for c in range(MOE_CH):
                            m_gate_up(it, j, c)
                            if c:
                                m_down(it, j, c - 1)
                            if j == 1 and c == 0:
                                y_transposes(it, 0)
                            if j == 1 and c == 1:
                                scatter(it, 0)
                        m_down(it, j, MOE_CH - 1)
                    y_transposes(it, 1)
                    pe.wait_ge(moe_acc, it * 4 + 2)
                    scatter(it, 1)
                    pe.wait_ge(moe_acc, it * 4 + 4)

        @block.scalar
        def _(act):
            A = nc.scalar.activation

            act.wait_ge(heads_landed, 32)
            A(negA, headp[:, 0:2 * DN_H], ACT.Exp).then_inc(expA, 1)

            def pre_norm_squares(u):
                for t in range(TT):
                    if u == 0:
                        act.wait_ge(x_landed, 16)
                    else:
                        act.wait_ge(x_ready, TT * (u - 1) + t + 1)
                    A(act_junk[t], xv[:, t, :], ACT.Square, accum_out=ssx[:, t:t + 1]).then_inc(ss_ready, 1)

            def hT_act_tiles(u, row):
                for k in (2, 3, 6, 7):
                    act.wait_ge(hT_ps, 4 * u + k // 2 + 1)
                    if u == 0 and k == 2:
                        act.wait_ge(params_ready, 1)
                    A(hT[:, k, :], bank(k // 2)[:, k % 2 * T:(k % 2 + 1) * T], ACT.Copy,
                      scale=prm[:, CONV_ROWS + row + k:CONV_ROWS + row + k + 1]).then_inc(hT_act, 1)

            def post_norm_squares(u, src):
                for t in range(TT):
                    src(act, t)
                    A(act_junk[t], bank(4 + 2 * t, 2), ACT.Square, accum_out=ssx[:, t:t + 1]).then_inc(post_ss, 1)

            def conv_dst(m):
                return (qk[:, m, 1, :] if m < 4 else qk[:, m - 4, 0, :] if m < 8 else vT[:, m - 8, :])

            def mixer(L):
                pre_norm_squares(2 * L)
                hT_act_tiles(2 * L, R_MIX + KD * L)

                def silu(m):
                    act.wait_ge(conv_taps, 3 * (CONV_T * L + m + 1))
                    A(conv_dst(m), conv_dst(m), ACT.Silu).then_inc(conv_silu, 1)

                for m in range(CONV_T):
                    act.wait_ge(*step_sem(L, m))
                    w3 = L * CONV_K * CONV_T + 3 * CONV_T + m
                    A(conv_dst(m), bank(4 + m % 4)[:, 0:T], ACT.Copy, scale=prm[:, w3:w3 + 1]).then_inc(conv_base, 1)
                    if m:
                        silu(m - 1)
                silu(CONV_T - 1)
                for t in range(TT):
                    act.wait_ge(*step_sem(L, 12 + t))
                    A(hv[:, t, 0:DN_W], bank(4 + t), ACT.Silu).then_inc(z_gate, 1)
                act.wait_ge(gate_in, L + 1)
                A(sabs, aa, ACT.Abs).then_inc(gate_exp, 1)
                A(eb, ba.rearrange("p (t c) -> p t c", t=TT)[:, :, 0:4], ACT.Exp, scale=-1.0).then_inc(gate_exp, 1)
                act.wait_ge(gate_exp, 4 * L + 1)
                A(sln, sabs, ACT.Exp, scale=-1.0).then_inc(gate_exp, 1)
                act.wait_ge(gate_exp, 4 * L + 3)
                A(sabs, sln, ACT.Ln, bias=1.0).then_inc(gate_exp, 1)

                def sb_copy(n):
                    kind, i = STEPS[n][0], STEPS[n][1]
                    act.wait_ge(*step_sem(L, n))
                    if kind == "sv":
                        dst, src = hv[:, i, DN_W:D], bank(4 + n % 4)
                    else:
                        dst, src = (sq_v if kind == "sq" else sk_v)[:, i, :], bank(4 + n % 4)[:, 0:T]
                    A(dst, src, ACT.Copy).then_inc(sb_copied, 1)

                if L:
                    act.wait_ge(x_ready, 2 * TT)
                for n in range(15, 19):
                    sb_copy(n)
                act.wait_ge(gcum_ready, L + 1)
                A(eg, gsum[:, 0:8], ACT.Exp).then_inc(gexp_ready, 1)
                act.wait_ge(gates_ready, 5 * L + 5)
                act.wait_ge(coef_ready, 5 * L + 1)
                A(egl, gdiff, ACT.Exp).then_inc(gexp_ready, 1)
                for n in range(19, 23):
                    sb_copy(n)
                act.wait_ge(decay_in, 8 * (L + 1))
                A(DR_sb[:, :], DR_sb[:, :], ACT.Exp).then_inc(decay_exp, 1)
                for n in range(23, 25):
                    sb_copy(n)

                def m1_copy(l, g):
                    act.wait_ge(M1_ps, 2 * (LEVELS * L + l) + g + 1)
                    if l >= 2:
                        act.wait_ge(XTM_ps, 2 * (6 * L + l - 2) + g + 1)
                    A(M1[:, 4 * g:4 * g + 4, :], bank(g).rearrange("p (a b) -> p a b", a=4), ACT.Copy)\
                        .then_inc(M1_ready, 1)

                def sb_softplus_parts(h):
                    act.wait_ge(sbz_ready, SB_H * L + h + 1)
                    if h:
                        act.wait_ge(sb_softplus, SB_H * L + h)
                    n = 3 * (SB_H * L + h)
                    A(sbe[:, :], zm[:, h % 2, :], ACT.Abs).then_inc(sb_soft, 1)
                    act.wait_ge(sb_soft, n + 1)
                    A(sbe[:, :], sbe[:, :], ACT.Exp, scale=-1.0).then_inc(sb_soft, 1)
                    act.wait_ge(sb_soft, n + 2)
                    A(sbe[:, :], sbe[:, :], ACT.Ln, bias=1.0).then_inc(sb_soft, 1)

                def sb_weights(h):
                    act.wait_ge(sb_expo, SB_H * L + h + 1)
                    A(wT[:, h, :], zm[:, h % 2, :], ACT.Exp).then_inc(sb_weight, 1)

                sb_softplus_parts(0)
                for l in range(1, LEVELS):
                    m1_copy(l, 0)
                    m1_copy(l, 1)
                    sb_weights(l - 1)
                    sb_softplus_parts(l)
                act.wait_ge(vnew_ps, 2 * L + 1)
                A(Vn[:, 0:4, :], bank(0).rearrange("p (a b) -> p a b", a=4), ACT.Copy).then_inc(vnew_ready, 1)
                sb_softplus_parts(SB_H - 1)
                act.wait_ge(state_ps, L + 1)
                A(S, bank(1).rearrange("p (a b) -> p a b", a=4), ACT.Copy).then_inc(state_ready, 1)
                sb_weights(SB_H - 2)
                sb_weights(SB_H - 1)
                act.wait_ge(vnew_ps, 2 * L + 2)
                A(Vn[:, 4:8, :], bank(0).rearrange("p (a b) -> p a b", a=4), ACT.Copy).then_inc(vnew_ready, 1)
                for t in range(TT):
                    act.wait_ge(sbo_ps, 2 * L + t + 1)
                    A((sbz, sbp)[t][:, 0:512], bank(6 + t), ACT.Square).then_inc(sb_sq, 1)
                for n, b in ((1, 3), (3, 1)):
                    act.wait_ge(mixT_ps, 4 * L + n + 1)
                    col = CONV_ROWS + (R_SB if b >= 2 else R_DN) + L
                    A(mixT[:, 2 * b:2 * b + 2, :], bank(b).rearrange("p (a b) -> p a b", a=2), ACT.Copy,
                      scale=prm[:, col:col + 1]).then_inc(mixT_act, 1)

                def src(eng, t):
                    eng.wait_ge(*((out_t0, L + 1) if t == 0 else (ring_used, FIRST_MIX[L] + N_MIX)))
                post_norm_squares(2 * L, src)

            def dense_ffn():
                pre_norm_squares(1)
                hT_act_tiles(1, R_FFN)
                for mt in range(D_FF // P):
                    act.wait_ge(gu_ps, mt + 1)
                    if mt >= 4:
                        act.wait_ge(hid_ready, mt - 3)
                    A(ffn_sg[:, mt % 4, :], bank(mt % 4)[:, 0:T], ACT.Silu).then_inc(sg_ready, 1)
                post_norm_squares(1, lambda eng, t: eng.wait_ge(ring_used, FIRST_FFN + FFN_CH))

            mixer(0)
            dense_ffn()
            mixer(1)
            pre_norm_squares(3)
            hT_act_tiles(3, R_FFN + KD)
            act.wait_ge(route_step, 10)
            A(ge, gd, ACT.Exp).then_inc(route_exp, 1)
            act.wait_ge(rounds_ready, 1)
            rounds = act.value_load(rounds_i[0:1, 0:1], min_val=1, max_val=3)
            with act.Fori(0, rounds) as r:
                with act.Fori(0, N_EXP // 2) as pair:
                    it = r * (N_EXP // 2) + pair

                    def yT_copy(j):
                        act.wait_ge(ring_used, it * (2 * MOE_CH) + (FIRST_MOE + (j + 1) * MOE_CH))
                        for b in range(2):
                            A(yT[:, 4 * b:4 * b + 4, :], bank(2 + b)[:, 0:4 * SLOTS].rearrange("p (a b) -> p a b", a=4),
                              ACT.Copy).then_inc(yT_ready, 1)

                    def y_copy(j):
                        act.wait_ge(y_ps, it * 4 + 2 * j + 1)
                        A(y_tok[:, 0:512], bank(4)[0:SLOTS, :], ACT.Copy).then_inc(y_act, 1)

                    for j in range(2):
                        act.wait_ge(ohT_ps, it * 2 + (j + 1))
                        A(onehotT[j], bank(6)[0:SLOTS, 0:T], ACT.Copy).then_inc(ohT_ready, 1)
                        if j == 1:
                            yT_copy(0)
                        for c in range(MOE_CH):
                            act.wait_ge(mgu_ps, it * (2 * MOE_CH) + (j * MOE_CH + c + 1))
                            if c >= 2:
                                act.wait_ge(mhid_ready, it * (2 * MOE_CH) + (j * MOE_CH + c - 1))
                            A(moe_sg[c % 2], bank(c % 2)[:, 0:2 * SLOTS].rearrange("p (a b) -> p a b", a=2),
                              ACT.Silu).then_inc(msg_ready, 1)
                            if j == 1 and c == 0:
                                y_copy(0)
                    yT_copy(1)
                    y_copy(1)
            for t in range(TT):
                act.wait_ge(moe_acc, rounds * (2 * N_EXP))
                A(act_junk[t], moe_yv[:, t, :], ACT.Square, accum_out=ssx[:, t:t + 1]).then_inc(post_ss, 1)

        @block.vector
        def _(dve):
            V = nc.vector

            dve.wait_ge(expA, 1)
            V.tensor_scalar(negA, negA, -1.0, None, ALU.mult).then_inc(negA_ready, 1)
            dve.wait_ge(params_ps, 1)
            V.tensor_copy(prm[:, :], bank(4)[:, 0:CONV_ROWS + NORM_ROWS]).then_inc(params_ready, 1)
            dve.wait_ge(params_ready, 1)
            dve.wait_ge(negA_ready, 1)

            def normalise(u):
                for t in range(TT):
                    dve.wait_ge(rstd_ready, TT * u + t + 1)
                    V.tensor_scalar(hv[:, t, :], xv[:, t, :], rsx[:, t:t + 1], None, ALU.mult).then_inc(h_ready, 1)

            def hT_dve_tiles(u, row):
                for k in (0, 1, 4, 5):
                    dve.wait_ge(hT_ps, 4 * u + k // 2 + 1)
                    V.tensor_scalar(hT[:, k, :], bank(k // 2)[:, k % 2 * T:(k % 2 + 1) * T],
                                    prm[:, CONV_ROWS + row + k:CONV_ROWS + row + k + 1], None,
                                    ALU.mult).then_inc(hT_dve, 1)

            def residual(u, source, w, landed):
                dve.wait_ge(*landed)
                for t in range(TT):
                    dve.wait_ge(post_rstd, TT * u + t + 1)
                    V.scalar_tensor_tensor(post_tmp, source(t), rsx[:, t:t + 1], w, ALU.mult, ALU.mult)\
                        .then_inc(post_scaled, 1)
                    dve.wait_ge(post_scaled, TT * u + t + 1)
                    V.tensor_tensor(xv[:, t, :], xv[:, t, :], post_tmp, ALU.add).then_inc(x_ready, 1)
                    dve.wait_ge(x_ready, TT * u + t + 1)

            def conv_dst(m):
                return (qk[:, m, 1, :] if m < 4 else qk[:, m - 4, 0, :] if m < 8 else vT[:, m - 8, :])

            def mixer(L):
                normalise(2 * L)
                hT_dve_tiles(2 * L, R_MIX + KD * L)
                for m in range(CONV_T):
                    dve.wait_ge(conv_base, CONV_T * L + m + 1)
                    for n, i in enumerate((2, 1, 0)):
                        s = 3 - i
                        if n:
                            dve.wait_ge(conv_taps, 3 * (CONV_T * L + m) + n)
                        w = L * CONV_K * CONV_T + i * CONV_T + m
                        V.scalar_tensor_tensor(conv_dst(m)[:, s:T], bank(4 + m % 4)[:, 0:T - s], prm[:, w:w + 1],
                                               conv_dst(m)[:, s:T], ALU.mult, ALU.add).then_inc(conv_taps, 1)
                dve.wait_ge(*step_sem(L, 14))
                V.tensor_copy(ba, bank(6)[:, 0:16]).then_inc(ba_copied, 1)
                dve.wait_ge(ba_copied, L + 1)
                a_v = ba.rearrange("p (t c) -> p t c", t=TT)[:, :, 4:8]
                dtb = headp[:, (DEPTH + L) * DN_H:(DEPTH + L + 1) * DN_H]
                V.tensor_tensor(aa.rearrange("p (t c) -> p t c", t=TT), a_v, bcm(dtb, TT), ALU.add)\
                    .then_inc(gate_in, 1)
                dve.wait_ge(norms_ps, L + 1)
                V.tensor_scalar(nsum, bank(0)[:, 0:16], EPS, None, ALU.add).then_inc(norms_sum, 1)
                dve.wait_ge(gate_in, L + 1)
                dve.wait_ge(gate_exp, 4 * (L + 1))
                g0 = 5 * L
                V.scalar_tensor_tensor(spl, aa, 0.0, sabs, ALU.max, ALU.add).then_inc(gates_ready, 1)
                V.tensor_scalar(eb, eb, 1.0, None, ALU.add).then_inc(gates_ready, 1)
                dve.wait_ge(gates_ready, g0 + 2)
                V.reciprocal(beta, eb).then_inc(gates_ready, 1)
                V.tensor_tensor(g_log.rearrange("p (t c) -> p t c", t=TT), spl.rearrange("p (t c) -> p t c", t=TT),
                                bcm(negA[:, L * DN_H:(L + 1) * DN_H], TT), ALU.mult).then_inc(gates_ready, 1)
                dve.wait_ge(gates_ready, g0 + 4)
                dve.wait_ge(norms_ready, L + 1)
                V.tensor_tensor(br, beta, rk, ALU.mult).then_inc(gates_ready, 1)
                for t in range(TT):
                    dve.wait_ge(v_ps, 2 * L + t + 1)
                    V.tensor_tensor(bv[:, 4 * t:4 * t + 4, :], bank(1 + t).rearrange("p (a b) -> p a b", a=4),
                                    bcl(beta[:, 4 * t:4 * t + 4], P), ALU.mult).then_inc(bv_ready, 1)
                dve.wait_ge(gcum_ps, L + 1)
                V.tensor_copy(gsum, bank(0)[:, 16:32]).then_inc(gcum_ready, 1)
                dve.wait_ge(gcum_ready, L + 1)
                c0 = 5 * L
                V.tensor_tensor(gdiff, gsum[:, 8:12], gsum[:, 0:4], ALU.subtract).then_inc(coef_ready, 1)
                V.tensor_scalar(coefq, rq, float(DN_D) ** -0.5, None, ALU.mult).then_inc(coef_ready, 1)
                dve.wait_ge(gexp_ready, 2 * L + 1)
                dve.wait_ge(gates_ready, g0 + 5)
                V.tensor_tensor(scoef, eg[:, 4:8], br[:, 4:8], ALU.mult).then_inc(coef_ready, 1)
                dve.wait_ge(coef_ready, c0 + 3)
                V.tensor_scalar(scoef, scoef, -1.0, None, ALU.mult).then_inc(coef_ready, 1)
                dve.wait_ge(gexp_ready, 2 * L + 2)
                V.tensor_tensor(kcoef, egl, rk[:, 0:4], ALU.mult).then_inc(coef_ready, 1)
                dve.wait_ge(coef_ready, c0 + 5)
                dve.wait_ge(kT_ps, L + 1)
                V.tensor_tensor(kend, bank(3).rearrange("p (a b) -> p a b", a=4), bcl(kcoef, P), ALU.mult)\
                    .then_inc(kend_ready, 1)
                dve.wait_ge(bc_ps, 2 * L + 1)
                for pr in range(NPR):
                    V.tensor_scalar(DR[:, pr, :], bank(0, 2)[:, pr * P:(pr + 1) * P], gsum[:, pr:pr + 1], 0.0,
                                    ALU.subtract, ALU.min).then_inc(decay_in, 1)
                dve.wait_ge(bc_ps, 2 * L + 2)
                dve.wait_ge(decay_ready, 2 * (L + 1))
                for g in range(2):
                    V.tensor_tensor(DF[:, 4 * g:4 * g + 4, :], DR[:, 4 * g:4 * g + 4, :],
                                    bank(2 + g).rearrange("p (a b) -> p a b", a=4), ALU.mult)\
                        .then_inc(betadecay_ready, 1)

                def sb_mask(h):
                    dve.wait_ge(sbz_ps, SB_H * L + h + 1)
                    if h >= 2:
                        dve.wait_ge(sb_weight, SB_H * L + h - 1)
                    V.scalar_tensor_tensor(zm[:, h % 2, :], bank(6 + h % 2)[:, 0:3 * P], SB_D ** -0.5, sbmask,
                                           ALU.mult, ALU.mult).then_inc(sbz_ready, 1)

                def sb_plus(h):
                    dve.wait_ge(sb_soft, 3 * (SB_H * L + h + 1))
                    if h >= 2:
                        dve.wait_ge(sbc_ps, SB_H * L + h - 1)
                    dve.wait_ge(sbz_ready, SB_H * L + h + 1)
                    V.scalar_tensor_tensor(sp[:, h % 2, :], zm[:, h % 2, :], 0.0, sbe[:, :], ALU.max, ALU.add)\
                        .then_inc(sb_softplus, 1)

                def sb_exponent(h):
                    dve.wait_ge(sbc_ps, SB_H * L + h + 1)
                    V.tensor_tensor(zm[:, h % 2, :], zm[:, h % 2, :], bank(6 + h % 2)[:, 0:3 * P], ALU.subtract)\
                        .then_inc(sb_expo, 1)

                sb_mask(0)
                dve.wait_ge(betadecay_ready, 2 * (L + 1))
                for g in range(2):
                    dve.wait_ge(kk_ps, 2 * L + g + 1)
                    two = ps[:, 2 * g:2 * g + 2, :].rearrange("p b (a k c) -> p (b a) k c", a=2, k=2)
                    V.tensor_tensor(LT[:, 4 * g:4 * g + 4, :], two[:, :, 0, :], DF[:, 4 * g:4 * g + 4, :],
                                    ALU.mult).then_inc(LT_ready, 1)
                    V.tensor_tensor(AT[:, 4 * g:4 * g + 4, :], two[:, :, 1, :], DR[:, 4 * g:4 * g + 4, :],
                                    ALU.mult).then_inc(AT_ready, 1)
                sb_plus(0)
                sb_mask(1)
                for l in range(LEVELS):
                    if l:
                        sb_exponent(l - 1)
                    for g in range(2):
                        s = slice(4 * g, 4 * g + 4)
                        if l and g:
                            sb_plus(l)
                        if l == 0:
                            dve.wait_ge(LT_ready, 2 * (L + 1))
                            dve.wait_ge(M1_ps, 2 * LEVELS * L + g + 1)
                            V.tensor_tensor(X[:, s, :], bcm(ident, 4), bank(g).rearrange("p (a b) -> p a b", a=4),
                                            ALU.subtract).then_inc(X_ready, 1)
                            V.tensor_tensor(XT[:, s, :], bcm(ident, 4), BT[:, s, :], ALU.subtract)\
                                .then_inc(XT_ready, 1)
                        else:
                            if l < LEVELS - 1:
                                dve.wait_ge(XM_ps, 2 * (5 * L + l - 1) + g + 1)
                                dve.wait_ge(X_ready, 2 * (6 * L + l - 1) + g + 1)
                                V.tensor_tensor(X[:, s, :], X[:, s, :],
                                                bank(2 + g).rearrange("p (a b) -> p a b", a=4),
                                                ALU.subtract).then_inc(X_ready, 1)
                            dve.wait_ge(XTM_ps, 2 * (6 * L + l - 1) + g + 1)
                            dve.wait_ge(XT_ready, 2 * (LEVELS * L + l - 1) + g + 1)
                            V.tensor_tensor(XT[:, s, :], XT[:, s, :],
                                            bank(4 + g).rearrange("p (a b) -> p a b", a=4),
                                            ALU.subtract).then_inc(XT_ready, 1)
                    if l:
                        sb_mask(l + 1)
                sb_exponent(SB_H - 2)
                sb_plus(SB_H - 1)
                sb_exponent(SB_H - 1)
                dve.wait_ge(ks_ps, L + 1)
                V.tensor_tensor(RH1, bank(2).rearrange("p (a b) -> p a b", a=4), bcl(scoef, P), ALU.mult)\
                    .then_inc(rhs1_ready, 1)
                dve.wait_ge(rhs1_ready, 2 * L + 1)
                V.tensor_tensor(RH1, RH1, bv[:, 4:8, :], ALU.add).then_inc(rhs1_ready, 1)
                for t in range(TT):
                    dve.wait_ge(sb_sq, 2 * L + t + 1)
                    V.tensor_reduce(sss[:, 8 * t:8 * t + 8], v3((sbz, sbp)[t], SB_H, 0, 512), AX_X, ALU.add)\
                        .then_inc(sb_ss, 1)
                dve.wait_ge(dno_ps, L + 1)
                c5 = 5 * L
                o0, o1 = v3(LT_sb, DN_H, 0, DN_W), v3(LT_sb, DN_H, DN_W, DN_W)
                V.tensor_tensor(o0, bank(4).rearrange("p (a b) -> p a b", a=4), bcl(coefq[:, 0:4], P), ALU.mult)\
                    .then_inc(dn_out, 1)
                V.tensor_tensor(o1, bank(3).rearrange("p (a b) -> p a b", a=4), bcl(eg[:, 4:8], P), ALU.mult)\
                    .then_inc(dn_out, 1)
                dve.wait_ge(dn_out, c5 + 2)
                V.tensor_tensor(o1, o1, bank(5).rearrange("p (a b) -> p a b", a=4), ALU.add).then_inc(dn_out, 1)
                dve.wait_ge(dn_out, c5 + 3)
                V.tensor_tensor(o1, o1, bcl(coefq[:, 4:8], P), ALU.mult).then_inc(dn_out, 1)
                dve.wait_ge(dn_out, c5 + 4)
                V.tensor_tensor(AT_sb[:, :], LT_sb[:, :], LT_sb[:, :], ALU.mult).then_inc(dn_out, 1)
                for t in range(TT):
                    dve.wait_ge(sb_rstd, 2 * L + t + 1)
                    dve.wait_ge(sbo_ps, 2 * (L + 1))
                    V.tensor_tensor(v3(h_sb, SB_H, t * D + DN_W, DN_W), bank(6 + t).rearrange("p (a b) -> p a b", a=SB_H),
                                    bcl(srs[:, 8 * t:8 * t + 8], SB_D), ALU.mult).then_inc(mixed_sb, 1)
                dve.wait_ge(dn_out, c5 + 5)
                V.tensor_reduce(dss, v3(AT_sb, NPR), AX_X, ALU.add).then_inc(dn_rstd_in, 1)
                dve.wait_ge(mixT_ps, 4 * L + 1)
                col = CONV_ROWS + R_SB + L
                V.tensor_scalar(mixT[:, 4:6, :], bank(2).rearrange("p (a b) -> p a b", a=2), prm[:, col:col + 1], None,
                                ALU.mult).then_inc(mixT_dve, 1)
                dve.wait_ge(dn_rstd, 2 * (L + 1))
                for t in range(TT):
                    V.tensor_tensor(v3(LT_sb, DN_H, t * DN_W, DN_W), v3(LT_sb, DN_H, t * DN_W, DN_W),
                                    bcl(drs[:, 4 * t:4 * t + 4], P), ALU.mult).then_inc(dn_rstd_in, 1)
                    dve.wait_ge(dn_rstd_in, 3 * L + t + 2)
                    V.tensor_tensor(hv[:, t, 0:DN_W], hv[:, t, 0:DN_W], LT_sb[:, t * DN_W:(t + 1) * DN_W],
                                    ALU.mult).then_inc(mixed_dn, 1)
                dve.wait_ge(mixT_ps, 4 * L + 3)
                col = CONV_ROWS + R_DN + L
                V.tensor_scalar(mixT[:, 0:2, :], bank(0).rearrange("p (a b) -> p a b", a=2), prm[:, col:col + 1], None,
                                ALU.mult).then_inc(mixT_dve, 1)
                residual(2 * L, lambda t: bank(4 + 2 * t, 2), wpost[:, :], (wpost_landed, 16 * (L + 1)))

            def dense_ffn():
                normalise(1)
                hT_dve_tiles(1, R_FFN)
                for mt in range(D_FF // P):
                    dve.wait_ge(sg_ready, mt + 1)
                    if mt >= 4:
                        if mt % 2:
                            dve.wait_ge(ring_used, FIRST_FFN + (mt - 4) // 2 + 1)
                        else:
                            dve.wait_ge(down_done, (mt - 4) // 2 + 1)
                    V.tensor_tensor(ffn_hid[:, mt % 4, :], ffn_sg[:, mt % 4, :], bank(mt % 4)[:, T:2 * T], ALU.mult)\
                        .then_inc(hid_ready, 1)
                residual(1, lambda t: bank(4 + 2 * t, 2), wpost_ffn, (wpostf_landed, 16))

            mixer(0)
            dense_ffn()
            mixer(1)
            normalise(3)
            hT_dve_tiles(3, R_FFN + KD)

            n = [0]

            def step(ins):
                n[0] += 1
                ins.then_inc(route_step, 1)
                dve.wait_ge(route_step, n[0])

            def tv(ap):
                return ap.rearrange("p (t e) -> p t e", t=TT)

            def first_max(src, best, chosen):
                step(V.tensor_reduce(best, tv(src), AX_X, ALU.max))
                step(V.tensor_tensor(tv(cand), tv(src), bcl(best, N_EXP), ALU.is_equal))
                step(V.tensor_tensor(tv(cand), tv(cand), bcm(w8, TT), ALU.mult))
                step(V.tensor_reduce(mx, tv(cand), AX_X, ALU.max))
                step(V.tensor_tensor(tv(chosen), tv(cand), bcl(mx, N_EXP), ALU.is_equal))

            dve.wait_ge(router_ps, 1)
            V.tensor_copy(lg, bank(4)[:, 0:16]).then_inc(moe_zero, 1)
            V.memset(moe_y[:, :], 0.0).then_inc(moe_zero, 1)
            dve.wait_ge(moe_zero, 2)
            step(V.tensor_reduce(m1, tv(lg), AX_X, ALU.max))
            first_max(lg, m1, sel1)
            step(V.scalar_tensor_tensor(lg2, sel1, -3.0e38, lg, ALU.mult, ALU.add))
            step(V.tensor_reduce(m2, tv(lg2), AX_X, ALU.max))
            step(V.tensor_tensor(gd, m2, m1, ALU.subtract))
            step(V.tensor_copy(mx, m2))
            assert n[0] == 10
            first_max(lg2, m2, sel2)
            V.tensor_tensor(sel, sel1, sel2, ALU.add).then_inc(sel_ready, 1)
            dve.wait_ge(sel_ready, 1)
            dve.wait_ge(route_exp, 1)
            step(V.tensor_scalar(g1, ge, 1.0, None, ALU.add))
            step(V.reciprocal(g1, g1))
            step(V.tensor_tensor(g2, g1, ge, ALU.mult))
            step(V.tensor_tensor(tv(sel1), tv(sel1), bcl(g1, N_EXP), ALU.mult))
            step(V.tensor_tensor(tv(sel2), tv(sel2), bcl(g2, N_EXP), ALU.mult))
            step(V.tensor_tensor(gate, sel1, sel2, ALU.add))
            dve.wait_ge(rank_ps, 1)
            step(V.tensor_reduce(cmax, bank(5)[:, 16:24], AX_X, ALU.max))
            step(V.scalar_tensor_tensor(rank, bank(5)[:, 0:16], 1000.0, sel, ALU.add, ALU.mult))
            step(V.tensor_scalar(rank, rank, -1000.0, None, ALU.add))
            step(V.tensor_scalar(cgt, cmax, float(ROUND_LIMITS[0]), None, ALU.is_gt))
            step(V.tensor_scalar(ctwo, cmax, float(ROUND_LIMITS[1]), 1.0, ALU.is_gt, ALU.add))
            V.tensor_tensor(rounds_i[:, :], cgt, ctwo, ALU.add).then_inc(rounds_ready, 1)
            dve.wait_ge(rounds_ready, 1)
            rounds = dve.value_load(rounds_i[0:1, 0:1], min_val=1, max_val=3)
            wffn = prm[:, CONV_ROWS + R_FFN + KD:CONV_ROWS + R_FFN + 2 * KD]

            with dve.Fori(0, rounds) as r:
                with dve.Fori(0, N_EXP // 2) as pair:
                    it = r * (N_EXP // 2) + pair

                    def choose(j):
                        e = pair * 2 + j
                        cr, cg = cur_rank[:, j * TT:(j + 1) * TT], cur_gate[:, j * TT:(j + 1) * TT]
                        V.tensor_copy(cr, tv(rank)[:, :, bass.ds(e, 1)].rearrange("p t e -> p (t e)"))\
                            .then_inc(cur_ready, 1)
                        V.tensor_copy(cg, tv(gate)[:, :, bass.ds(e, 1)].rearrange("p t e -> p (t e)"))\
                            .then_inc(cur_ready, 1)
                        dve.wait_ge(cur_ready, it * 4 + 2 * (j + 1))
                        for t in range(TT):
                            V.tensor_scalar(onehot[j][:, t, :], iota, cr[:, t:t + 1], None, ALU.is_equal)\
                                .then_inc(onehot_ready, 1)

                    def gathered(j):
                        for b in range(2):
                            dve.wait_ge(gather_ps, it * 4 + (2 * j + b + 1))
                            V.tensor_tensor(xgT[:, 4 * b:4 * b + 4, :],
                                            bank(4 + b)[:, 0:4 * SLOTS].rearrange("p (a b) -> p a b", a=4),
                                            bcl(wffn[:, 4 * b:4 * b + 4], SLOTS), ALU.mult).then_inc(xg_ready, 1)

                    def y_copy(j):
                        dve.wait_ge(y_ps, it * 4 + 2 * (j + 1))
                        V.tensor_copy(y_tok[:, 512:D], bank(5)[0:SLOTS, :]).then_inc(y_dve, 1)

                    def accumulate(j):
                        for t in range(TT):
                            dve.wait_ge(scatter_ps, it * 4 + (2 * j + t + 1))
                            V.scalar_tensor_tensor(moe_yv[:, t, :], bank((6, 4)[t], 2),
                                                   cur_gate[:, j * TT + t:j * TT + t + 1], moe_yv[:, t, :],
                                                   ALU.mult, ALU.add).then_inc(moe_acc, 1)
                        dve.wait_ge(moe_acc, it * 4 + 2 * (j + 1))

                    for j in range(2):
                        choose(j)
                        gathered(j)
                        for c in range(MOE_CH):
                            dve.wait_ge(msg_ready, it * (2 * MOE_CH) + (j * MOE_CH + c + 1))
                            if c >= 2:
                                dve.wait_ge(ring_used, it * (2 * MOE_CH) + (FIRST_MOE + j * MOE_CH + c - 1))
                            V.tensor_tensor(moe_hid[c % 2], moe_sg[c % 2],
                                            bank(c % 2)[:, 2 * SLOTS:4 * SLOTS].rearrange("p (a b) -> p a b", a=2),
                                            ALU.mult).then_inc(mhid_ready, 1)
                            if j == 1 and c == 0:
                                y_copy(0)
                            if j == 1 and c == 1:
                                accumulate(0)
                    y_copy(1)
                    accumulate(1)
                V.tensor_scalar(rank, rank, -float(SLOTS), None, ALU.add).then_inc(route_step, 1)
                dve.wait_ge(route_step, r + (n[0] + 1))
            residual(3, lambda t: moe_yv[:, t, :], wpost_ffn, (wpostf_landed, 32))

        @block.gpsimd
        def _(pool):
            G = nc.gpsimd
            pool.dma_start(rows[0:CONV_ROWS, 0:P], conv_w.rearrange("l k (t p) -> (l k t) p", p=P))\
                .then_inc(rows_landed, 16)
            pool.dma_start(rows[R_MIX:R_MIX + 16, P:2 * P], norm_mix_pre.rearrange("l (k p) -> (l k) p", p=P))\
                .then_inc(rows_landed, 16)
            pool.dma_start(rows[R_FFN:R_FFN + 16, P:2 * P], norm_ffn_pre.rearrange("l (k p) -> (l k) p", p=P))\
                .then_inc(rows_landed, 16)
            pool.dma_start(rows[R_DN:R_DN + 2, P:2 * P], dn_norm_w).then_inc(rows_landed, 16)
            pool.dma_start(rows[R_SB:R_SB + 2, P:P + SB_D], sb_norm_w).then_inc(rows_landed, 16)
            pool.dma_start(rows[R_SB:R_SB + 2, P + SB_D:2 * P], sb_norm_w).then_inc(rows_landed, 16)
            pool.dma_start(wpost[:, :], norm_mix_post[0].partition_broadcast(P)).then_inc(wpost_landed, 16)
            pool.dma_start(headp[:, 0:8], dn_a_log.rearrange("l h -> (l h)").partition_broadcast(P))\
                .then_inc(heads_landed, 16)
            pool.dma_start(headp[:, 8:16], dn_dt_bias.rearrange("l h -> (l h)").partition_broadcast(P))\
                .then_inc(heads_landed, 16)
            pool.dma_start(v3(routw, KD), router_w[0].rearrange("(k p) e -> p k e", p=P)).then_inc(router_landed, 16)
            G.memset(mhalf, -0.5).then_inc(half_ready, 1)
            pool.wait_ge(half_ready, 1)

            def rsqrt(dst, src, scale, mid, done, n_mid):
                G.tensor_scalar(src, src, scale, EPS, ALU.mult, ALU.add).then_inc(mid, 1)
                pool.wait_ge(mid, n_mid)
                G.tensor_tensor(dst, src, mhalf[:, 0:src.shape[1]], ALU.pow).then_inc(done, 1)

            def pre_rstd(u):
                for t in range(TT):
                    pool.wait_ge(ss_ready, TT * u + t + 1)
                    rsqrt(rsx[:, t:t + 1], ssx[:, t:t + 1], 1.0 / D, rstd_mean, rstd_ready, TT * u + t + 1)

            def post_norm_rstd(u):
                for t in range(TT):
                    pool.wait_ge(post_ss, TT * u + t + 1)
                    rsqrt(rsx[:, t:t + 1], ssx[:, t:t + 1], 1.0 / D, post_mean, post_rstd, TT * u + t + 1)

            def mixer(L):
                pre_rstd(2 * L)
                for m in range(8):
                    pool.wait_ge(conv_silu, CONV_T * L + m + 1)
                    src = qk[:, m, 1, :] if m < 4 else qk[:, m - 4, 0, :]
                    if m == 0:
                        pool.wait_ge(params_ps, 1)
                    G.tensor_tensor(squares[:, m, :], src, src, ALU.mult).then_inc(qk_squares, 1)
                pool.wait_ge(norms_sum, L + 1)
                G.tensor_tensor(rn, nsum, mhalf, ALU.pow).then_inc(norms_ready, 1)
                pool.wait_ge(gcum_ready, L + 1)
                G.tensor_tensor(diag_g, bcm(ident, NPR), bcl(gsum[:, 0:8], P), ALU.mult).then_inc(diag_ready, 1)
                pool.wait_ge(gates_ready, 5 * (L + 1))
                G.tensor_tensor(diag_b, bcm(ident, NPR), bcl(br, P), ALU.mult).then_inc(diag_ready, 1)
                pool.wait_ge(decay_exp, L + 1)
                G.tensor_tensor(DR, DR, bcm(uinc, NPR), ALU.mult).then_inc(decay_ready, 1)
                pool.wait_ge(decay_ready, 2 * L + 1)
                G.tensor_tensor(DR, DR, bcl(rk, P), ALU.mult).then_inc(decay_ready, 1)

                def blocks(l, g):
                    s = slice(4 * g, 4 * g + 4)
                    pool.wait_ge(LT_ready, 2 * L + g + 1)
                    if l:
                        pool.wait_ge(M1_ps, 2 * (LEVELS * L + l - 1) + g + 1)
                        if l == 1:
                            pool.wait_ge(XT_ready, 2 * LEVELS * L + g + 1)
                    G.tensor_tensor(BT[:, s, :], LT[:, s, :], bcm(cst[:, C_LVL + l * P:C_LVL + (l + 1) * P], 4),
                                    ALU.mult).then_inc(BT_ready, 1)

                def sb_keep_mask(h):
                    pool.wait_ge(sb_softplus, SB_H * L + h + 1)
                    G.tensor_tensor(sp[:, h % 2, :], sp[:, h % 2, :], sbmask, ALU.mult).then_inc(sb_keep, 1)

                def sb_weight_mask(h):
                    pool.wait_ge(sb_weight, SB_H * L + h + 1)
                    G.tensor_tensor(wT[:, h, :], wT[:, h, :], sbmask, ALU.mult).then_inc(sb_wmask, 1)

                blocks(0, 0)
                blocks(0, 1)
                sb_keep_mask(0)
                for l in range(1, LEVELS):
                    blocks(l, 0)
                    blocks(l, 1)
                    sb_weight_mask(l - 1)
                    sb_keep_mask(l)
                sb_keep_mask(SB_H - 1)
                sb_weight_mask(SB_H - 2)
                sb_weight_mask(SB_H - 1)
                for t in range(TT):
                    pool.wait_ge(sb_ss, 2 * L + t + 1)
                    rsqrt(srs[:, 8 * t:8 * t + 8], sss[:, 8 * t:8 * t + 8], 1.0 / SB_D, sb_rstd_in, sb_rstd,
                          2 * L + t + 1)
                pool.wait_ge(dn_rstd_in, 3 * L + 1)
                G.tensor_scalar(dss, dss, 1.0 / DN_D, EPS, ALU.mult, ALU.add).then_inc(dn_rstd, 1)
                pool.wait_ge(dn_rstd, 2 * L + 1)
                G.tensor_tensor(drs, dss, mhalf[:, 0:8], ALU.pow).then_inc(dn_rstd, 1)
                pool.wait_ge(sbz_ps, SB_H * (L + 1))
                pool.dma_start(wpost_ffn, norm_ffn_post[L].partition_broadcast(P)).then_inc(wpostf_landed, 16)
                post_norm_rstd(2 * L)

            mixer(0)
            pool.wait_ge(x_ready, TT)
            pool.dma_start(wpost[:, :], norm_mix_post[1].partition_broadcast(P)).then_inc(wpost_landed, 16)
            pre_rstd(1)
            post_norm_rstd(1)
            mixer(1)
            pre_rstd(3)
            post_norm_rstd(3)


_INS = ["x", "norm_mix_pre", "norm_mix_post", "norm_ffn_pre", "norm_ffn_post", "w_in", "conv_w", "dn_a_log",
        "dn_dt_bias", "dn_norm_w", "sb_norm_w", "w_out", "ffn_w_gate", "ffn_w_up", "ffn_w_down", "router_w",
        "moe_w_gate", "moe_w_up", "moe_w_down"]


def constants():
    c = np.zeros((P, C_ALL), np.float32)
    i, j = np.arange(P)[:, None], np.arange(P)[None, :]
    c[:, C_ID:C_ID + P] = i == j
    c[:, C_UINC:C_UINC + P] = i <= j
    c[:, C_TRI:C_TRI + P] = i >= j
    c[:, C_SB:C_SB + P] = i < j
    c[:, C_SB + P:C_SB + 2 * P] = 1.0
    c[:, C_SB + 2 * P:C_SB + 3 * P] = i < j
    for l in range(LEVELS):
        b = 1 << l
        c[:, C_LVL + l * P:C_LVL + (l + 1) * P] = (i // (2 * b) == j // (2 * b)) & (i % (2 * b) < b) & (j % (2 * b) >= b)
    c[:, C_IOTA:C_IOTA + SLOTS] = np.arange(SLOTS)
    c[:, C_W8:C_W8 + N_EXP] = N_EXP - np.arange(N_EXP)
    return c


def kernel(**inputs):
    import concourse.bacc as _bacc
    from concourse.bass_utils import run_bass_kernel_spmd as _run

    nc = _bacc.Bacc("TRN2", target_bir_lowering=False, num_devices=1)
    arrays, args = {}, []
    for name in _INS:
        a = np.ascontiguousarray(inputs[name])
        arrays[f"in_{name}"] = a
        args.append(nc.dram_tensor(f"in_{name}", a.shape, mybir.dt.from_np(a.dtype), kind="ExternalInput").ap())
    arrays["in_consts"] = constants()
    consts = nc.dram_tensor("in_consts", (P, C_ALL), F32, kind="ExternalInput").ap()
    out = nc.dram_tensor("out_x", (1, T, D), F32, kind="ExternalOutput").ap()
    build(nc, args[0], consts, *args[1:], out)
    r = _run(nc, [arrays], core_ids=[0])
    return r.results[0]["out_x"]
```

```python
from contextlib import ExitStack

import numpy as np

import concourse.bass as bass
from concourse import mybir

F32 = mybir.dt.float32
I32 = mybir.dt.int32
ALU = mybir.AluOpType
ACT = mybir.ActivationFunctionType
AX_X = mybir.AxisListType.X

P = 128
D = 1024
KD = D // P
T = 256
TT = T // P
DEPTH = 2
DN_H, DN_D = 4, 128
DN_W = DN_H * DN_D
SB_H, SB_D = 8, 64
NPR = TT * DN_H
D_FF = 2816
N_EXP = 8
FF_E = 3584
EPS = 1e-6
SLOTS = 96
ROUND_LIMITS = (SLOTS, 2 * SLOTS)

FC = 256
SLOT = 2 * KD * FC + (FC // P) * D
NSLOT = 4
PARTS = 3
LANDED = 16 * PARTS
FFN_CH = D_FF // FC
MOE_CH = FF_E // FC
C_BA = 4 * DN_W
C_Q = C_BA + 2 * DN_H
IN_RANGES = (((C_BA, C_Q), (0, 640)), ((640, 1408),), ((1408, 2048),),
             ((C_Q, C_Q + 512),), ((C_Q + 512, C_Q + 1024),), ((C_Q + 1024, C_Q + 1536),))
IN_WIDTH = tuple(sum(b - a for a, b in r) for r in IN_RANGES)
N_IN = len(IN_RANGES)
N_MIX = N_IN + 2
FIRST_FFN = N_MIX
FIRST_MIX = (0, N_MIX + FFN_CH)
FIRST_MOE = 2 * N_MIX + FFN_CH
N_STEPS = 25
LEVELS = 7

C_ID = 0
C_UINC = C_ID + P
C_TRI = C_UINC + P
C_SB = C_TRI + P
C_LVL = C_SB + 3 * P
C_IOTA = C_LVL + LEVELS * P
C_W8 = C_IOTA + SLOTS
C_ALL = C_W8 + N_EXP

CONV_K = 4
CONV_T = 3 * DN_W // P
CONV_ROWS = DEPTH * CONV_K * CONV_T
R_MIX, R_FFN, R_DN, R_SB = 0, DEPTH * KD, 2 * DEPTH * KD, 2 * DEPTH * KD + DEPTH
NORM_ROWS = 2 * DEPTH * KD + 2 * DEPTH


def proj_steps():
    s = [("ba", 0, 0, 0)]
    for m in range(CONV_T):
        s.append(("conv", m, 0, 8 + m * P) if m < 5 else ("conv", m, 1, (m - 5) * P) if m < 11 else ("conv", m, 2, 0))
    s += [("z", 0, 2, P), ("z", 1, 2, P)]
    for i in range(4):
        s += [("sq", i, 3, i * P), ("sk", i, 4, i * P)]
    s += [("sv", 0, 5, 0), ("sv", 1, 5, 0)]
    return s


STEPS = proj_steps()
S_Z, S_SB, S_FILL = 13, 15, 18


def step_bank(n):
    return 4 + n % 4 if n < S_FILL else 7


BANK_PREV = {n: max((m for m in range(n) if step_bank(m) == step_bank(n)), default=None) for n in range(N_STEPS)}
LAST_STEP = {max(n for n, s in enumerate(STEPS) if s[2] == c): c for c in range(N_IN)}


def build(nc, x_in, consts, norm_mix_pre, norm_mix_post, norm_ffn_pre, norm_ffn_post, w_in, conv_w,
          dn_a_log, dn_dt_bias, dn_norm_w, sb_norm_w, w_out, ffn_gate, ffn_up, ffn_down, router_w,
          moe_gate, moe_up, moe_down, out):
    with ExitStack() as ctx:
        def sb(name, cols, dt=F32):
            return ctx.enter_context(nc.sbuf_tensor(name, [P, cols], dt))

        def sem(name):
            return ctx.enter_context(nc.semaphore(name))

        ps = ctx.enter_context(nc.psum_tensor("ps", [P, 8, 512], F32))

        def bank(b, n=1):
            return ps[:, b:b + n, :].rearrange("p b c -> p (b c)")

        ring = sb("ring", NSLOT * SLOT)
        cst = sb("cst", C_ALL)
        prm = sb("prm", CONV_ROWS + NORM_ROWS)
        headp = sb("headp", 2 * DEPTH * DN_H)
        routw = sb("routw", KD * N_EXP)
        x_sb = sb("x_sb", TT * D)
        h_sb = sb("h_sb", TT * D)
        hT_sb = sb("hT_sb", TT * D)
        wT01 = sb("wT01", 2 * 3 * P)
        wT45 = sb("wT45", 2 * 3 * P)
        wpost = sb("wpost", D)
        qk_sb = sb("qk_sb", DN_H * 2 * T)
        bv_sb = sb("bv_sb", NPR * P)
        kend_sb = sb("kend_sb", DN_H * P)
        sbq = sb("sbq", 4 * T)
        sbk = sb("sbk", 4 * T)
        DR_sb = sb("DR_sb", NPR * P)
        LT_sb = sb("LT_sb", NPR * P)
        AT_sb = sb("AT_sb", NPR * P)
        X_sb = sb("X_sb", NPR * P)
        XT_sb = sb("XT_sb", NPR * P)
        BM = sb("BM", 2 * NPR * P)
        Vn_sb = sb("Vn_sb", 2 * DN_H * P)
        SR = sb("SR", 2 * DN_H * P)
        sbz = sb("sbz", 2 * 3 * P)
        sbe = sb("sbe", 3 * P)
        sbp = sb("sbp", 2 * 3 * P)
        small = sb("small", 416)
        rounds_i = sb("rounds_i", 1, I32)

        def v3(t, a, lo=0, n=None):
            n = n or t.shape[1] - lo
            return t[:, lo:lo + n].rearrange("p (a b) -> p a b", a=a)

        ident = cst[:, C_ID:C_ID + P]
        uinc = cst[:, C_UINC:C_UINC + P]
        tri = cst[:, C_TRI:C_TRI + P]
        sbmask = cst[:, C_SB:C_SB + 3 * P]
        ustrict = cst[:, C_SB:C_SB + P]
        ones = cst[:, C_SB + P:C_SB + 2 * P]
        iota = cst[:, C_IOTA:C_IOTA + SLOTS]
        w8 = cst[:, C_W8:C_W8 + N_EXP]
        xv = v3(x_sb, TT)
        hv = v3(h_sb, TT)
        hT = v3(hT_sb, KD)
        mixT = hT

        def wT(h):
            return (wT01, DR_sb, wT45, hT_sb)[h // 2][:, h % 2 * 3 * P:(h % 2 + 1) * 3 * P]

        qk = qk_sb[:, :].rearrange("p (h k t) -> p h k t", h=DN_H, k=2)
        vT = v3(X_sb, DN_H)
        bv = v3(bv_sb, NPR)
        kend = v3(kend_sb, DN_H)
        sq_v, sk_v = v3(sbq, 4), v3(sbk, 4)
        DR, LT, AT, X, XT = (v3(t, NPR) for t in (DR_sb, LT_sb, AT_sb, X_sb, XT_sb))
        DF = XT
        diag_g, diag_b = LT, AT
        BT = v3(BM, NPR, 0, NPR * P)
        M1 = v3(BM, NPR, NPR * P, NPR * P)
        squares = v3(BM, 8)
        Vn = v3(Vn_sb, NPR)
        S = v3(SR, DN_H, 0, DN_H * P)
        RH1 = v3(SR, DN_H, DN_H * P, DN_H * P)
        zm = v3(sbz, 2)
        sp = v3(sbp, 2)
        dn_o = v3(LT_sb, TT)
        dn_sq = v3(AT_sb, TT)
        post_tmp = (DR_sb, LT_sb)
        act_junk = (XT_sb[:, :], X_sb[:, :])
        rows = BM
        wpost_ffn = sbq[:, :]

        at = [0]

        def cols(n):
            at[0] += n
            return small[:, at[0] - n:at[0]]

        ssx, rsx, ssum = cols(2 * TT), cols(TT), cols(TT)
        mhalf = cols(16)
        negA = cols(2 * DN_H)
        nsum, rn = cols(16), cols(16)
        ba = cols(16)
        aa, sabs, sln, spl, g_log = cols(8), cols(8), cols(8), cols(8), cols(8)
        eb, beta = cols(8), cols(8)
        gsum = cols(16)
        gdiff, egl, kcoef = cols(4), cols(4), cols(4)
        eg, scoef, coefq, br = cols(8), cols(4), cols(8), cols(8)
        dss, drs = cols(8), cols(8)
        sss, srs = cols(16), cols(16)
        lg, sel1, sel2, lg2, cand, sel, gate, rank = (cols(16) for _ in range(8))
        m1, m2, mx, ge, gd, g1, g2 = (cols(2) for _ in range(7))
        cmax, cgt, ctwo = cols(1), cols(1), cols(1)
        cur_rank, cur_gate = cols(2 * TT), cols(2 * TT)
        assert at[0] <= 416
        rk, rq = rn[:, 0:8], rn[:, 8:16]

        ffn_hid = v3(LT_sb, 4)
        ffn_sg = v3(AT_sb, 4)
        moe_y = qk_sb
        moe_yv = v3(qk_sb, TT)
        xgT = v3(bv_sb, KD, 0, KD * SLOTS)
        onehot = [v3(AT_sb, TT, j * TT * SLOTS, TT * SLOTS) for j in range(2)]
        onehotT = [X_sb[0:SLOTS, j * T:(j + 1) * T] for j in range(2)]
        moe_sg = [v3(LT_sb, 2, j * 2 * SLOTS, 2 * SLOTS) for j in range(2)]
        moe_hid = [v3(LT_sb, 2, (2 + j) * 2 * SLOTS, 2 * SLOTS) for j in range(2)]
        yT = v3(BM, KD, 0, KD * SLOTS)
        y_tok = BM[0:SLOTS, D:2 * D]

        ring_landed = [sem(f"ring_landed{i}") for i in range(NSLOT)]
        ring_used = sem("ring_used")
        x_landed = [sem(f"x_landed{t}") for t in range(TT)]
        consts_landed, rows_landed, heads_landed, router_landed = (
            sem(n) for n in ("consts_landed", "rows_landed", "heads_landed", "router_landed"))
        wpost_landed, wpostf_landed, out_landed = (sem(n) for n in ("wpost_landed", "wpostf_landed", "out_landed"))
        params_ps, params_ready, half_ready, expA, negA_ready = (
            sem(n) for n in ("params_ps", "params_ready", "half_ready", "expA", "negA_ready"))
        ss_ready, rstd_mean, rstd_ready, h_dve, h_act = (
            sem(n) for n in ("ss_ready", "rstd_mean", "rstd_ready", "h_dve", "h_act"))
        hT_ps, hT_dve, hT_act = (sem(n) for n in ("hT_ps", "hT_dve", "hT_act"))
        proj_done, conv_base, conv_taps, conv_silu, qk_squares, z_gate, ba_copied, sb_copied = (
            sem(n) for n in ("proj_done", "conv_base", "conv_taps", "conv_silu", "qk_squares", "z_gate",
                             "ba_copied", "sb_copied"))
        norms_ps, norms_sum, norms_ready, v_ps, kT_ps = (
            sem(n) for n in ("norms_ps", "norms_sum", "norms_ready", "v_ps", "kT_ps"))
        gate_in, gate_exp, gates_ready, gcum_ps, gcum_ready, gexp_ready, coef_ready, bv_ready, kend_ready = (
            sem(n) for n in ("gate_in", "gate_exp", "gates_ready", "gcum_ps", "gcum_ready", "gexp_ready",
                             "coef_ready", "bv_ready", "kend_ready"))
        diag_ready, bc_ps, decay_in, decay_exp, decay_ready, betadecay_ready, kk_ps, LT_ready, AT_ready = (
            sem(n) for n in ("diag_ready", "bc_ps", "decay_in", "decay_exp", "decay_ready",
                             "betadecay_ready", "kk_ps", "LT_ready", "AT_ready"))
        BT_ready, M1_ps, M1_ready, XM_ps, XTM_ps, X_ready, XT_ready = (
            sem(n) for n in ("BT_ready", "M1_ps", "M1_ready", "XM_ps", "XTM_ps", "X_ready", "XT_ready"))
        vnew_ps, vnew_ready, state_ps, state_ready, ks_ps, rhs1_ready, dno_ps = (
            sem(n) for n in ("vnew_ps", "vnew_ready", "state_ps", "state_ready", "ks_ps", "rhs1_ready", "dno_ps"))
        dn_out, dn_rstd_in, dn_rstd, mixed_dn = (sem(n) for n in ("dn_out", "dn_rstd_in", "dn_rstd", "mixed_dn"))
        sbz_ps, sbz_ready, sb_soft, sb_softplus, sb_keep, sbc_ps, sb_expo, sb_weight, sb_wmask, sbo_ps = (
            sem(n) for n in ("sbz_ps", "sbz_ready", "sb_soft", "sb_softplus", "sb_keep", "sbc_ps", "sb_expo",
                             "sb_weight", "sb_wmask", "sbo_ps"))
        sb_sq, sb_ss, sb_rstd_in, sb_rstd, mixed_sb = (
            sem(n) for n in ("sb_sq", "sb_ss", "sb_rstd_in", "sb_rstd", "mixed_sb"))
        mixT_ps, mixT_dve, mixT_act, out_t0 = (sem(n) for n in ("mixT_ps", "mixT_dve", "mixT_act", "out_t0"))
        post_ss, post_mean, post_rstd, post_w, x_ready = (
            sem(n) for n in ("post_ss", "post_mean", "post_rstd", "post_w", "x_ready"))
        gu_ps, sg_ready, hid_ready, down_done = (sem(n) for n in ("gu_ps", "sg_ready", "hid_ready", "down_done"))
        router_ps, route_step, route_exp, sel_ready, rank_ps, rounds_ready, moe_zero = (
            sem(n) for n in ("router_ps", "route_step", "route_exp", "sel_ready", "rank_ps", "rounds_ready",
                             "moe_zero"))
        cur_ready, onehot_ready, gather_ps, xg_ready, ohT_ps, ohT_ready = (
            sem(n) for n in ("cur_ready", "onehot_ready", "gather_ps", "xg_ready", "ohT_ps", "ohT_ready"))
        mgu_ps, msg_ready, mhid_ready, yT_ready, y_ps, y_act, y_dve, scatter_ps, moe_acc = (
            sem(n) for n in ("mgu_ps", "msg_ready", "mhid_ready", "yT_ready", "y_ps", "y_act", "y_dve",
                             "scatter_ps", "moe_acc"))

        def bcl(ap, n):
            return ap.unsqueeze(2).broadcast_to([ap.shape[0], ap.shape[1], n])

        def bcm(ap, n):
            return ap.unsqueeze(1).broadcast_to([ap.shape[0], n, ap.shape[1]])

        def slot_of(n):
            return ring[:, (n % NSLOT) * SLOT:(n % NSLOT + 1) * SLOT]

        def chunk_landed(eng, n, extra=0):
            eng.wait_ge(ring_landed[n % NSLOT], extra + LANDED * (n // NSLOT + 1))

        def gate_up_down(n):
            s = slot_of(n)
            g = s[:, 0:KD * FC].rearrange("p (k f) -> p k f", k=KD)
            u = s[:, KD * FC:2 * KD * FC].rearrange("p (k f) -> p k f", k=KD)
            d = s[:, 2 * KD * FC:SLOT].rearrange("p (i d) -> p i d", i=FC // P)
            return g, u, d

        def in_cols(n, width):
            return slot_of(n)[:, 0:KD * width].rearrange("p (k c) -> p k c", k=KD)

        def step_sem(L, n):
            if n in LAST_STEP:
                return ring_used, FIRST_MIX[L] + LAST_STEP[n] + 1
            before = sum(1 for m in range(n) if m not in LAST_STEP)
            return proj_done, (N_STEPS - N_IN) * L + before + 1

        def evac_sem(L, n):
            kind, i = STEPS[n][:2]
            if kind == "ba":
                return ba_copied, L + 1
            if kind == "conv":
                return conv_taps, 3 * (CONV_T * L + i + 1)
            if kind == "z":
                return z_gate, TT * L + i + 1
            return sb_copied, (N_STEPS - S_SB) * L + n - S_SB + 1

        def half(h):
            return slice(h * 512, (h + 1) * 512)

        block = ctx.enter_context(nc.Block())

        @block.sync
        def _(sp_):
            for t in range(TT):
                sp_.dma_start(xv[:, t, :], x_in[0, t * P:(t + 1) * P, :]).then_inc(x_landed[t], 16)
            sp_.dma_start(cst[:, :], consts).then_inc(consts_landed, 16)

            def free_slot(n):
                if n >= NSLOT:
                    sp_.wait_ge(ring_used, n - NSLOT + 1)

            def load_rows(n, ranges, src):
                free_slot(n)
                dst = in_cols(n, sum(b - a for a, b in ranges))
                src = src.rearrange("(k p) c -> p k c", p=P)
                at = 0
                for i, (a, b) in enumerate(ranges):
                    cuts = (0, KD) if i < len(ranges) - 1 else (0, 4, KD) if len(ranges) > 1 else (0, 3, 6, KD)
                    for lo, hi in zip(cuts, cuts[1:]):
                        sp_.dma_start(dst[:, lo:hi, at:at + b - a], src[:, lo:hi, a:b])\
                           .then_inc(ring_landed[n % NSLOT], 16)
                    at += b - a

            def load_mixer(L):
                for c in range(N_IN):
                    load_rows(FIRST_MIX[L] + c, IN_RANGES[c], w_in[L])
                for h in range(2):
                    load_rows(FIRST_MIX[L] + N_IN + h, ((h * 512, (h + 1) * 512),), w_out[L])

            def load_ffn(n, wg, wu, wd):
                g, u, d = gate_up_down(n)
                s = ring_landed[n % NSLOT]
                sp_.dma_start(g, wg.rearrange("(k p) f -> p k f", p=P)).then_inc(s, 16)
                sp_.dma_start(u, wu.rearrange("(k p) f -> p k f", p=P)).then_inc(s, 16)
                sp_.dma_start(d, wd.rearrange("(i p) d -> p i d", p=P)).then_inc(s, 16)

            load_mixer(0)
            for c in range(FFN_CH):
                free_slot(FIRST_FFN + c)
                f = slice(c * FC, (c + 1) * FC)
                load_ffn(FIRST_FFN + c, ffn_gate[0][:, f], ffn_up[0][:, f], ffn_down[0][f, :])
            load_mixer(1)

            def moe_pair(pair, it):
                for j in range(2):
                    for c in range(MOE_CH):
                        n = FIRST_MOE + j * MOE_CH + c
                        sp_.wait_ge(ring_used, it * (2 * MOE_CH) + (n - NSLOT + 1))
                        f = slice(c * FC, (c + 1) * FC)
                        e = pair * 2 + j
                        load_ffn(n, moe_gate[0, e][:, f], moe_up[0, e][:, f], moe_down[0, e][f, :])

            with sp_.Fori(0, N_EXP // 2) as pair:
                moe_pair(pair, pair)
            sp_.wait_ge(rounds_ready, 1)
            rounds = sp_.value_load(rounds_i[0:1, 0:1], min_val=1, max_val=3)
            with sp_.If(rounds > 1):
                with sp_.Fori(1, rounds) as r:
                    with sp_.Fori(0, N_EXP // 2) as pair:
                        moe_pair(pair, r * (N_EXP // 2) + pair)
            for t in range(TT):
                sp_.wait_ge(x_ready, 2 * (3 * TT + t + 1))
                sp_.dma_start(out[0].rearrange("(t p) d -> p t d", p=P)[:, t, :], xv[:, t, :]).then_inc(out_landed, 16)
            sp_.wait_ge(out_landed, 32)

        @block.tensor
        def _(pe):
            mm = nc.tensor.matmul

            pe.wait_ge(consts_landed, 16)
            pe.wait_ge(rows_landed, 16 * 6)
            nc.tensor.transpose(bank(4)[:, 0:CONV_ROWS], rows[0:CONV_ROWS, 0:P],
                                ident[0:CONV_ROWS, 0:CONV_ROWS])
            nc.tensor.transpose(bank(4)[:, CONV_ROWS:CONV_ROWS + NORM_ROWS], rows[0:NORM_ROWS, P:2 * P],
                                ident[0:NORM_ROWS, 0:NORM_ROWS]).then_inc(params_ps, 1)

            def transpose_h(u):
                for t in range(TT):
                    for k in range(KD):
                        if k % 4 == 0:
                            pe.wait_ge(h_act if k else h_dve, TT * u + t + 1)
                        o = (k % 2) * T + t * P
                        ins = nc.tensor.transpose(bank(k // 2)[:, o:o + P], hv[:, t, k * P:(k + 1) * P], ident)
                        if t and k % 2:
                            ins.then_inc(hT_ps, 1)

            def hT_wait(u, k):
                pe.wait_ge(hT_act if k // 2 % 2 else hT_dve, 4 * u + 2 * (k // 4) + k % 2 + 1)

            def project(L, n):
                kind, i, c, col = STEPS[n]
                if BANK_PREV[n] is not None:
                    pe.wait_ge(*evac_sem(L, BANK_PREV[n]))
                chunk = FIRST_MIX[L] + c
                chunk_landed(pe, chunk)
                w = in_cols(chunk, IN_WIDTH[c])
                o = bank(step_bank(n))
                if kind in ("conv", "sq", "sk"):
                    for k in range(KD):
                        ins = mm(o[:, 0:T], w[:, k, col:col + P], hT[:, k, :], start=(k == 0), stop=(k == KD - 1))
                elif kind == "ba":
                    for t in range(TT):
                        for k in range(KD):
                            if t == 0:
                                hT_wait(2 * L, k)
                            ins = mm(o[:, t * 8:(t + 1) * 8], hT[:, k, t * P:(t + 1) * P], w[:, k, col:col + 8],
                                     start=(k == 0), stop=(k == KD - 1))
                else:
                    for k in range(KD):
                        ins = mm(o, hT[:, k, i * P:(i + 1) * P], w[:, k, col:col + 512],
                                 start=(k == 0), stop=(k == KD - 1))
                ins.then_inc(step_sem(L, n)[0], 1)

            def sb_scores(L, h):
                if h:
                    pe.wait_ge(sb_expo, SB_H * L + h)
                else:
                    pe.wait_ge(*evac_sem(L, S_Z + 1))
                pe.wait_ge(*evac_sem(L, S_SB + 1 + 2 * (h // 2)))
                r = (h % 2) * SB_D
                kh, qh = sk_v[r:r + SB_D, h // 2, :], sq_v[r:r + SB_D, h // 2, :]
                o = bank(6)
                mm(o[:, 0:T], kh[:, 0:P], qh[:, 0:T], start=True, stop=True)
                mm(o[:, T:T + P], kh[:, P:T], qh[:, P:T], start=True, stop=True).then_inc(sbz_ps, 1)

            def sb_cumsum(L, h):
                pe.wait_ge(sb_keep, SB_H * L + h + 1)
                o = bank(6)
                mm(o[:, 0:3 * P], tri, sp[:, h % 2, :], start=True, stop=True)
                mm(o[:, P:2 * P], ones, sp[:, h % 2, 2 * P:3 * P], start=False, stop=True,
                   skip_group_check=True).then_inc(sbc_ps, 1)

            def sb_output(L):
                pe.wait_ge(sb_wmask, SB_H * (L + 1))
                pe.wait_ge(sb_expo, SB_H * (L + 1))
                pe.wait_ge(*evac_sem(L, N_STEPS - 1))
                for t in range(TT):
                    for h in range(SB_H):
                        o = bank(6 + t)[:, h * SB_D:(h + 1) * SB_D]
                        v = [hv[:, s, DN_W + h * SB_D:DN_W + (h + 1) * SB_D] for s in range(TT)]
                        ins = mm(o, wT(h)[:, t * P:(t + 1) * P], v[0], start=True, stop=(t == 0))
                        if t == 1:
                            ins = mm(o, wT(h)[:, 2 * P:3 * P], v[1], start=False, stop=True)
                    ins.then_inc(sbo_ps, 1)

            def qk_norms(L):
                pe.wait_ge(qk_squares, 8 * (L + 1))
                for kind in range(2):
                    for t in range(TT):
                        for h in range(DN_H):
                            c = kind * 8 + t * DN_H + h
                            ins = mm(bank(2)[:, c:c + 1], squares[:, (1 - kind) * 4 + h, t * P:(t + 1) * P],
                                     ones[:, 0:1], start=True, stop=True)
                ins.then_inc(norms_ps, 1)

            def k_transposes(L):
                for h in range(DN_H):
                    ins = nc.tensor.transpose(bank(3)[:, h * P:(h + 1) * P], qk[:, h, 0, 0:P], ident)
                ins.then_inc(kT_ps, 1)

            def v_transposes(L):
                pe.wait_ge(conv_silu, CONV_T * (L + 1))
                for t in range(TT):
                    for h in range(DN_H):
                        ins = nc.tensor.transpose(bank(t)[:, h * P:(h + 1) * P], vT[:, h, t * P:(t + 1) * P], ident)
                    ins.then_inc(v_ps, 1)

            def decay_sums(L):
                pe.wait_ge(gates_ready, 5 * L + 4)
                mm(bank(0)[:, 0:8], uinc, g_log, start=True, stop=True)
                mm(bank(0)[:, 8:16], ones, g_log, start=True, stop=True).then_inc(gcum_ps, 1)

            def broadcast(L, n, dg):
                pe.wait_ge(diag_ready, 2 * L + n + 1)
                for b in range(2):
                    ins = mm(bank(2 * n + b), ones, dg[:, 4 * b:4 * b + 4, :], start=True, stop=True)
                ins.then_inc(bc_ps, 1)

            def key_products(L):
                pe.wait_ge(bv_ready, 2 * (L + 1))
                pe.wait_ge(betadecay_ready, 2 * (L + 1))
                for pr in range(NPR):
                    t, h = pr // DN_H, pr % DN_H
                    o = bank(pr // 2)[:, (pr % 2) * T:(pr % 2 + 1) * T]
                    ins = mm(o, qk[:, h, 0, t * P:(t + 1) * P], qk[:, h, :, t * P:(t + 1) * P],
                             start=True, stop=True)
                    if pr % 4 == 3:
                        ins.then_inc(kk_ps, 1)

            def level_product(L, l, g):
                pe.wait_ge(BT_ready, 2 * (LEVELS * L + l) + g + 1)
                if l == 0:
                    pe.wait_ge(AT_ready, 2 * (L + 1))
                    pe.wait_ge(LT_ready, 2 * (L + 1))
                else:
                    pe.wait_ge(X_ready, 2 * (6 * L + l - 1) + g + 1)
                    if l >= 2:
                        pe.wait_ge(M1_ready, 2 * (6 * L + l - 2) + g + 1)
                for pr in range(4 * g, 4 * g + 4):
                    rhs = ident if l == 0 else X[:, pr, :]
                    ins = mm(bank(g)[:, (pr % 4) * P:(pr % 4 + 1) * P], BT[:, pr, :], rhs, start=True, stop=True)
                ins.then_inc(M1_ps, 1)

            def level_update(L, l, g):
                pe.wait_ge(M1_ready, 2 * (6 * L + l - 1) + g + 1)
                pe.wait_ge(XT_ready, 2 * (LEVELS * L + l - 1) + g + 1)
                if l == 1:
                    pe.wait_ge(*evac_sem(L, 17))
                if l < LEVELS - 1:
                    for pr in range(4 * g, 4 * g + 4):
                        ins = mm(bank(2 + g)[:, (pr % 4) * P:(pr % 4 + 1) * P], XT[:, pr, :], M1[:, pr, :],
                                 start=True, stop=True)
                    ins.then_inc(XM_ps, 1)
                for pr in range(4 * g, 4 * g + 4):
                    ins = mm(bank(4 + g)[:, (pr % 4) * P:(pr % 4 + 1) * P], M1[:, pr, :], XT[:, pr, :],
                             start=True, stop=True)
                ins.then_inc(XTM_ps, 1)

            def per_head(b, lhs, rhs, signal):
                for h in range(DN_H):
                    ins = mm(bank(b)[:, h * P:(h + 1) * P], lhs(h), rhs(h), start=True, stop=True)
                if signal is not None:
                    ins.then_inc(signal, 1)

            def out_part(L, ks, mine):
                c = FIRST_MIX[L] + N_IN
                for t in range(TT):
                    for hf in range(2):
                        w = in_cols(c + hf, 512)
                        if mine == 0:
                            pe.wait_ge(*((mixT_dve, 2 * L + 1), (mixT_act, 2 * L + 1))[hf] if t == 0 else
                                       (mixed_sb, TT * (L + 1)))
                        for n, k in enumerate(ks):
                            if t == 0 and hf == 0:
                                pe.wait_ge(mixT_act if n // 2 else mixT_dve, 2 * L + mine + 1)
                            ins = mm(bank(4 + 2 * t + hf), mixT[:, k, t * P:(t + 1) * P], w[:, k, :],
                                     start=(mine == 0 and n == 0), stop=(mine == 1 and n == 3))
                    if mine:
                        ins.then_inc(*((out_t0, 1) if t == 0 else (ring_used, 2)))

            def mix_transposes(ks, banks):
                for b, pair in zip(banks, (ks[0:2], ks[2:4])):
                    for i, k in enumerate(pair):
                        for t in range(TT):
                            o = i * T + t * P
                            ins = nc.tensor.transpose(bank(b)[:, o:o + P], hv[:, t, k * P:(k + 1) * P], ident)
                    ins.then_inc(mixT_ps, 1)

            def mixer(L):
                transpose_h(2 * L)
                for n in range(0, 3):
                    project(L, n)
                decay_sums(L)
                for n in range(3, 5):
                    project(L, n)
                pe.wait_ge(gcum_ready, L + 1)
                broadcast(L, 0, diag_g)
                for n in range(5, 11):
                    project(L, n)
                qk_norms(L)
                k_transposes(L)
                for n in range(11, 14):
                    project(L, n)
                pe.wait_ge(norms_sum, L + 1)
                pe.wait_ge(kend_ready, L + 1)
                broadcast(L, 1, diag_b)
                project(L, 14)
                pe.wait_ge(decay_in, NPR * (L + 1))
                v_transposes(L)
                project(L, 15)
                key_products(L)
                project(L, 16)
                project(L, 17)
                sb_scores(L, 0)
                for l in range(LEVELS):
                    level_product(L, l, 0)
                    level_product(L, l, 1)
                    project(L, S_FILL + l)
                    sb_cumsum(L, l)
                    if l:
                        level_update(L, l, 0)
                        level_update(L, l, 1)
                    sb_scores(L, l + 1)
                pe.wait_ge(XT_ready, 2 * LEVELS * (L + 1))
                per_head(0, lambda h: XT[:, h, :], lambda h: bv[:, h, :], vnew_ps)
                pe.wait_ge(vnew_ready, 2 * L + 1)
                per_head(1, lambda h: kend[:, h, :], lambda h: Vn[:, h, :], state_ps)
                sb_cumsum(L, SB_H - 1)
                pe.wait_ge(state_ready, L + 1)
                per_head(2, lambda h: qk[:, h, 0, P:T], lambda h: S[:, h, :], ks_ps)
                per_head(3, lambda h: qk[:, h, 1, P:T], lambda h: S[:, h, :], None)
                per_head(1, lambda h: AT[:, h, :], lambda h: Vn[:, h, :], None)
                pe.wait_ge(rhs1_ready, 2 * (L + 1))
                per_head(0, lambda h: XT[:, 4 + h, :], lambda h: RH1[:, h, :], vnew_ps)
                sb_output(L)
                pe.wait_ge(vnew_ready, 2 * L + 2)
                per_head(2, lambda h: AT[:, 4 + h, :], lambda h: Vn[:, 4 + h, :], dno_ps)
                pe.wait_ge(mixed_sb, TT * (L + 1))
                mix_transposes((4, 5, 6, 7), (4, 5))
                chunk_landed(pe, FIRST_MIX[L] + N_IN)
                chunk_landed(pe, FIRST_MIX[L] + N_IN + 1)
                out_part(L, (4, 5, 6, 7), 0)
                pe.wait_ge(mixed_dn, TT * (L + 1))
                mix_transposes((0, 1, 2, 3), (0, 3))
                out_part(L, (0, 1, 2, 3), 1)

            def dense_ffn():
                transpose_h(1)
                n_mt = D_FF // P

                def gate_up(mt):
                    c, i = FIRST_FFN + mt // 2, mt % 2
                    chunk_landed(pe, c)
                    g, u, _ = gate_up_down(c)
                    if mt >= 4:
                        pe.wait_ge(hid_ready, mt - 3)
                    for which, w in enumerate((g, u)):
                        for k in range(KD):
                            if mt == 0 and which == 0:
                                hT_wait(1, max(k, 1))
                            ins = mm(bank(mt % 4)[:, which * T:(which + 1) * T], w[:, k, i * P:(i + 1) * P],
                                     hT[:, k, :], start=(k == 0), stop=(k == KD - 1))
                    ins.then_inc(gu_ps, 1)

                def down(mt):
                    c, i = FIRST_FFN + mt // 2, mt % 2
                    d = gate_up_down(c)[2]
                    pe.wait_ge(hid_ready, mt + 1)
                    for t in range(TT):
                        for half in range(2):
                            ins = mm(bank(4 + 2 * t + half), ffn_hid[:, mt % 4, t * P:(t + 1) * P],
                                     d[:, i, half * 512:(half + 1) * 512], start=(mt == 0), stop=(mt == n_mt - 1))
                    ins.then_inc(ring_used if i else down_done, 1)

                for mt in range(n_mt):
                    gate_up(mt)
                    if mt >= 2:
                        down(mt - 2)
                down(n_mt - 2)
                down(n_mt - 1)

            mixer(0)
            dense_ffn()
            mixer(1)

            transpose_h(3)
            pe.wait_ge(router_landed, 16)
            rw = v3(routw, KD)
            for t in range(TT):
                for k in range(KD):
                    if t == 0:
                        hT_wait(3, k)
                    ins = mm(bank(4)[:, t * 8:(t + 1) * 8], hT[:, k, t * P:(t + 1) * P], rw[:, k, :],
                             start=(k == 0), stop=(k == KD - 1))
            ins.then_inc(router_ps, 1)
            pe.wait_ge(sel_ready, 1)
            r5 = bank(5)
            mm(r5[:, 0:8], ustrict, sel[:, 0:8], start=True, stop=True)
            mm(r5[:, 8:16], ustrict, sel[:, 8:16], start=True, stop=False)
            mm(r5[:, 8:16], ones, sel[:, 0:8], start=False, stop=True)
            mm(r5[:, 16:24], ones, sel[:, 0:8], start=True, stop=False)
            mm(r5[:, 16:24], ones, sel[:, 8:16], start=False, stop=True).then_inc(rank_ps, 1)
            pe.wait_ge(rounds_ready, 1)
            rounds = pe.value_load(rounds_i[0:1, 0:1], min_val=1, max_val=3)

            def gather(it, j):
                pe.wait_ge(onehot_ready, it * (2 * TT) + TT * (j + 1))
                for k in range(KD):
                    for t in range(TT):
                        ins = mm(bank(4 + k // 4)[:, (k % 4) * SLOTS:(k % 4 + 1) * SLOTS],
                                 hv[:, t, k * P:(k + 1) * P], onehot[j][:, t, :], start=(t == 0), stop=(t == 1))
                    if k % 4 == 3:
                        ins.then_inc(gather_ps, 1)
                for t in range(TT):
                    ins = nc.tensor.transpose(bank(6)[0:SLOTS, t * P:(t + 1) * P], onehot[j][:, t, :], ident)
                ins.then_inc(ohT_ps, 1)

            def m_gate_up(it, j, c):
                n = FIRST_MOE + j * MOE_CH + c
                chunk_landed(pe, n, it * (LANDED * 2 * MOE_CH // NSLOT))
                if c == 0:
                    pe.wait_ge(xg_ready, it * 4 + 2 * (j + 1))
                if c >= 2:
                    pe.wait_ge(mhid_ready, it * (2 * MOE_CH) + (j * MOE_CH + c - 1))
                g, u, _ = gate_up_down(n)
                for i in range(FC // P):
                    for which, w in enumerate((g, u)):
                        o = bank(c % 2)[:, (2 * which + i) * SLOTS:(2 * which + i + 1) * SLOTS]
                        for k in range(KD):
                            ins = mm(o, w[:, k, i * P:(i + 1) * P], xgT[:, k, :], start=(k == 0), stop=(k == KD - 1))
                ins.then_inc(mgu_ps, 1)

            def m_down(it, j, c):
                d = gate_up_down(FIRST_MOE + j * MOE_CH + c)[2]
                pe.wait_ge(mhid_ready, it * (2 * MOE_CH) + (j * MOE_CH + c + 1))
                if j == 1 and c == 0:
                    pe.wait_ge(yT_ready, it * 4 + 2)
                for i in range(FC // P):
                    for k in range(KD):
                        ins = mm(bank(2 + k // 4)[:, (k % 4) * SLOTS:(k % 4 + 1) * SLOTS],
                                 d[:, i, k * P:(k + 1) * P], moe_hid[c % 2][:, i, :],
                                 start=(c == 0 and i == 0 and k % 4 == 0),
                                 stop=(c == MOE_CH - 1 and i == 1), skip_group_check=True)
                ins.then_inc(ring_used, 1)

            def y_transposes(it, j):
                pe.wait_ge(yT_ready, it * 4 + 2 * (j + 1))
                for k in range(KD):
                    ins = nc.tensor.transpose(bank(4 + k // 4)[0:SLOTS, (k % 4) * P:(k % 4 + 1) * P],
                                              yT[:, k, :], ident)
                    if k % 4 == 3:
                        ins.then_inc(y_ps, 1)

            def scatter(it, j):
                pe.wait_ge(ohT_ready, it * 2 + (j + 1))
                pe.wait_ge(y_act, it * 2 + (j + 1))
                pe.wait_ge(y_dve, it * 2 + (j + 1))
                for t in range(TT):
                    for half in range(2):
                        ins = mm(bank((6, 4)[t] + half), onehotT[j][:, t * P:(t + 1) * P],
                                 y_tok[:, half * 512:(half + 1) * 512], start=True, stop=True)
                    ins.then_inc(scatter_ps, 1)

            with pe.Fori(0, rounds) as r:
                with pe.Fori(0, N_EXP // 2) as pair:
                    it = r * (N_EXP // 2) + pair
                    for j in range(2):
                        gather(it, j)
                        for c in range(MOE_CH):
                            m_gate_up(it, j, c)
                            if c:
                                m_down(it, j, c - 1)
                            if j == 1 and c == 0:
                                y_transposes(it, 0)
                            if j == 1 and c == 1:
                                scatter(it, 0)
                        m_down(it, j, MOE_CH - 1)
                    y_transposes(it, 1)
                    pe.wait_ge(moe_acc, it * 4 + 2)
                    scatter(it, 1)
                    pe.wait_ge(moe_acc, it * 4 + 4)

        @block.scalar
        def _(act):
            A = nc.scalar.activation

            act.dma_start(rows[0:CONV_ROWS, 0:P], conv_w.rearrange("l k (t p) -> (l k t) p", p=P))\
                .then_inc(rows_landed, 16)
            act.dma_start(rows[R_MIX:R_MIX + 16, P:2 * P], norm_mix_pre.rearrange("l (k p) -> (l k) p", p=P))\
                .then_inc(rows_landed, 16)
            act.dma_start(rows[R_FFN:R_FFN + 16, P:2 * P], norm_ffn_pre.rearrange("l (k p) -> (l k) p", p=P))\
                .then_inc(rows_landed, 16)
            act.dma_start(rows[R_DN:R_DN + 2, P:2 * P], dn_norm_w).then_inc(rows_landed, 16)
            act.dma_start(rows[R_SB:R_SB + 2, P:P + SB_D], sb_norm_w).then_inc(rows_landed, 16)
            act.dma_start(rows[R_SB:R_SB + 2, P + SB_D:2 * P], sb_norm_w).then_inc(rows_landed, 16)
            nc.scalar.preload_act_table_set("natural_log_exp_and_others")
            act.wait_ge(heads_landed, 32)
            A(negA, headp[:, 0:2 * DN_H], ACT.Exp).then_inc(expA, 1)

            def pre_norm(u):
                for t in range(TT):
                    for hf in range(2):
                        if u == 0:
                            act.wait_ge(x_landed[t], 16)
                        else:
                            act.wait_ge(x_ready, 2 * (TT * (u - 1) + t) + hf + 1)
                        A(act_junk[t][:, half(hf)], xv[:, t, half(hf)], ACT.Square,
                          accum_out=ssx[:, 2 * t + hf:2 * t + hf + 1]).then_inc(ss_ready, 1)
                for t in range(TT):
                    act.wait_ge(rstd_ready, TT * u + t + 1)
                    A(hv[:, t, half(1)], xv[:, t, half(1)], ACT.Copy, scale=rsx[:, t:t + 1]).then_inc(h_act, 1)

            def hT_act_tiles(u, row):
                for k in (2, 3, 6, 7):
                    act.wait_ge(hT_ps, 4 * u + k // 2 + 1)
                    if u == 0 and k == 2:
                        act.wait_ge(params_ready, 1)
                    A(hT[:, k, :], bank(k // 2)[:, k % 2 * T:(k % 2 + 1) * T], ACT.Copy,
                      scale=prm[:, CONV_ROWS + row + k:CONV_ROWS + row + k + 1]).then_inc(hT_act, 1)

            def post_norm_squares(u, wait, src):
                for t in range(TT):
                    wait(act, t)
                    for hf in range(2):
                        if hf:
                            act.wait_ge(post_w, 2 * (TT * u + t) + 1)
                        A(act_junk[t][:, half(hf)], src(t, hf), ACT.Square,
                          accum_out=ssx[:, 2 * t + hf:2 * t + hf + 1]).then_inc(post_ss, 1)

            def bank_half(t, hf):
                return bank(4 + 2 * t + hf)

            def conv_dst(m):
                return (qk[:, m, 1, :] if m < 4 else qk[:, m - 4, 0, :] if m < 8 else vT[:, m - 8, :])

            def mixer(L):
                pre_norm(2 * L)
                hT_act_tiles(2 * L, R_MIX + KD * L)
                nc.scalar.preload_act_table_set("natural_log_exp_and_others")
                act.wait_ge(gate_in, L + 1)
                A(sabs, aa, ACT.Abs).then_inc(gate_exp, 1)
                A(eb, ba.rearrange("p (t c) -> p t c", t=TT)[:, :, 0:4], ACT.Exp, scale=-1.0).then_inc(gate_exp, 1)
                act.wait_ge(gate_exp, 4 * L + 1)
                A(sln, sabs, ACT.Exp, scale=-1.0).then_inc(gate_exp, 1)
                act.wait_ge(gate_exp, 4 * L + 3)
                A(sabs, sln, ACT.Ln, bias=1.0).then_inc(gate_exp, 1)

                def conv_first(m):
                    act.wait_ge(*step_sem(L, m + 1))
                    w3 = L * CONV_K * CONV_T + 3 * CONV_T + m
                    A(conv_dst(m), bank(step_bank(m + 1))[:, 0:T], ACT.Copy, scale=prm[:, w3:w3 + 1])\
                        .then_inc(conv_base, 1)

                def silu(m):
                    act.wait_ge(conv_taps, 3 * (CONV_T * L + m + 1))
                    A(conv_dst(m), conv_dst(m), ACT.Silu).then_inc(conv_silu, 1)

                for m in range(2):
                    conv_first(m)
                act.wait_ge(gcum_ready, L + 1)
                A(eg, gsum[:, 0:8], ACT.Exp).then_inc(gexp_ready, 1)
                act.wait_ge(coef_ready, 5 * L + 1)
                A(egl, gdiff, ACT.Exp).then_inc(gexp_ready, 1)
                for m in range(2, 5):
                    conv_first(m)
                act.wait_ge(decay_in, 8 * (L + 1))
                A(DR_sb[:, :], DR_sb[:, :], ACT.Exp).then_inc(decay_exp, 1)
                for m in range(4):
                    silu(m)
                for m in range(5, CONV_T):
                    conv_first(m)
                    silu(m - 1)
                silu(CONV_T - 1)
                for t in range(TT):
                    act.wait_ge(*step_sem(L, S_Z + t))
                    A(hv[:, t, 0:DN_W], bank(step_bank(S_Z + t)), ACT.Silu).then_inc(z_gate, 1)
                nc.scalar.preload_act_table_set("natural_log_exp_and_others")

                def sb_copy(n):
                    kind, i = STEPS[n][0], STEPS[n][1]
                    act.wait_ge(*step_sem(L, n))
                    if kind == "sv":
                        dst, src = hv[:, i, DN_W:D], bank(step_bank(n))
                    else:
                        dst, src = (sq_v if kind == "sq" else sk_v)[:, i, :], bank(step_bank(n))[:, 0:T]
                    A(dst, src, ACT.Copy).then_inc(sb_copied, 1)

                if L:
                    act.wait_ge(x_ready, 4 * TT)
                for n in range(S_SB, S_FILL):
                    sb_copy(n)

                def m1_copy(l, g):
                    act.wait_ge(M1_ps, 2 * (LEVELS * L + l) + g + 1)
                    if l >= 2:
                        act.wait_ge(XTM_ps, 2 * (6 * L + l - 2) + g + 1)
                    A(M1[:, 4 * g:4 * g + 4, :], bank(g).rearrange("p (a b) -> p a b", a=4), ACT.Copy)\
                        .then_inc(M1_ready, 1)

                def sb_softplus_parts(h):
                    act.wait_ge(sbz_ready, SB_H * L + h + 1)
                    if h:
                        act.wait_ge(sb_softplus, SB_H * L + h)
                    n = 3 * (SB_H * L + h)
                    A(sbe[:, :], zm[:, h % 2, :], ACT.Abs).then_inc(sb_soft, 1)
                    act.wait_ge(sb_soft, n + 1)
                    A(sbe[:, :], sbe[:, :], ACT.Exp, scale=-1.0).then_inc(sb_soft, 1)
                    act.wait_ge(sb_soft, n + 2)
                    A(sbe[:, :], sbe[:, :], ACT.Ln, bias=1.0).then_inc(sb_soft, 1)

                def sb_weights(h):
                    act.wait_ge(sb_expo, SB_H * L + h + 1)
                    A(wT(h), zm[:, h % 2, :], ACT.Exp).then_inc(sb_weight, 1)

                for l in range(LEVELS):
                    sb_softplus_parts(l)
                    if l:
                        m1_copy(l, 0)
                        m1_copy(l, 1)
                    sb_copy(S_FILL + l)
                    sb_weights(l)
                act.wait_ge(vnew_ps, 2 * L + 1)
                A(Vn[:, 0:4, :], bank(0).rearrange("p (a b) -> p a b", a=4), ACT.Copy).then_inc(vnew_ready, 1)
                sb_softplus_parts(SB_H - 1)
                act.wait_ge(state_ps, L + 1)
                A(S, bank(1).rearrange("p (a b) -> p a b", a=4), ACT.Copy).then_inc(state_ready, 1)
                sb_weights(SB_H - 1)
                act.wait_ge(vnew_ps, 2 * L + 2)
                A(Vn[:, 4:8, :], bank(0).rearrange("p (a b) -> p a b", a=4), ACT.Copy).then_inc(vnew_ready, 1)
                for t in range(TT):
                    act.wait_ge(sbo_ps, 2 * L + t + 1)
                    A((sbz, sbp)[t][:, 0:512], bank(6 + t), ACT.Square).then_inc(sb_sq, 1)
                for n, b in ((1, 5), (3, 3)):
                    act.wait_ge(mixT_ps, 4 * L + n + 1)
                    col = CONV_ROWS + (R_SB if n == 1 else R_DN) + L
                    k = 6 if n == 1 else 2
                    A(mixT[:, k:k + 2, :], bank(b).rearrange("p (a b) -> p a b", a=2), ACT.Copy,
                      scale=prm[:, col:col + 1]).then_inc(mixT_act, 1)

                def through(eng, t):
                    eng.wait_ge(*((out_t0, L + 1) if t == 0 else (ring_used, FIRST_MIX[L] + N_MIX)))
                post_norm_squares(2 * L, through, bank_half)

            def dense_ffn():
                pre_norm(1)
                hT_act_tiles(1, R_FFN)
                for mt in range(D_FF // P):
                    act.wait_ge(gu_ps, mt + 1)
                    if mt >= 4:
                        act.wait_ge(hid_ready, mt - 3)
                    A(ffn_sg[:, mt % 4, :], bank(mt % 4)[:, 0:T], ACT.Silu).then_inc(sg_ready, 1)
                post_norm_squares(1, lambda eng, t: eng.wait_ge(ring_used, FIRST_FFN + FFN_CH), bank_half)

            mixer(0)
            dense_ffn()
            mixer(1)
            pre_norm(3)
            hT_act_tiles(3, R_FFN + KD)
            act.wait_ge(route_step, 10)
            A(ge, gd, ACT.Exp).then_inc(route_exp, 1)
            act.wait_ge(rounds_ready, 1)
            rounds = act.value_load(rounds_i[0:1, 0:1], min_val=1, max_val=3)
            with act.Fori(0, rounds) as r:
                with act.Fori(0, N_EXP // 2) as pair:
                    it = r * (N_EXP // 2) + pair

                    def yT_copy(j):
                        act.wait_ge(ring_used, it * (2 * MOE_CH) + (FIRST_MOE + (j + 1) * MOE_CH))
                        for b in range(2):
                            A(yT[:, 4 * b:4 * b + 4, :], bank(2 + b)[:, 0:4 * SLOTS].rearrange("p (a b) -> p a b", a=4),
                              ACT.Copy).then_inc(yT_ready, 1)

                    def y_copy(j):
                        act.wait_ge(y_ps, it * 4 + 2 * j + 1)
                        A(y_tok[:, 0:512], bank(4)[0:SLOTS, :], ACT.Copy).then_inc(y_act, 1)

                    for j in range(2):
                        act.wait_ge(ohT_ps, it * 2 + (j + 1))
                        A(onehotT[j], bank(6)[0:SLOTS, 0:T], ACT.Copy).then_inc(ohT_ready, 1)
                        if j == 1:
                            yT_copy(0)
                        for c in range(MOE_CH):
                            act.wait_ge(mgu_ps, it * (2 * MOE_CH) + (j * MOE_CH + c + 1))
                            if c >= 2:
                                act.wait_ge(mhid_ready, it * (2 * MOE_CH) + (j * MOE_CH + c - 1))
                            A(moe_sg[c % 2], bank(c % 2)[:, 0:2 * SLOTS].rearrange("p (a b) -> p a b", a=2),
                              ACT.Silu).then_inc(msg_ready, 1)
                            if j == 1 and c == 0:
                                y_copy(0)
                    yT_copy(1)
                    y_copy(1)
            post_norm_squares(3, lambda eng, t: eng.wait_ge(moe_acc, rounds * (2 * N_EXP)),
                              lambda t, hf: moe_yv[:, t, half(hf)])

        @block.vector
        def _(dve):
            V = nc.vector

            dve.wait_ge(expA, 1)
            V.tensor_scalar(negA, negA, -1.0, None, ALU.mult).then_inc(negA_ready, 1)
            dve.wait_ge(params_ps, 1)
            V.tensor_copy(prm[:, :], bank(4)[:, 0:CONV_ROWS + NORM_ROWS]).then_inc(params_ready, 1)
            dve.wait_ge(params_ready, 1)
            dve.wait_ge(negA_ready, 1)

            def normalise(u):
                for t in range(TT):
                    dve.wait_ge(rstd_ready, TT * u + t + 1)
                    V.tensor_scalar(hv[:, t, half(0)], xv[:, t, half(0)], rsx[:, t:t + 1], None, ALU.mult)\
                        .then_inc(h_dve, 1)

            def hT_dve_tiles(u, row):
                for k in (0, 1, 4, 5):
                    dve.wait_ge(hT_ps, 4 * u + k // 2 + 1)
                    V.tensor_scalar(hT[:, k, :], bank(k // 2)[:, k % 2 * T:(k % 2 + 1) * T],
                                    prm[:, CONV_ROWS + row + k:CONV_ROWS + row + k + 1], None,
                                    ALU.mult).then_inc(hT_dve, 1)

            def residual(u, through, source, w, landed):
                dve.wait_ge(*landed)
                for t in range(TT):
                    through(dve, t)
                    for n, hf in enumerate((1, 0)):
                        if n:
                            dve.wait_ge(post_ss, 2 * (TT * u + t) + 1)
                        V.tensor_tensor(post_tmp[t][:, half(hf)], source(t, hf), w[:, half(hf)], ALU.mult)\
                            .then_inc(post_w, 1)
                    dve.wait_ge(post_rstd, TT * u + t + 1)
                    dve.wait_ge(post_w, 2 * (TT * u + t + 1))
                    for hf in range(2):
                        V.scalar_tensor_tensor(xv[:, t, half(hf)], post_tmp[t][:, half(hf)], rsx[:, t:t + 1],
                                               xv[:, t, half(hf)], ALU.mult, ALU.add).then_inc(x_ready, 1)

            def bank_half(t, hf):
                return bank(4 + 2 * t + hf)

            def conv_dst(m):
                return (qk[:, m, 1, :] if m < 4 else qk[:, m - 4, 0, :] if m < 8 else vT[:, m - 8, :])

            def mixer(L):
                normalise(2 * L)
                hT_dve_tiles(2 * L, R_MIX + KD * L)
                def taps(m):
                    dve.wait_ge(conv_base, CONV_T * L + m + 1)
                    for n, i in enumerate((2, 1, 0)):
                        s = 3 - i
                        if n:
                            dve.wait_ge(conv_taps, 3 * (CONV_T * L + m) + n)
                        w = L * CONV_K * CONV_T + i * CONV_T + m
                        V.scalar_tensor_tensor(conv_dst(m)[:, s:T], bank(step_bank(m + 1))[:, 0:T - s],
                                               prm[:, w:w + 1], conv_dst(m)[:, s:T], ALU.mult, ALU.add)\
                            .then_inc(conv_taps, 1)

                g0, c0 = 5 * L, 5 * L
                dve.wait_ge(*step_sem(L, 0))
                V.tensor_copy(ba, bank(4)[:, 0:16]).then_inc(ba_copied, 1)
                dve.wait_ge(ba_copied, L + 1)
                a_v = ba.rearrange("p (t c) -> p t c", t=TT)[:, :, 4:8]
                dtb = headp[:, (DEPTH + L) * DN_H:(DEPTH + L + 1) * DN_H]
                V.tensor_tensor(aa.rearrange("p (t c) -> p t c", t=TT), a_v, bcm(dtb, TT), ALU.add)\
                    .then_inc(gate_in, 1)
                dve.wait_ge(gate_in, L + 1)
                dve.wait_ge(gate_exp, 4 * (L + 1))
                V.scalar_tensor_tensor(spl, aa, 0.0, sabs, ALU.max, ALU.add).then_inc(gates_ready, 1)
                V.tensor_scalar(eb, eb, 1.0, None, ALU.add).then_inc(gates_ready, 1)
                dve.wait_ge(gates_ready, g0 + 2)
                V.reciprocal(beta, eb).then_inc(gates_ready, 1)
                V.tensor_tensor(g_log.rearrange("p (t c) -> p t c", t=TT), spl.rearrange("p (t c) -> p t c", t=TT),
                                bcm(negA[:, L * DN_H:(L + 1) * DN_H], TT), ALU.mult).then_inc(gates_ready, 1)
                taps(0)
                taps(1)
                dve.wait_ge(gcum_ps, L + 1)
                V.tensor_copy(gsum, bank(0)[:, 0:16]).then_inc(gcum_ready, 1)
                dve.wait_ge(gcum_ready, L + 1)
                V.tensor_tensor(gdiff, gsum[:, 8:12], gsum[:, 0:4], ALU.subtract).then_inc(coef_ready, 1)
                for m in range(2, 4):
                    taps(m)
                dve.wait_ge(bc_ps, 2 * L + 1)
                for pr in range(NPR):
                    V.tensor_scalar(DR[:, pr, :], bank(0, 2)[:, pr * P:(pr + 1) * P], gsum[:, pr:pr + 1], 0.0,
                                    ALU.subtract, ALU.min).then_inc(decay_in, 1)
                for m in range(4, 10):
                    taps(m)
                dve.wait_ge(norms_ps, L + 1)
                V.tensor_scalar(nsum, bank(2)[:, 0:16], EPS, None, ALU.add).then_inc(norms_sum, 1)
                taps(10)
                dve.wait_ge(gates_ready, g0 + 4)
                dve.wait_ge(norms_ready, L + 1)
                V.tensor_tensor(br, beta, rk, ALU.mult).then_inc(gates_ready, 1)
                V.tensor_scalar(coefq, rq, float(DN_D) ** -0.5, None, ALU.mult).then_inc(coef_ready, 1)
                dve.wait_ge(gexp_ready, 2 * (L + 1))
                dve.wait_ge(gates_ready, g0 + 5)
                V.tensor_tensor(scoef, eg[:, 4:8], br[:, 4:8], ALU.mult).then_inc(coef_ready, 1)
                dve.wait_ge(coef_ready, c0 + 3)
                V.tensor_scalar(scoef, scoef, -1.0, None, ALU.mult).then_inc(coef_ready, 1)
                V.tensor_tensor(kcoef, egl, rk[:, 0:4], ALU.mult).then_inc(coef_ready, 1)
                dve.wait_ge(coef_ready, c0 + 5)
                dve.wait_ge(kT_ps, L + 1)
                V.tensor_tensor(kend, bank(3).rearrange("p (a b) -> p a b", a=4), bcl(kcoef, P), ALU.mult)\
                    .then_inc(kend_ready, 1)
                taps(11)
                dve.wait_ge(bc_ps, 2 * L + 2)
                dve.wait_ge(decay_ready, 2 * (L + 1))
                for g in range(2):
                    V.tensor_tensor(DF[:, 4 * g:4 * g + 4, :], DR[:, 4 * g:4 * g + 4, :],
                                    bank(2 + g).rearrange("p (a b) -> p a b", a=4), ALU.mult)\
                        .then_inc(betadecay_ready, 1)
                for t in range(TT):
                    dve.wait_ge(v_ps, 2 * L + t + 1)
                    V.tensor_tensor(bv[:, 4 * t:4 * t + 4, :], bank(t).rearrange("p (a b) -> p a b", a=4),
                                    bcl(beta[:, 4 * t:4 * t + 4], P), ALU.mult).then_inc(bv_ready, 1)

                def sb_mask(h):
                    dve.wait_ge(sbz_ps, SB_H * L + h + 1)
                    if h >= 2:
                        dve.wait_ge(sb_weight, SB_H * L + h - 1)
                    V.scalar_tensor_tensor(zm[:, h % 2, :], bank(6)[:, 0:3 * P], SB_D ** -0.5, sbmask,
                                           ALU.mult, ALU.mult).then_inc(sbz_ready, 1)

                def sb_plus(h):
                    dve.wait_ge(sb_soft, 3 * (SB_H * L + h + 1))
                    if h >= 2:
                        dve.wait_ge(sbc_ps, SB_H * L + h - 1)
                    dve.wait_ge(sbz_ready, SB_H * L + h + 1)
                    V.scalar_tensor_tensor(sp[:, h % 2, :], zm[:, h % 2, :], 0.0, sbe[:, :], ALU.max, ALU.add)\
                        .then_inc(sb_softplus, 1)

                def sb_exponent(h):
                    dve.wait_ge(sbc_ps, SB_H * L + h + 1)
                    V.tensor_tensor(zm[:, h % 2, :], zm[:, h % 2, :], bank(6)[:, 0:3 * P], ALU.subtract)\
                        .then_inc(sb_expo, 1)

                dve.wait_ge(betadecay_ready, 2 * (L + 1))
                for g in range(2):
                    dve.wait_ge(kk_ps, 2 * L + g + 1)
                    two = ps[:, 2 * g:2 * g + 2, :].rearrange("p b (a k c) -> p (b a) k c", a=2, k=2)
                    V.tensor_tensor(LT[:, 4 * g:4 * g + 4, :], two[:, :, 0, :], DF[:, 4 * g:4 * g + 4, :],
                                    ALU.mult).then_inc(LT_ready, 1)
                    V.tensor_tensor(AT[:, 4 * g:4 * g + 4, :], two[:, :, 1, :], DR[:, 4 * g:4 * g + 4, :],
                                    ALU.mult).then_inc(AT_ready, 1)
                dve.wait_ge(LT_ready, 2 * (L + 1))
                for l in range(LEVELS):
                    sb_mask(l)
                    sb_plus(l)
                    if l:
                        sb_exponent(l)
                    for g in range(2):
                        s = slice(4 * g, 4 * g + 4)
                        if l == 0:
                            dve.wait_ge(M1_ps, 2 * LEVELS * L + g + 1)
                            V.tensor_tensor(X[:, s, :], bcm(ident, 4), bank(g).rearrange("p (a b) -> p a b", a=4),
                                            ALU.subtract).then_inc(X_ready, 1)
                            V.tensor_tensor(XT[:, s, :], bcm(ident, 4), BT[:, s, :], ALU.subtract)\
                                .then_inc(XT_ready, 1)
                            continue
                        if l < LEVELS - 1:
                            dve.wait_ge(XM_ps, 2 * (5 * L + l - 1) + g + 1)
                            dve.wait_ge(X_ready, 2 * (6 * L + l - 1) + g + 1)
                            V.tensor_tensor(X[:, s, :], X[:, s, :], bank(2 + g).rearrange("p (a b) -> p a b", a=4),
                                            ALU.subtract).then_inc(X_ready, 1)
                        dve.wait_ge(XTM_ps, 2 * (6 * L + l - 1) + g + 1)
                        dve.wait_ge(XT_ready, 2 * (LEVELS * L + l - 1) + g + 1)
                        V.tensor_tensor(XT[:, s, :], XT[:, s, :], bank(4 + g).rearrange("p (a b) -> p a b", a=4),
                                        ALU.subtract).then_inc(XT_ready, 1)
                    if l == 0:
                        sb_exponent(0)
                sb_mask(SB_H - 1)
                sb_plus(SB_H - 1)
                sb_exponent(SB_H - 1)
                dve.wait_ge(ks_ps, L + 1)
                V.tensor_tensor(RH1, bank(2).rearrange("p (a b) -> p a b", a=4), bcl(scoef, P), ALU.mult)\
                    .then_inc(rhs1_ready, 1)
                dve.wait_ge(rhs1_ready, 2 * L + 1)
                V.tensor_tensor(RH1, RH1, bv[:, 4:8, :], ALU.add).then_inc(rhs1_ready, 1)
                for t in range(TT):
                    dve.wait_ge(sb_sq, 2 * L + t + 1)
                    V.tensor_reduce(sss[:, 8 * t:8 * t + 8], v3((sbz, sbp)[t], SB_H, 0, 512), AX_X, ALU.add)\
                        .then_inc(sb_ss, 1)
                for t in range(TT):
                    dve.wait_ge(sb_rstd, 2 * L + t + 1)
                    dve.wait_ge(sbo_ps, 2 * (L + 1))
                    V.tensor_tensor(v3(h_sb, SB_H, t * D + DN_W, DN_W), bank(6 + t).rearrange("p (a b) -> p a b", a=SB_H),
                                    bcl(srs[:, 8 * t:8 * t + 8], SB_D), ALU.mult).then_inc(mixed_sb, 1)
                dve.wait_ge(mixT_ps, 4 * L + 1)
                col = CONV_ROWS + R_SB + L
                V.tensor_scalar(mixT[:, 4:6, :], bank(4).rearrange("p (a b) -> p a b", a=2), prm[:, col:col + 1], None,
                                ALU.mult).then_inc(mixT_dve, 1)
                dve.wait_ge(dno_ps, L + 1)
                c5 = 5 * L
                o0, o1 = v3(LT_sb, DN_H, 0, DN_W), v3(LT_sb, DN_H, DN_W, DN_W)
                V.tensor_tensor(o0, bank(1).rearrange("p (a b) -> p a b", a=4), bcl(coefq[:, 0:4], P), ALU.mult)\
                    .then_inc(dn_out, 1)
                V.tensor_tensor(o1, bank(3).rearrange("p (a b) -> p a b", a=4), bcl(eg[:, 4:8], P), ALU.mult)\
                    .then_inc(dn_out, 1)
                dve.wait_ge(dn_out, c5 + 2)
                V.tensor_tensor(o1, o1, bank(2).rearrange("p (a b) -> p a b", a=4), ALU.add).then_inc(dn_out, 1)
                dve.wait_ge(dn_out, c5 + 3)
                V.tensor_tensor(o1, o1, bcl(coefq[:, 4:8], P), ALU.mult).then_inc(dn_out, 1)
                dve.wait_ge(dn_out, c5 + 4)
                V.tensor_tensor(AT_sb[:, :], LT_sb[:, :], LT_sb[:, :], ALU.mult).then_inc(dn_out, 1)
                dve.wait_ge(dn_out, c5 + 5)
                V.tensor_reduce(dss, v3(AT_sb, NPR), AX_X, ALU.add).then_inc(dn_rstd_in, 1)
                dve.wait_ge(dn_rstd, 2 * (L + 1))
                for t in range(TT):
                    V.tensor_tensor(v3(LT_sb, DN_H, t * DN_W, DN_W), v3(LT_sb, DN_H, t * DN_W, DN_W),
                                    bcl(drs[:, 4 * t:4 * t + 4], P), ALU.mult).then_inc(dn_rstd_in, 1)
                    dve.wait_ge(dn_rstd_in, 3 * L + t + 2)
                    V.tensor_tensor(hv[:, t, 0:DN_W], hv[:, t, 0:DN_W], LT_sb[:, t * DN_W:(t + 1) * DN_W],
                                    ALU.mult).then_inc(mixed_dn, 1)
                dve.wait_ge(mixT_ps, 4 * L + 3)
                col = CONV_ROWS + R_DN + L
                V.tensor_scalar(mixT[:, 0:2, :], bank(0).rearrange("p (a b) -> p a b", a=2), prm[:, col:col + 1], None,
                                ALU.mult).then_inc(mixT_dve, 1)

                def through(eng, t):
                    eng.wait_ge(*((out_t0, L + 1) if t == 0 else (ring_used, FIRST_MIX[L] + N_MIX)))
                residual(2 * L, through, bank_half, wpost, (wpost_landed, 16 * (L + 1)))

            def dense_ffn():
                normalise(1)
                hT_dve_tiles(1, R_FFN)
                for mt in range(D_FF // P):
                    dve.wait_ge(sg_ready, mt + 1)
                    if mt >= 4:
                        if mt % 2:
                            dve.wait_ge(ring_used, FIRST_FFN + (mt - 4) // 2 + 1)
                        else:
                            dve.wait_ge(down_done, (mt - 4) // 2 + 1)
                    V.tensor_tensor(ffn_hid[:, mt % 4, :], ffn_sg[:, mt % 4, :], bank(mt % 4)[:, T:2 * T], ALU.mult)\
                        .then_inc(hid_ready, 1)
                residual(1, lambda eng, t: eng.wait_ge(ring_used, FIRST_FFN + FFN_CH), bank_half, wpost_ffn,
                         (wpostf_landed, 16))

            mixer(0)
            dense_ffn()
            mixer(1)
            normalise(3)
            hT_dve_tiles(3, R_FFN + KD)

            n = [0]

            def step(ins):
                n[0] += 1
                ins.then_inc(route_step, 1)
                dve.wait_ge(route_step, n[0])

            def tv(ap):
                return ap.rearrange("p (t e) -> p t e", t=TT)

            def first_max(src, best, chosen):
                step(V.tensor_reduce(best, tv(src), AX_X, ALU.max))
                step(V.tensor_tensor(tv(cand), tv(src), bcl(best, N_EXP), ALU.is_equal))
                step(V.tensor_tensor(tv(cand), tv(cand), bcm(w8, TT), ALU.mult))
                step(V.tensor_reduce(mx, tv(cand), AX_X, ALU.max))
                step(V.tensor_tensor(tv(chosen), tv(cand), bcl(mx, N_EXP), ALU.is_equal))

            dve.wait_ge(router_ps, 1)
            V.tensor_copy(lg, bank(4)[:, 0:16]).then_inc(moe_zero, 1)
            V.memset(moe_y[:, :], 0.0).then_inc(moe_zero, 1)
            dve.wait_ge(moe_zero, 2)
            step(V.tensor_reduce(m1, tv(lg), AX_X, ALU.max))
            first_max(lg, m1, sel1)
            step(V.scalar_tensor_tensor(lg2, sel1, -3.0e38, lg, ALU.mult, ALU.add))
            step(V.tensor_reduce(m2, tv(lg2), AX_X, ALU.max))
            step(V.tensor_tensor(gd, m2, m1, ALU.subtract))
            step(V.tensor_copy(mx, m2))
            assert n[0] == 10
            first_max(lg2, m2, sel2)
            V.tensor_tensor(sel, sel1, sel2, ALU.add).then_inc(sel_ready, 1)
            dve.wait_ge(sel_ready, 1)
            dve.wait_ge(route_exp, 1)
            step(V.tensor_scalar(g1, ge, 1.0, None, ALU.add))
            step(V.reciprocal(g1, g1))
            step(V.tensor_tensor(g2, g1, ge, ALU.mult))
            step(V.tensor_tensor(tv(sel1), tv(sel1), bcl(g1, N_EXP), ALU.mult))
            step(V.tensor_tensor(tv(sel2), tv(sel2), bcl(g2, N_EXP), ALU.mult))
            step(V.tensor_tensor(gate, sel1, sel2, ALU.add))
            dve.wait_ge(rank_ps, 1)
            step(V.tensor_reduce(cmax, bank(5)[:, 16:24], AX_X, ALU.max))
            step(V.scalar_tensor_tensor(rank, bank(5)[:, 0:16], 1000.0, sel, ALU.add, ALU.mult))
            step(V.tensor_scalar(rank, rank, -1000.0, None, ALU.add))
            step(V.tensor_scalar(cgt, cmax, float(ROUND_LIMITS[0]), None, ALU.is_gt))
            step(V.tensor_scalar(ctwo, cmax, float(ROUND_LIMITS[1]), 1.0, ALU.is_gt, ALU.add))
            V.tensor_tensor(rounds_i[:, :], cgt, ctwo, ALU.add).then_inc(rounds_ready, 1)
            dve.wait_ge(rounds_ready, 1)
            rounds = dve.value_load(rounds_i[0:1, 0:1], min_val=1, max_val=3)
            wffn = prm[:, CONV_ROWS + R_FFN + KD:CONV_ROWS + R_FFN + 2 * KD]

            with dve.Fori(0, rounds) as r:
                with dve.Fori(0, N_EXP // 2) as pair:
                    it = r * (N_EXP // 2) + pair

                    def choose(j):
                        e = pair * 2 + j
                        cr, cg = cur_rank[:, j * TT:(j + 1) * TT], cur_gate[:, j * TT:(j + 1) * TT]
                        V.tensor_copy(cr, tv(rank)[:, :, bass.ds(e, 1)].rearrange("p t e -> p (t e)"))\
                            .then_inc(cur_ready, 1)
                        V.tensor_copy(cg, tv(gate)[:, :, bass.ds(e, 1)].rearrange("p t e -> p (t e)"))\
                            .then_inc(cur_ready, 1)
                        dve.wait_ge(cur_ready, it * 4 + 2 * (j + 1))
                        for t in range(TT):
                            V.tensor_scalar(onehot[j][:, t, :], iota, cr[:, t:t + 1], None, ALU.is_equal)\
                                .then_inc(onehot_ready, 1)

                    def gathered(j):
                        for b in range(2):
                            dve.wait_ge(gather_ps, it * 4 + (2 * j + b + 1))
                            V.tensor_tensor(xgT[:, 4 * b:4 * b + 4, :],
                                            bank(4 + b)[:, 0:4 * SLOTS].rearrange("p (a b) -> p a b", a=4),
                                            bcl(wffn[:, 4 * b:4 * b + 4], SLOTS), ALU.mult).then_inc(xg_ready, 1)

                    def y_copy(j):
                        dve.wait_ge(y_ps, it * 4 + 2 * (j + 1))
                        V.tensor_copy(y_tok[:, 512:D], bank(5)[0:SLOTS, :]).then_inc(y_dve, 1)

                    def accumulate(j):
                        for t in range(TT):
                            dve.wait_ge(scatter_ps, it * 4 + (2 * j + t + 1))
                            V.scalar_tensor_tensor(moe_yv[:, t, :], bank((6, 4)[t], 2),
                                                   cur_gate[:, j * TT + t:j * TT + t + 1], moe_yv[:, t, :],
                                                   ALU.mult, ALU.add).then_inc(moe_acc, 1)
                        dve.wait_ge(moe_acc, it * 4 + 2 * (j + 1))

                    for j in range(2):
                        choose(j)
                        gathered(j)
                        for c in range(MOE_CH):
                            dve.wait_ge(msg_ready, it * (2 * MOE_CH) + (j * MOE_CH + c + 1))
                            if c >= 2:
                                dve.wait_ge(ring_used, it * (2 * MOE_CH) + (FIRST_MOE + j * MOE_CH + c - 1))
                            V.tensor_tensor(moe_hid[c % 2], moe_sg[c % 2],
                                            bank(c % 2)[:, 2 * SLOTS:4 * SLOTS].rearrange("p (a b) -> p a b", a=2),
                                            ALU.mult).then_inc(mhid_ready, 1)
                            if j == 1 and c == 0:
                                y_copy(0)
                            if j == 1 and c == 1:
                                accumulate(0)
                    y_copy(1)
                    accumulate(1)
                V.tensor_scalar(rank, rank, -float(SLOTS), None, ALU.add).then_inc(route_step, 1)
                dve.wait_ge(route_step, r + (n[0] + 1))
            residual(3, lambda eng, t: None, lambda t, hf: moe_yv[:, t, half(hf)], wpost_ffn, (wpostf_landed, 32))

        @block.gpsimd
        def _(pool):
            G = nc.gpsimd
            pool.dma_start(headp[:, 0:8], dn_a_log.rearrange("l h -> (l h)").partition_broadcast(P))\
                .then_inc(heads_landed, 16)
            pool.dma_start(headp[:, 8:16], dn_dt_bias.rearrange("l h -> (l h)").partition_broadcast(P))\
                .then_inc(heads_landed, 16)
            pool.dma_start(v3(routw, KD), router_w[0].rearrange("(k p) e -> p k e", p=P)).then_inc(router_landed, 16)
            pool.dma_start(wpost[:, :], norm_mix_post[0].partition_broadcast(P)).then_inc(wpost_landed, 16)
            G.memset(mhalf, -0.5).then_inc(half_ready, 1)
            pool.wait_ge(half_ready, 1)

            def rsqrt(dst, src, scale, mid, done, n_mid):
                G.tensor_scalar(src, src, scale, EPS, ALU.mult, ALU.add).then_inc(mid, 1)
                pool.wait_ge(mid, n_mid)
                G.tensor_tensor(dst, src, mhalf[:, 0:src.shape[1]], ALU.pow).then_inc(done, 1)

            def row_rstd(u, parts, mid, done):
                for t in range(TT):
                    pool.wait_ge(parts, 2 * (TT * u + t + 1))
                    G.tensor_tensor(ssum[:, t:t + 1], ssx[:, 2 * t:2 * t + 1], ssx[:, 2 * t + 1:2 * t + 2], ALU.add)\
                        .then_inc(mid, 1)
                    pool.wait_ge(mid, 2 * (TT * u + t) + 1)
                    rsqrt(rsx[:, t:t + 1], ssum[:, t:t + 1], 1.0 / D, mid, done, 2 * (TT * u + t) + 2)

            def pre_rstd(u):
                row_rstd(u, ss_ready, rstd_mean, rstd_ready)

            def post_norm_rstd(u):
                row_rstd(u, post_ss, post_mean, post_rstd)

            def mixer(L):
                pre_rstd(2 * L)
                pool.wait_ge(gcum_ready, L + 1)
                G.tensor_tensor(diag_g, bcm(ident, NPR), bcl(gsum[:, 0:8], P), ALU.mult).then_inc(diag_ready, 1)
                pool.wait_ge(decay_exp, L + 1)
                G.tensor_tensor(DR, DR, bcm(uinc, NPR), ALU.mult).then_inc(decay_ready, 1)
                for m in range(8):
                    pool.wait_ge(conv_silu, CONV_T * L + m + 1)
                    src = qk[:, m, 1, :] if m < 4 else qk[:, m - 4, 0, :]
                    if m == 0:
                        pool.wait_ge(params_ps, 1)
                    G.tensor_tensor(squares[:, m, :], src, src, ALU.mult).then_inc(qk_squares, 1)
                pool.wait_ge(norms_sum, L + 1)
                G.tensor_tensor(rn, nsum, mhalf, ALU.pow).then_inc(norms_ready, 1)
                pool.wait_ge(gates_ready, 5 * (L + 1))
                G.tensor_tensor(diag_b, bcm(ident, NPR), bcl(br, P), ALU.mult).then_inc(diag_ready, 1)
                pool.wait_ge(decay_ready, 2 * L + 1)
                pool.wait_ge(norms_ready, L + 1)
                G.tensor_tensor(DR, DR, bcl(rk, P), ALU.mult).then_inc(decay_ready, 1)

                def blocks(l, g):
                    s = slice(4 * g, 4 * g + 4)
                    pool.wait_ge(LT_ready, 2 * L + g + 1)
                    if l:
                        pool.wait_ge(M1_ps, 2 * (LEVELS * L + l - 1) + g + 1)
                        if l == 1:
                            pool.wait_ge(XT_ready, 2 * LEVELS * L + g + 1)
                    G.tensor_tensor(BT[:, s, :], LT[:, s, :], bcm(cst[:, C_LVL + l * P:C_LVL + (l + 1) * P], 4),
                                    ALU.mult).then_inc(BT_ready, 1)

                def sb_keep_mask(h):
                    pool.wait_ge(sb_softplus, SB_H * L + h + 1)
                    G.tensor_tensor(sp[:, h % 2, :], sp[:, h % 2, :], sbmask, ALU.mult).then_inc(sb_keep, 1)

                def sb_weight_mask(h):
                    pool.wait_ge(sb_weight, SB_H * L + h + 1)
                    G.tensor_tensor(wT(h), wT(h), sbmask, ALU.mult).then_inc(sb_wmask, 1)

                blocks(0, 0)
                blocks(0, 1)
                for l in range(LEVELS):
                    if l and l + 1 < LEVELS:
                        blocks(l + 1, 0)
                        blocks(l + 1, 1)
                    sb_keep_mask(l)
                    if l == 0:
                        blocks(1, 0)
                        blocks(1, 1)
                    sb_weight_mask(l)
                sb_keep_mask(SB_H - 1)
                sb_weight_mask(SB_H - 1)
                for t in range(TT):
                    pool.wait_ge(sb_ss, 2 * L + t + 1)
                    rsqrt(srs[:, 8 * t:8 * t + 8], sss[:, 8 * t:8 * t + 8], 1.0 / SB_D, sb_rstd_in, sb_rstd,
                          2 * L + t + 1)
                pool.wait_ge(dn_rstd_in, 3 * L + 1)
                G.tensor_scalar(dss, dss, 1.0 / DN_D, EPS, ALU.mult, ALU.add).then_inc(dn_rstd, 1)
                pool.wait_ge(dn_rstd, 2 * L + 1)
                G.tensor_tensor(drs, dss, mhalf[:, 0:8], ALU.pow).then_inc(dn_rstd, 1)
                pool.wait_ge(sbz_ps, SB_H * (L + 1))
                pool.dma_start(wpost_ffn, norm_ffn_post[L].partition_broadcast(P)).then_inc(wpostf_landed, 16)
                post_norm_rstd(2 * L)

            mixer(0)
            pool.wait_ge(x_ready, 2 * TT)
            pool.dma_start(wpost[:, :], norm_mix_post[1].partition_broadcast(P)).then_inc(wpost_landed, 16)
            pre_rstd(1)
            post_norm_rstd(1)
            mixer(1)
            pre_rstd(3)
            post_norm_rstd(3)


_INS = ["x", "norm_mix_pre", "norm_mix_post", "norm_ffn_pre", "norm_ffn_post", "w_in", "conv_w", "dn_a_log",
        "dn_dt_bias", "dn_norm_w", "sb_norm_w", "w_out", "ffn_w_gate", "ffn_w_up", "ffn_w_down", "router_w",
        "moe_w_gate", "moe_w_up", "moe_w_down"]


def constants():
    c = np.zeros((P, C_ALL), np.float32)
    i, j = np.arange(P)[:, None], np.arange(P)[None, :]
    c[:, C_ID:C_ID + P] = i == j
    c[:, C_UINC:C_UINC + P] = i <= j
    c[:, C_TRI:C_TRI + P] = i >= j
    c[:, C_SB:C_SB + P] = i < j
    c[:, C_SB + P:C_SB + 2 * P] = 1.0
    c[:, C_SB + 2 * P:C_SB + 3 * P] = i < j
    for l in range(LEVELS):
        b = 1 << l
        c[:, C_LVL + l * P:C_LVL + (l + 1) * P] = (i // (2 * b) == j // (2 * b)) & (i % (2 * b) < b) & (j % (2 * b) >= b)
    c[:, C_IOTA:C_IOTA + SLOTS] = np.arange(SLOTS)
    c[:, C_W8:C_W8 + N_EXP] = N_EXP - np.arange(N_EXP)
    return c


def kernel(**inputs):
    import concourse.bacc as _bacc
    from concourse.bass_utils import run_bass_kernel_spmd as _run

    nc = _bacc.Bacc("TRN2", target_bir_lowering=False, num_devices=1)
    arrays, args = {}, []
    for name in _INS:
        a = np.ascontiguousarray(inputs[name])
        arrays[f"in_{name}"] = a
        args.append(nc.dram_tensor(f"in_{name}", a.shape, mybir.dt.from_np(a.dtype), kind="ExternalInput").ap())
    arrays["in_consts"] = constants()
    consts = nc.dram_tensor("in_consts", (P, C_ALL), F32, kind="ExternalInput").ap()
    out = nc.dram_tensor("out_x", (1, T, D), F32, kind="ExternalOutput").ap()
    build(nc, args[0], consts, *args[1:], out)
    r = _run(nc, [arrays], core_ids=[0])
    return r.results[0]["out_x"]
```

```python
from contextlib import ExitStack

import numpy as np

import concourse.bass as bass
from concourse import mybir

F32 = mybir.dt.float32
BF16 = mybir.dt.bfloat16
I32 = mybir.dt.int32
ALU = mybir.AluOpType
ACT = mybir.ActivationFunctionType
AX_X = mybir.AxisListType.X

P = 128
D = 1024
KD = D // P
T = 256
TT = T // P
DEPTH = 2
DN_H, DN_D = 4, 128
DN_W = DN_H * DN_D
SB_H, SB_D = 8, 64
NPR = TT * DN_H
D_FF = 2816
N_EXP = 8
PAIRS = N_EXP // 2
FF_E = 3584
EPS = 1e-6
SLOTS = 96
ROUND_LIMITS = (SLOTS, 2 * SLOTS)

FC = 256
SLOT = 2 * KD * FC + (FC // P) * D
NSLOT = 4
PARTS = 3
LANDED = 16 * PARTS
FFN_CH = D_FF // FC
MOE_CH = FF_E // FC
C_BA = 4 * DN_W
C_Q = C_BA + 2 * DN_H
IN_RANGES = (((C_BA, C_Q), (0, 640)), ((640, 1408),), ((1408, 2048),),
             ((C_Q, C_Q + 512),), ((C_Q + 512, C_Q + 1024),), ((C_Q + 1024, C_Q + 1536),))
IN_WIDTH = tuple(sum(b - a for a, b in r) for r in IN_RANGES)
N_IN = len(IN_RANGES)
N_MIX = N_IN + 2
FIRST_FFN = N_MIX
FIRST_MIX = (0, N_MIX + FFN_CH)
FIRST_MOE = 2 * N_MIX + FFN_CH
N_STEPS = 25
ROUTE_GD = 15
LEVELS = 7

C_ID = 0
C_UINC = C_ID + P
C_TRI = C_UINC + P
C_SB = C_TRI + P
C_LVL = C_SB + 3 * P
C_IOTA = C_LVL + LEVELS * P
C_W8 = C_IOTA + SLOTS
C_ALL = C_W8 + N_EXP

CONV_K = 4
CONV_T = 3 * DN_W // P
CONV_ROWS = DEPTH * CONV_K * CONV_T
R_MIX, R_FFN, R_DN, R_SB = 0, DEPTH * KD, 2 * DEPTH * KD, 2 * DEPTH * KD + DEPTH
NORM_ROWS = 2 * DEPTH * KD + 2 * DEPTH


def proj_steps():
    s = [("ba", 0, 0, 0)]
    for m in range(CONV_T):
        s.append(("conv", m, 0, 8 + m * P) if m < 5 else ("conv", m, 1, (m - 5) * P) if m < 11 else ("conv", m, 2, 0))
    s += [("z", 0, 2, P), ("z", 1, 2, P)]
    for i in range(4):
        s += [("sq", i, 3, i * P), ("sk", i, 4, i * P)]
    s += [("sv", 0, 5, 0), ("sv", 1, 5, 0)]
    return s


STEPS = proj_steps()
S_Z, S_SB, S_FILL = 13, 15, 18


def step_bank(n):
    return 4 + n % 4 if n < S_FILL else 7


BANK_PREV = {n: max((m for m in range(n) if step_bank(m) == step_bank(n)), default=None) for n in range(N_STEPS)}
LAST_STEP = {max(n for n, s in enumerate(STEPS) if s[2] == c): c for c in range(N_IN)}


def build(nc, x_in, consts, norm_mix_pre, norm_mix_post, norm_ffn_pre, norm_ffn_post, w_in, conv_w,
          dn_a_log, dn_dt_bias, dn_norm_w, sb_norm_w, w_out, ffn_gate, ffn_up, ffn_down, router_w,
          moe_gate, moe_up, moe_down, out):
    with ExitStack() as ctx:
        def sb(name, cols, dt=F32):
            return ctx.enter_context(nc.sbuf_tensor(name, [P, cols], dt))

        def sem(name):
            return ctx.enter_context(nc.semaphore(name))

        ps = ctx.enter_context(nc.psum_tensor("ps", [P, 8, 512], F32))

        def bank(b, n=1):
            return ps[:, b:b + n, :].rearrange("p b c -> p (b c)")

        ring = sb("ring", NSLOT * SLOT)
        cst = sb("cst", C_ALL)
        prm = sb("prm", CONV_ROWS + NORM_ROWS)
        headp = sb("headp", 2 * DEPTH * DN_H)
        routw = sb("routw", KD * N_EXP)
        x_sb = sb("x_sb", TT * D)
        h_sb = sb("h_sb", TT * D)
        hT_sb = sb("hT_sb", TT * D)
        wT01 = sb("wT01", 2 * 3 * P)
        wT45 = sb("wT45", 2 * 3 * P)
        wpost = sb("wpost", D)
        qk_sb = sb("qk_sb", DN_H * 2 * T)
        bv_sb = sb("bv_sb", NPR * P)
        kend_sb = sb("kend_sb", DN_H * P)
        sbq = sb("sbq", 4 * T)
        sbk = sb("sbk", 4 * T)
        DR_sb = sb("DR_sb", NPR * P)
        LT_sb = sb("LT_sb", NPR * P)
        AT_sb = sb("AT_sb", NPR * P)
        X_sb = sb("X_sb", NPR * P)
        XT_sb = sb("XT_sb", NPR * P)
        BM = sb("BM", 2 * NPR * P)
        Vn_sb = sb("Vn_sb", 2 * DN_H * P)
        SR = sb("SR", 2 * DN_H * P)
        sbz = sb("sbz", 2 * 3 * P)
        sbe = sb("sbe", 3 * P)
        sbp = sb("sbp", 2 * 3 * P)
        small = sb("small", 416)
        rounds_i = sb("rounds_i", 1, I32)

        def v3(t, a, lo=0, n=None):
            n = n or t.shape[1] - lo
            return t[:, lo:lo + n].rearrange("p (a b) -> p a b", a=a)

        ident = cst[:, C_ID:C_ID + P]
        uinc = cst[:, C_UINC:C_UINC + P]
        tri = cst[:, C_TRI:C_TRI + P]
        sbmask = cst[:, C_SB:C_SB + 3 * P]
        ustrict = cst[:, C_SB:C_SB + P]
        ones = cst[:, C_SB + P:C_SB + 2 * P]
        iota = cst[:, C_IOTA:C_IOTA + SLOTS]
        w8 = cst[:, C_W8:C_W8 + N_EXP]
        xv = v3(x_sb, TT)
        hv = v3(h_sb, TT)
        hT = v3(hT_sb, KD)
        mixT = hT

        def wT(h):
            return (wT01, DR_sb, wT45, wpost)[h // 2][:, h % 2 * 3 * P:(h % 2 + 1) * 3 * P]

        qk = qk_sb[:, :].rearrange("p (h k t) -> p h k t", h=DN_H, k=2)
        vT = v3(X_sb, DN_H)
        bv = v3(bv_sb, NPR)
        kend = v3(kend_sb, DN_H)
        sq_v, sk_v = v3(sbq, 4), v3(sbk, 4)
        DR, LT, AT, X, XT = (v3(t, NPR) for t in (DR_sb, LT_sb, AT_sb, X_sb, XT_sb))
        DF = XT
        diag_g, diag_b = LT, AT
        BT = v3(BM, NPR, 0, NPR * P)
        M1 = v3(BM, NPR, NPR * P, NPR * P)
        squares = v3(BM, 8)
        Vn = v3(Vn_sb, NPR)
        S = v3(SR, DN_H, 0, DN_H * P)
        RH1 = v3(SR, DN_H, DN_H * P, DN_H * P)
        zm = v3(sbz, 2)
        sp = v3(sbp, 2)
        dn_o = v3(LT_sb, TT)
        dn_sq = v3(AT_sb, TT)
        post_tmp = (DR_sb, LT_sb)
        act_junk = (XT_sb[:, :], X_sb[:, :])
        rows = BM
        wpost_ffn = sbq[:, :]

        at = [0]

        def cols(n):
            at[0] += n
            return small[:, at[0] - n:at[0]]

        ssx, rsx, ssum = cols(2 * TT), cols(TT), cols(TT)
        mhalf = cols(16)
        negA = cols(2 * DN_H)
        nsum, rn = cols(16), cols(16)
        ba = cols(16)
        aa, sabs, sln, spl, g_log = cols(8), cols(8), cols(8), cols(8), cols(8)
        eb, beta = cols(8), cols(8)
        gsum = cols(16)
        gdiff, egl, kcoef = cols(4), cols(4), cols(4)
        eg, scoef, coefq, br = cols(8), cols(4), cols(8), cols(8)
        dss, drs = cols(8), cols(8)
        sss, srs = cols(16), cols(16)
        lg, sel1, sel2, lg2, cand, sel, gate, rank = (cols(16) for _ in range(8))
        m1, m2, mx, ge, gd, g1, g2 = (cols(2) for _ in range(7))
        cmax, cgt, ctwo = cols(1), cols(1), cols(1)
        cur_rank, cur_gate = cols(2 * TT), cols(2 * TT)
        assert at[0] <= 416
        rk, rq = rn[:, 0:8], rn[:, 8:16]

        ffn_hid = v3(LT_sb, 4)
        ffn_sg = v3(AT_sb, 4)
        moe_y = qk_sb
        moe_yv = v3(qk_sb, TT)
        xgT = v3(bv_sb, KD, 0, KD * SLOTS)
        onehot = [v3(AT_sb[:, :].bitcast(BF16), TT, j * TT * SLOTS, TT * SLOTS) for j in range(2)]
        h_part = [v3(b[:, :].bitcast(BF16), TT) for b in (DR_sb, SR, Vn_sb)]
        h_rest = v3(BM, TT)
        ident_bf = sbe[:, 0:P // 2].bitcast(BF16)
        onehotT = [X_sb[0:SLOTS, j * T:(j + 1) * T] for j in range(2)]
        moe_sg = [v3(LT_sb, 2, j * 2 * SLOTS, 2 * SLOTS) for j in range(2)]
        moe_hid = [v3(LT_sb, 2, (2 + j) * 2 * SLOTS, 2 * SLOTS) for j in range(2)]
        y_tok = BM[0:SLOTS, D:2 * D]

        ring_landed = [sem(f"ring_landed{i}") for i in range(NSLOT)]
        ring_used = sem("ring_used")
        x_landed = [sem(f"x_landed{t}") for t in range(TT)]
        consts_landed, rows_landed, heads_landed, router_landed = (
            sem(n) for n in ("consts_landed", "rows_landed", "heads_landed", "router_landed"))
        wpost_landed, wpostf_landed, out_landed = (sem(n) for n in ("wpost_landed", "wpostf_landed", "out_landed"))
        params_ps, params_ready, half_ready, expA, negA_ready = (
            sem(n) for n in ("params_ps", "params_ready", "half_ready", "expA", "negA_ready"))
        ss_ready, rstd_mean, rstd_ready, h_dve, h_act = (
            sem(n) for n in ("ss_ready", "rstd_mean", "rstd_ready", "h_dve", "h_act"))
        hT_ps, hT_dve, hT_act = (sem(n) for n in ("hT_ps", "hT_dve", "hT_act"))
        proj_done, conv_base, conv_taps, conv_silu, qk_squares, z_gate, ba_copied, sb_copied = (
            sem(n) for n in ("proj_done", "conv_base", "conv_taps", "conv_silu", "qk_squares", "z_gate",
                             "ba_copied", "sb_copied"))
        norms_ps, norms_sum, norms_ready, v_ps, kT_ps = (
            sem(n) for n in ("norms_ps", "norms_sum", "norms_ready", "v_ps", "kT_ps"))
        gate_in, gate_exp, gates_ready, gcum_ps, gcum_ready, gexp_ready, coef_ready, bv_ready, kend_ready = (
            sem(n) for n in ("gate_in", "gate_exp", "gates_ready", "gcum_ps", "gcum_ready", "gexp_ready",
                             "coef_ready", "bv_ready", "kend_ready"))
        diag_ready, bc_ps, decay_in, decay_exp, decay_ready, betadecay_ready, kk_ps, LT_ready, AT_ready = (
            sem(n) for n in ("diag_ready", "bc_ps", "decay_in", "decay_exp", "decay_ready",
                             "betadecay_ready", "kk_ps", "LT_ready", "AT_ready"))
        BT_ready, M1_ps, M1_ready, XM_ps, XTM_ps, X_ready, XT_ready = (
            sem(n) for n in ("BT_ready", "M1_ps", "M1_ready", "XM_ps", "XTM_ps", "X_ready", "XT_ready"))
        vnew_ps, vnew_ready, state_ps, state_ready, ks_ps, rhs1_ready, dno_ps = (
            sem(n) for n in ("vnew_ps", "vnew_ready", "state_ps", "state_ready", "ks_ps", "rhs1_ready", "dno_ps"))
        dn_out, dn_rstd_in, dn_rstd, mixed_dn = (sem(n) for n in ("dn_out", "dn_rstd_in", "dn_rstd", "mixed_dn"))
        sbz_ps, sbz_ready, sb_soft, sb_softplus, sb_keep, sbc_ps, sb_expo, sb_weight, sb_wmask, sbo_ps = (
            sem(n) for n in ("sbz_ps", "sbz_ready", "sb_soft", "sb_softplus", "sb_keep", "sbc_ps", "sb_expo",
                             "sb_weight", "sb_wmask", "sbo_ps"))
        sb_sq, sb_ss, sb_rstd_in, sb_rstd, mixed_sb = (
            sem(n) for n in ("sb_sq", "sb_ss", "sb_rstd_in", "sb_rstd", "mixed_sb"))
        mixT_ps, mixT_dve, mixT_act = (sem(n) for n in ("mixT_ps", "mixT_dve", "mixT_act"))
        out_t0, ffn_t0, ident_landed = (sem(n) for n in ("out_t0", "ffn_t0", "ident_landed"))
        ba_landed, q01_landed = (sem(n) for n in ("ba_landed", "q01_landed"))
        part_ready, rest_ready, ident_ready = (sem(n) for n in ("part_ready", "rest_ready", "ident_ready"))
        post_ss, post_mean, post_rstd, post_w, x_ready = (
            sem(n) for n in ("post_ss", "post_mean", "post_rstd", "post_w", "x_ready"))
        gu_ps, sg_ready, hid_ready, down_done = (sem(n) for n in ("gu_ps", "sg_ready", "hid_ready", "down_done"))
        router_ps, route_step, route_exp, sel_ready, rank_ps, rounds_ready, moe_zero = (
            sem(n) for n in ("router_ps", "route_step", "route_exp", "sel_ready", "rank_ps", "rounds_ready",
                             "moe_zero"))
        cur_ready, onehot_ready, gather_ps, xg_ready, ohT_ps, ohT_ready = (
            sem(n) for n in ("cur_ready", "onehot_ready", "gather_ps", "xg_ready", "ohT_ps", "ohT_ready"))
        mgu_ps, msg_ready, mhid_ready, y_act, y_dve, scatter_ps = (
            sem(n) for n in ("mgu_ps", "msg_ready", "mhid_ready", "y_act", "y_dve", "scatter_ps"))
        moe_acc = [sem(f"moe_acc{t}") for t in range(TT)]

        def bcl(ap, n):
            return ap.unsqueeze(2).broadcast_to([ap.shape[0], ap.shape[1], n])

        def bcm(ap, n):
            return ap.unsqueeze(1).broadcast_to([ap.shape[0], n, ap.shape[1]])

        def slot_of(n):
            return ring[:, (n % NSLOT) * SLOT:(n % NSLOT + 1) * SLOT]

        def chunk_landed(eng, n, extra=0):
            eng.wait_ge(ring_landed[n % NSLOT], extra + LANDED * (n // NSLOT + 1))

        def gate_up_down(n):
            s = slot_of(n)
            g = s[:, 0:KD * FC].rearrange("p (k f) -> p k f", k=KD)
            u = s[:, KD * FC:2 * KD * FC].rearrange("p (k f) -> p k f", k=KD)
            d = s[:, 2 * KD * FC:SLOT].rearrange("p (i d) -> p i d", i=FC // P)
            return g, u, d

        def in_cols(n, width):
            return slot_of(n)[:, 0:KD * width].rearrange("p (k c) -> p k c", k=KD)

        def step_sem(L, n):
            if n in LAST_STEP:
                return ring_used, FIRST_MIX[L] + LAST_STEP[n] + 1
            before = sum(1 for m in range(n) if m not in LAST_STEP)
            return proj_done, (N_STEPS - N_IN) * L + before + 1

        def evac_sem(L, n):
            kind, i = STEPS[n][:2]
            if kind == "ba":
                return ba_copied, L + 1
            if kind == "conv":
                return conv_taps, 3 * (CONV_T * L + i + 1)
            if kind == "z":
                return z_gate, TT * L + i + 1
            return sb_copied, (N_STEPS - S_SB) * L + n - S_SB + 1

        def half(h):
            return slice(h * 512, (h + 1) * 512)

        def ffn_through(eng, t):
            eng.wait_ge(*((ring_used, FIRST_FFN + FFN_CH) if t else (ffn_t0, 1)))

        block = ctx.enter_context(nc.Block())

        @block.sync
        def _(sp_):
            for t in range(TT):
                sp_.dma_start(xv[:, t, :], x_in[0, t * P:(t + 1) * P, :]).then_inc(x_landed[t], 16)

            def free_slot(n):
                if n >= NSLOT:
                    sp_.wait_ge(ring_used, n - NSLOT + 1)

            def load_rest_of_parameters():
                sp_.dma_start(rows[0:CONV_ROWS, 0:P], conv_w.rearrange("l k (t p) -> (l k t) p", p=P))\
                   .then_inc(rows_landed, 16)
                sp_.dma_start(rows[R_DN:R_DN + 2, P:2 * P], dn_norm_w).then_inc(rows_landed, 16)
                sp_.dma_start(rows[R_SB:R_SB + 2, P:P + SB_D], sb_norm_w).then_inc(rows_landed, 16)
                sp_.dma_start(rows[R_SB:R_SB + 2, P + SB_D:2 * P], sb_norm_w).then_inc(rows_landed, 16)
                sp_.dma_start(cst[:, P:C_ALL], consts[:, P:C_ALL]).then_inc(consts_landed, 16)

            def load_rows(n, ranges, src):
                free_slot(n)
                dst = in_cols(n, sum(b - a for a, b in ranges))
                src = src.rearrange("(k p) c -> p k c", p=P)
                at = 0
                if n == 0:
                    (a, b), (c, d) = ranges
                    sp_.dma_start(dst[:, :, 0:b - a], src[:, :, a:b]).then_inc(ba_landed, 16)
                    sp_.dma_start(dst[:, :, 8:8 + 2 * P], src[:, :, c:c + 2 * P]).then_inc(q01_landed, 16)
                    load_rest_of_parameters()
                    for lo, hi in ((0, 3), (3, 6), (6, KD)):
                        sp_.dma_start(dst[:, lo:hi, 8 + 2 * P:], src[:, lo:hi, c + 2 * P:d])\
                           .then_inc(ring_landed[0], 16)
                    return
                for i, (a, b) in enumerate(ranges):
                    cuts = (0, KD) if i < len(ranges) - 1 else (0, 4, KD) if len(ranges) > 1 else (0, 3, 6, KD)
                    for lo, hi in zip(cuts, cuts[1:]):
                        sp_.dma_start(dst[:, lo:hi, at:at + b - a], src[:, lo:hi, a:b])\
                           .then_inc(ring_landed[n % NSLOT], 16)
                    at += b - a

            def load_mixer(L):
                for c in range(N_IN):
                    load_rows(FIRST_MIX[L] + c, IN_RANGES[c], w_in[L])
                for h in range(2):
                    load_rows(FIRST_MIX[L] + N_IN + h, ((h * 512, (h + 1) * 512),), w_out[L])

            def load_ffn(n, wg, wu, wd):
                g, u, d = gate_up_down(n)
                s = ring_landed[n % NSLOT]
                sp_.dma_start(g, wg.rearrange("(k p) f -> p k f", p=P)).then_inc(s, 16)
                sp_.dma_start(u, wu.rearrange("(k p) f -> p k f", p=P)).then_inc(s, 16)
                sp_.dma_start(d, wd.rearrange("(i p) d -> p i d", p=P)).then_inc(s, 16)

            load_mixer(0)
            for c in range(FFN_CH):
                free_slot(FIRST_FFN + c)
                f = slice(c * FC, (c + 1) * FC)
                load_ffn(FIRST_FFN + c, ffn_gate[0][:, f], ffn_up[0][:, f], ffn_down[0][f, :])
            load_mixer(1)

            def moe_pair(pair, it):
                for j in range(2):
                    for c in range(MOE_CH):
                        n = FIRST_MOE + j * MOE_CH + c
                        sp_.wait_ge(ring_used, it * (2 * MOE_CH) + (n - NSLOT + 1))
                        f = slice(c * FC, (c + 1) * FC)
                        e = pair * 2 + j
                        load_ffn(n, moe_gate[0, e][:, f], moe_up[0, e][:, f], moe_down[0, e][f, :])

            with sp_.Fori(0, PAIRS) as pair:
                moe_pair(pair, pair)
            sp_.wait_ge(rounds_ready, 1)
            rounds = sp_.value_load(rounds_i[0:1, 0:1], min_val=1, max_val=3)
            with sp_.If(rounds > 1):
                with sp_.Fori(1, rounds) as r:
                    with sp_.Fori(0, PAIRS) as pair:
                        moe_pair(pair, r * PAIRS + pair)
            for t in range(TT):
                sp_.wait_ge(x_ready, 2 * (3 * TT + t + 1))
                sp_.dma_start(out[0].rearrange("(t p) d -> p t d", p=P)[:, t, :], xv[:, t, :]).then_inc(out_landed, 16)
            sp_.wait_ge(out_landed, 32)

        @block.tensor
        def _(pe):
            mm = nc.tensor.matmul

            pe.wait_ge(ident_landed, 16)

            def param_transposes():
                pe.wait_ge(rows_landed, 16 * 6)
                nc.tensor.transpose(bank(7)[:, 0:CONV_ROWS], rows[0:CONV_ROWS, 0:P],
                                    ident[0:CONV_ROWS, 0:CONV_ROWS])
                nc.tensor.transpose(bank(7)[:, CONV_ROWS:CONV_ROWS + NORM_ROWS], rows[0:NORM_ROWS, P:2 * P],
                                    ident[0:NORM_ROWS, 0:NORM_ROWS]).then_inc(params_ps, 1)

            def transpose_h(u, t):
                for k in range(KD):
                    if k % 4 == 0:
                        pe.wait_ge(h_act if k else h_dve, TT * u + t + 1)
                    ins = nc.tensor.transpose(bank(2 * t + k // 4)[:, (k % 4) * P:(k % 4 + 1) * P],
                                              hv[:, t, k * P:(k + 1) * P], ident)
                    if k % 4 == 3:
                        ins.then_inc(hT_ps, 1)

            def hT_wait(u, t, k):
                if k < 4:
                    pe.wait_ge(hT_dve, TT * u + t + 1)
                else:
                    pe.wait_ge(hT_act, 4 * (TT * u + t) + k - 3)

            def project(L, n, tiles=None, ks=range(KD)):
                kind, i, c, col = STEPS[n]
                if BANK_PREV[n] is not None and 0 in ks:
                    pe.wait_ge(*evac_sem(L, BANK_PREV[n]))
                chunk = FIRST_MIX[L] + c
                if L == 0 and n <= 2:
                    pe.wait_ge(q01_landed if n else ba_landed, 16)
                else:
                    chunk_landed(pe, chunk)
                w = in_cols(chunk, IN_WIDTH[c])
                o = bank(step_bank(n))
                if kind == "conv" and tiles is not None:
                    for t in tiles:
                        for k in range(KD):
                            hT_wait(2 * L, t, k)
                            ins = mm(o[:, t * P:(t + 1) * P], w[:, k, col:col + P], hT[:, k, t * P:(t + 1) * P],
                                     start=(k == 0), stop=(k == KD - 1))
                elif kind in ("conv", "sq", "sk"):
                    for k in range(KD):
                        ins = mm(o[:, 0:T], w[:, k, col:col + P], hT[:, k, :], start=(k == 0), stop=(k == KD - 1))
                elif kind == "ba":
                    for t in range(TT) if tiles is None else tiles:
                        for k in range(KD):
                            hT_wait(2 * L, t, k)
                            ins = mm(o[:, t * 8:(t + 1) * 8], hT[:, k, t * P:(t + 1) * P], w[:, k, col:col + 8],
                                     start=(k == 0), stop=(k == KD - 1))
                else:
                    for k in ks:
                        ins = mm(o, hT[:, k, i * P:(i + 1) * P], w[:, k, col:col + 512],
                                 start=(k == 0), stop=(k == KD - 1))
                if (tiles is None or TT - 1 in tiles) and KD - 1 in ks:
                    ins.then_inc(step_sem(L, n)[0], 1)

            def sb_scores(L, h):
                if h:
                    pe.wait_ge(sb_expo, SB_H * L + h)
                else:
                    pe.wait_ge(*evac_sem(L, S_Z + 1))
                pe.wait_ge(*evac_sem(L, S_SB + 1 + 2 * (h // 2)))
                r = (h % 2) * SB_D
                kh, qh = sk_v[r:r + SB_D, h // 2, :], sq_v[r:r + SB_D, h // 2, :]
                o = bank(6)
                mm(o[:, 0:T], kh[:, 0:P], qh[:, 0:T], start=True, stop=True)
                mm(o[:, T:T + P], kh[:, P:T], qh[:, P:T], start=True, stop=True).then_inc(sbz_ps, 1)

            def sb_cumsum(L, h):
                pe.wait_ge(sb_keep, SB_H * L + h + 1)
                o = bank(6)
                mm(o[:, 0:3 * P], tri, sp[:, h % 2, :], start=True, stop=True)
                mm(o[:, P:2 * P], ones, sp[:, h % 2, 2 * P:3 * P], start=False, stop=True,
                   skip_group_check=True).then_inc(sbc_ps, 1)

            def sb_output(L):
                pe.wait_ge(sb_wmask, SB_H * (L + 1))
                pe.wait_ge(sb_expo, SB_H * (L + 1))
                pe.wait_ge(*evac_sem(L, N_STEPS - 1))
                for t in range(TT):
                    for h in range(SB_H):
                        o = bank(6 + t)[:, h * SB_D:(h + 1) * SB_D]
                        v = [hv[:, s, DN_W + h * SB_D:DN_W + (h + 1) * SB_D] for s in range(TT)]
                        ins = mm(o, wT(h)[:, t * P:(t + 1) * P], v[0], start=True, stop=(t == 0))
                        if t == 1:
                            ins = mm(o, wT(h)[:, 2 * P:3 * P], v[1], start=False, stop=True)
                    ins.then_inc(sbo_ps, 1)

            def qk_norms(L):
                pe.wait_ge(qk_squares, 8 * (L + 1))
                for kind in range(2):
                    for t in range(TT):
                        for h in range(DN_H):
                            c = kind * 8 + t * DN_H + h
                            ins = mm(bank(2)[:, c:c + 1], squares[:, (1 - kind) * 4 + h, t * P:(t + 1) * P],
                                     ones[:, 0:1], start=True, stop=True)
                ins.then_inc(norms_ps, 1)

            def k_transposes(L):
                for h in range(DN_H):
                    ins = nc.tensor.transpose(bank(3)[:, h * P:(h + 1) * P], qk[:, h, 0, 0:P], ident)
                ins.then_inc(kT_ps, 1)

            def v_transposes(L):
                pe.wait_ge(conv_silu, CONV_T * (L + 1))
                for t in range(TT):
                    for h in range(DN_H):
                        ins = nc.tensor.transpose(bank(t)[:, h * P:(h + 1) * P], vT[:, h, t * P:(t + 1) * P], ident)
                    ins.then_inc(v_ps, 1)

            def decay_sums(L):
                pe.wait_ge(gates_ready, 5 * L + 4)
                mm(bank(0)[:, 0:8], uinc, g_log, start=True, stop=True)
                mm(bank(0)[:, 8:16], ones, g_log, start=True, stop=True).then_inc(gcum_ps, 1)

            def broadcast(L, n, dg):
                pe.wait_ge(diag_ready, 2 * L + n + 1)
                for b in range(2):
                    ins = mm(bank(2 * n + b), ones, dg[:, 4 * b:4 * b + 4, :], start=True, stop=True)
                ins.then_inc(bc_ps, 1)

            def key_products(L):
                pe.wait_ge(bv_ready, 2 * (L + 1))
                pe.wait_ge(betadecay_ready, 2 * (L + 1))
                for pr in range(NPR):
                    t, h = pr // DN_H, pr % DN_H
                    o = bank(pr // 2)[:, (pr % 2) * T:(pr % 2 + 1) * T]
                    ins = mm(o, qk[:, h, 0, t * P:(t + 1) * P], qk[:, h, :, t * P:(t + 1) * P],
                             start=True, stop=True)
                    if pr % 4 == 3:
                        ins.then_inc(kk_ps, 1)

            def level_product(L, l, g):
                pe.wait_ge(BT_ready, 2 * (LEVELS * L + l) + g + 1)
                if l == 0:
                    pe.wait_ge(AT_ready, 2 * (L + 1))
                    pe.wait_ge(LT_ready, 2 * (L + 1))
                else:
                    pe.wait_ge(X_ready, 2 * (6 * L + l - 1) + g + 1)
                    if l >= 2:
                        pe.wait_ge(M1_ready, 2 * (6 * L + l - 2) + g + 1)
                for pr in range(4 * g, 4 * g + 4):
                    o = bank(g)[:, (pr % 4) * P:(pr % 4 + 1) * P]
                    if l == 0:
                        ins = nc.tensor.transpose(o, BT[:, pr, :], ident)
                    else:
                        ins = mm(o, BT[:, pr, :], X[:, pr, :], start=True, stop=True)
                ins.then_inc(M1_ps, 1)

            def level_update(L, l, g):
                pe.wait_ge(M1_ready, 2 * (6 * L + l - 1) + g + 1)
                pe.wait_ge(XT_ready, 2 * (LEVELS * L + l - 1) + g + 1)
                if l == 1:
                    pe.wait_ge(*evac_sem(L, 17))
                if l < LEVELS - 1:
                    for pr in range(4 * g, 4 * g + 4):
                        ins = mm(bank(2 + g)[:, (pr % 4) * P:(pr % 4 + 1) * P], XT[:, pr, :], M1[:, pr, :],
                                 start=True, stop=True)
                    ins.then_inc(XM_ps, 1)
                for pr in range(4 * g, 4 * g + 4):
                    ins = mm(bank(4 + g)[:, (pr % 4) * P:(pr % 4 + 1) * P], M1[:, pr, :], XT[:, pr, :],
                             start=True, stop=True)
                ins.then_inc(XTM_ps, 1)

            def per_head(b, lhs, rhs, signal):
                for h in range(DN_H):
                    ins = mm(bank(b)[:, h * P:(h + 1) * P], lhs(h), rhs(h), start=True, stop=True)
                if signal is not None:
                    ins.then_inc(signal, 1)

            def out_part(L, ks, t, hf):
                w = in_cols(FIRST_MIX[L] + N_IN + hf, 512)
                for k in ks:
                    ins = mm(bank(4 + 2 * t + hf), mixT[:, k, t * P:(t + 1) * P], w[:, k, :],
                             start=(k == 4), stop=(k == 3))
                return ins

            def mix_transpose(L, ks, t, b):
                for i, k in enumerate(ks):
                    ins = nc.tensor.transpose(bank(b)[:, i * P:(i + 1) * P], hv[:, t, k * P:(k + 1) * P], ident)
                ins.then_inc(mixT_ps, 1)

            def mixer(L):
                if L:
                    project(L, 0, (0,))
                    project(L, 1, (0,))
                    transpose_h(2 * L, 1)
                    project(L, 2, (0,))
                    for n in range(0, 3):
                        project(L, n, (1,))
                else:
                    transpose_h(0, 0)
                    transpose_h(0, 1)
                    param_transposes()
                    for n in range(0, 3):
                        project(L, n)
                    pe.wait_ge(consts_landed, 16)
                decay_sums(L)
                for n in range(3, 5):
                    project(L, n)
                pe.wait_ge(gcum_ready, L + 1)
                broadcast(L, 0, diag_g)
                for n in range(5, 11):
                    project(L, n)
                qk_norms(L)
                k_transposes(L)
                for n in range(11, 14):
                    project(L, n)
                pe.wait_ge(norms_sum, L + 1)
                pe.wait_ge(kend_ready, L + 1)
                broadcast(L, 1, diag_b)
                project(L, 14)
                pe.wait_ge(decay_in, NPR * (L + 1))
                v_transposes(L)
                project(L, 15)
                key_products(L)
                project(L, 16)
                project(L, 17)
                sb_scores(L, 0)
                for l in range(LEVELS):
                    level_product(L, l, 0)
                    level_product(L, l, 1)
                    project(L, S_FILL + l, ks=range(KD) if l < LEVELS - 1 else range(0, 2))
                    sb_cumsum(L, l)
                    if l:
                        level_update(L, l, 0)
                        level_update(L, l, 1)
                    sb_scores(L, l + 1)
                pe.wait_ge(XT_ready, 2 * LEVELS * (L + 1))
                per_head(0, lambda h: XT[:, h, :], lambda h: bv[:, h, :], vnew_ps)
                project(L, N_STEPS - 1, ks=range(2, 5))
                pe.wait_ge(vnew_ready, 2 * L + 1)
                per_head(1, lambda h: kend[:, h, :], lambda h: Vn[:, h, :], state_ps)
                sb_cumsum(L, SB_H - 1)
                project(L, N_STEPS - 1, ks=range(5, KD))
                pe.wait_ge(state_ready, L + 1)
                per_head(2, lambda h: qk[:, h, 0, P:T], lambda h: S[:, h, :], ks_ps)
                per_head(3, lambda h: qk[:, h, 1, P:T], lambda h: S[:, h, :], None)
                per_head(1, lambda h: AT[:, h, :], lambda h: Vn[:, h, :], None)
                pe.wait_ge(rhs1_ready, 2 * (L + 1))
                per_head(0, lambda h: XT[:, 4 + h, :], lambda h: RH1[:, h, :], vnew_ps)
                sb_output(L)
                pe.wait_ge(vnew_ready, 2 * L + 2)
                per_head(2, lambda h: AT[:, 4 + h, :], lambda h: Vn[:, 4 + h, :], dno_ps)
                att, dn = (4, 5, 6, 7), (0, 1, 2, 3)
                pe.wait_ge(mixed_sb, TT * L + 1)
                mix_transpose(L, att, 0, 4)
                chunk_landed(pe, FIRST_MIX[L] + N_IN)
                chunk_landed(pe, FIRST_MIX[L] + N_IN + 1)
                pe.wait_ge(mixT_act, 3 * L + 1)
                out_part(L, att, 0, 0)
                pe.wait_ge(mixed_sb, TT * L + 2)
                mix_transpose(L, att, 1, 6)
                out_part(L, att, 0, 1)
                pe.wait_ge(mixT_act, 3 * L + 2)
                out_part(L, att, 1, 0)
                pe.wait_ge(mixed_dn, TT * L + 1)
                mix_transpose(L, dn, 0, 0)
                out_part(L, att[:2], 1, 1)
                pe.wait_ge(mixed_dn, TT * L + 2)
                mix_transpose(L, dn, 1, 3)
                pe.wait_ge(mixT_dve, L + 1)
                out_part(L, dn, 0, 0)
                out_part(L, dn, 0, 1).then_inc(out_t0, 1)
                out_part(L, att[2:], 1, 1)
                pe.wait_ge(mixT_act, 3 * L + 3)
                out_part(L, dn, 1, 0)
                out_part(L, dn[:2], 1, 1)
                transpose_h(2 * L + 1, 0)
                out_part(L, dn[2:], 1, 1).then_inc(ring_used, 2)

            def dense_ffn():
                n_mt = D_FF // P

                def gate_up(mt, tiles=None, parts=(0, 1)):
                    c, i = FIRST_FFN + mt // 2, mt % 2
                    chunk_landed(pe, c)
                    g, u, _ = gate_up_down(c)
                    if mt >= 4:
                        pe.wait_ge(hid_ready, mt - 3)
                    for which in parts:
                        w = (g, u)[which]
                        for t in (None,) if tiles is None else tiles:
                            lo, hi = (0, T) if t is None else (t * P, (t + 1) * P)
                            for k in range(KD):
                                if t is not None:
                                    if mt < 2 and which == 0 and k == 0:
                                        hT_wait(1, t, KD - 1 if mt else 0)
                                    hT_wait(1, t, k)
                                ins = mm(bank(mt % 4)[:, which * T + lo:which * T + hi], w[:, k, i * P:(i + 1) * P],
                                         hT[:, k, lo:hi], start=(k == 0), stop=(k == KD - 1))
                    if tiles is None or (TT - 1 in tiles and 1 in parts):
                        ins.then_inc(gu_ps, 1)

                def down(mt):
                    c, i = FIRST_FFN + mt // 2, mt % 2
                    d = gate_up_down(c)[2]
                    pe.wait_ge(hid_ready, mt + 1)
                    for t in range(TT):
                        for half in range(2):
                            ins = mm(bank(4 + 2 * t + half), ffn_hid[:, mt % 4, t * P:(t + 1) * P],
                                     d[:, i, half * 512:(half + 1) * 512], start=(mt == 0), stop=(mt == n_mt - 1))
                    ins.then_inc(ring_used if i else down_done, 1)

                def last_downs():
                    for t in range(TT):
                        for mt in range(n_mt - 4, n_mt):
                            if t == 0:
                                pe.wait_ge(hid_ready, mt + 1)
                            d = gate_up_down(FIRST_FFN + mt // 2)[2]
                            for half in range(2):
                                if t == 1 and mt == n_mt - 1 and half == 1:
                                    transpose_h(2, 0)
                                ins = mm(bank(4 + 2 * t + half), ffn_hid[:, mt % 4, t * P:(t + 1) * P],
                                         d[:, mt % 2, half * 512:(half + 1) * 512],
                                         start=False, stop=(mt == n_mt - 1))
                        ins.then_inc(*((ring_used, 2) if t else (ffn_t0, 1)))

                gate_up(0, (0,))
                gate_up(1, (0,), (0,))
                transpose_h(1, 1)
                gate_up(1, (0,), (1,))
                gate_up(0, (1,))
                gate_up(1, (1,))
                for mt in range(2, n_mt):
                    gate_up(mt)
                    if mt < n_mt - 2:
                        down(mt - 2)
                last_downs()

            mixer(0)
            dense_ffn()
            mixer(1)

            pe.wait_ge(router_landed, 16)
            rw = v3(routw, KD)
            for t in range(TT):
                if t:
                    transpose_h(3, 1)
                for k in range(KD):
                    hT_wait(3, t, k)
                    ins = mm(bank(4)[:, t * 8:(t + 1) * 8], hT[:, k, t * P:(t + 1) * P], rw[:, k, :],
                             start=(k == 0), stop=(k == KD - 1))
            ins.then_inc(router_ps, 1)
            pe.wait_ge(sel_ready, 1)
            r5 = bank(5)
            mm(r5[:, 0:8], ustrict, sel[:, 0:8], start=True, stop=True)
            mm(r5[:, 8:16], ustrict, sel[:, 8:16], start=True, stop=False)
            mm(r5[:, 8:16], ones, sel[:, 0:8], start=False, stop=True)
            mm(r5[:, 16:24], ones, sel[:, 0:8], start=True, stop=False)
            mm(r5[:, 16:24], ones, sel[:, 8:16], start=False, stop=True).then_inc(rank_ps, 1)
            pe.wait_ge(rounds_ready, 1)
            rounds = pe.value_load(rounds_i[0:1, 0:1], min_val=1, max_val=3)

            def gather(it, j):
                pe.wait_ge(onehot_ready, it * (2 * TT) + TT * (j + 1))
                for k in range(KD):
                    for t in range(TT):
                        for n, part in enumerate(h_part):
                            ins = mm(bank(4 + k // 4)[:, (k % 4) * SLOTS:(k % 4 + 1) * SLOTS],
                                     part[:, t, k * P:(k + 1) * P], onehot[j][:, t, :],
                                     start=(t == 0 and n == 0), stop=(t == 1 and n == 2))
                    if k % 4 == 3:
                        ins.then_inc(gather_ps, 1)
                for t in range(TT):
                    ins = mm(bank(6)[0:SLOTS, t * P:(t + 1) * P], onehot[j][:, t, :], ident_bf, start=True, stop=True)
                ins.then_inc(ohT_ps, 1)

            def m_gate_up(it, j, c):
                n = FIRST_MOE + j * MOE_CH + c
                chunk_landed(pe, n, it * (LANDED * 2 * MOE_CH // NSLOT))
                if c == 0:
                    pe.wait_ge(xg_ready, it * 4 + 2 * (j + 1))
                if c >= 2:
                    pe.wait_ge(mhid_ready, it * (2 * MOE_CH) + (j * MOE_CH + c - 1))
                g, u, _ = gate_up_down(n)
                for i in range(FC // P):
                    for which, w in enumerate((g, u)):
                        o = bank(c % 2)[:, (2 * which + i) * SLOTS:(2 * which + i + 1) * SLOTS]
                        for k in range(KD):
                            ins = mm(o, w[:, k, i * P:(i + 1) * P], xgT[:, k, :], start=(k == 0), stop=(k == KD - 1))
                ins.then_inc(mgu_ps, 1)

            def m_down(it, j, c, tail=False):
                d = gate_up_down(FIRST_MOE + j * MOE_CH + c)[2]
                pe.wait_ge(mhid_ready, it * (2 * MOE_CH) + (j * MOE_CH + c + 1))
                if tail and c == 0:
                    pe.wait_ge(y_act, it * 2 + j)
                    pe.wait_ge(y_dve, it * 2 + j)
                for i in range(FC // P):
                    for half in range(2):
                        ins = mm(bank(2 + half)[0:SLOTS, :], moe_hid[c % 2][:, i, :],
                                 d[:, i, half * 512:(half + 1) * 512],
                                 start=(c == 0 and i == 0), stop=(c == MOE_CH - 1 and i == 1))
                ins.then_inc(ring_used, 1)

            def scatter(it, j):
                pe.wait_ge(ohT_ready, it * 2 + (j + 1))
                pe.wait_ge(y_act, it * 2 + (j + 1))
                pe.wait_ge(y_dve, it * 2 + (j + 1))
                for t in range(TT):
                    for half in range(2):
                        ins = mm(bank((6, 4)[t] + half), onehotT[j][:, t * P:(t + 1) * P],
                                 y_tok[:, half * 512:(half + 1) * 512], start=True, stop=True)
                    ins.then_inc(scatter_ps, 1)

            def expert(it, j, tail, nxt):
                for c in range(MOE_CH):
                    m_gate_up(it, j, c)
                    if c:
                        m_down(it, j, c - 1, tail)
                    if tail and c == 0:
                        scatter(*tail)
                if nxt:
                    if tail:
                        for t in range(TT):
                            pe.wait_ge(moe_acc[t], it * 2 + j)
                    gather(*nxt)
                m_down(it, j, MOE_CH - 1)

            pe.wait_ge(part_ready, 3 * TT)
            pe.wait_ge(ident_ready, 1)
            with pe.Fori(0, rounds) as r:
                first = r * PAIRS
                gather(first, 0)
                expert(first, 0, None, (first, 1))
                with pe.Fori(0, PAIRS - 1) as pair:
                    it = r * PAIRS + pair
                    expert(it, 1, (it, 0), (it + 1, 0))
                    expert(it + 1, 0, (it, 1), (it + 1, 1))
                last = r * PAIRS + (PAIRS - 1)
                expert(last, 1, (last, 0), None)
                for t in range(TT):
                    pe.wait_ge(moe_acc[t], last * 2 + 1)
                scatter(last, 1)
                for t in range(TT):
                    pe.wait_ge(moe_acc[t], last * 2 + 2)

        @block.scalar
        def _(act):
            A = nc.scalar.activation

            nc.scalar.preload_act_table_set("natural_log_exp_and_others")
            act.dma_start(cst[:, 0:P], consts[:, 0:P]).then_inc(ident_landed, 16)
            act.dma_start(rows[R_MIX:R_MIX + 16, P:2 * P], norm_mix_pre.rearrange("l (k p) -> (l k) p", p=P))\
                .then_inc(rows_landed, 16)
            act.dma_start(rows[R_FFN:R_FFN + 16, P:2 * P], norm_ffn_pre.rearrange("l (k p) -> (l k) p", p=P))\
                .then_inc(rows_landed, 16)

            def pre_squares(u, t):
                for hf in range(2):
                    if u == 0:
                        act.wait_ge(x_landed[t], 16)
                    else:
                        act.wait_ge(x_ready, 2 * (TT * (u - 1) + t) + hf + 1)
                    A(act_junk[t][:, half(hf)], xv[:, t, half(hf)], ACT.Square, scale=D ** -0.5,
                      accum_out=ssx[:, 2 * t + hf:2 * t + hf + 1]).then_inc(ss_ready, 1)

            def normalise(u, t):
                act.wait_ge(rstd_ready, TT * u + t + 1)
                A(hv[:, t, half(1)], xv[:, t, half(1)], ACT.Copy, scale=rsx[:, t:t + 1]).then_inc(h_act, 1)

            def hT_tiles(u, row, t):
                act.wait_ge(hT_ps, 2 * (TT * u + t) + 2)
                if u == 0 and t == 0:
                    act.wait_ge(params_ready, 1)
                for k in range(4, KD):
                    A(hT[:, k, t * P:(t + 1) * P], bank(2 * t + 1)[:, (k - 4) * P:(k - 3) * P], ACT.Copy,
                      scale=prm[:, CONV_ROWS + row + k:CONV_ROWS + row + k + 1]).then_inc(hT_act, 1)

            def post_squares(u, wait, src, t):
                wait(act, t)
                for hf in range(2):
                    if hf and u < 3:
                        act.wait_ge(post_w, 2 * (TT * u + t) + 1)
                    A(act_junk[t][:, half(hf)], src(t, hf), ACT.Square, scale=D ** -0.5,
                      accum_out=ssx[:, 2 * t + hf:2 * t + hf + 1]).then_inc(post_ss, 1)

            def post_then_pre(u, wait, row):
                for t in range(TT):
                    post_squares(u, wait, bank_half, t)
                    pre_squares(u + 1, t)
                    normalise(u + 1, t)
                    hT_tiles(u + 1, row, t)

            def bank_half(t, hf):
                return bank(4 + 2 * t + hf)

            def conv_dst(m):
                return (qk[:, m, 1, :] if m < 4 else qk[:, m - 4, 0, :] if m < 8 else vT[:, m - 8, :])

            def mixer(L):
                if L == 0:
                    for t in range(TT):
                        pre_squares(0, t)
                    for t in range(TT):
                        normalise(0, t)
                    act.wait_ge(heads_landed, 32)
                    A(negA, headp[:, 0:2 * DN_H], ACT.Exp).then_inc(expA, 1)
                    for t in range(TT):
                        hT_tiles(0, R_MIX, t)
                nc.scalar.preload_act_table_set("natural_log_exp_and_others")
                act.wait_ge(gate_in, L + 1)
                A(sabs, aa, ACT.Abs).then_inc(gate_exp, 1)
                A(eb, ba.rearrange("p (t c) -> p t c", t=TT)[:, :, 0:4], ACT.Exp, scale=-1.0).then_inc(gate_exp, 1)
                act.wait_ge(gate_exp, 4 * L + 1)
                A(sln, sabs, ACT.Exp, scale=-1.0).then_inc(gate_exp, 1)
                act.wait_ge(gate_exp, 4 * L + 3)
                A(sabs, sln, ACT.Ln, bias=1.0).then_inc(gate_exp, 1)

                def conv_first(m):
                    act.wait_ge(*step_sem(L, m + 1))
                    w3 = L * CONV_K * CONV_T + 3 * CONV_T + m
                    A(conv_dst(m), bank(step_bank(m + 1))[:, 0:T], ACT.Copy, scale=prm[:, w3:w3 + 1])\
                        .then_inc(conv_base, 1)

                def silu(m):
                    act.wait_ge(conv_taps, 3 * (CONV_T * L + m + 1))
                    A(conv_dst(m), conv_dst(m), ACT.Silu).then_inc(conv_silu, 1)

                for m in range(2):
                    conv_first(m)
                act.wait_ge(gcum_ready, L + 1)
                A(eg, gsum[:, 0:8], ACT.Exp).then_inc(gexp_ready, 1)
                act.wait_ge(coef_ready, 5 * L + 1)
                A(egl, gdiff, ACT.Exp).then_inc(gexp_ready, 1)
                for m in range(2, 5):
                    conv_first(m)
                act.wait_ge(decay_in, 8 * (L + 1))
                A(DR_sb[:, :], DR_sb[:, :], ACT.Exp).then_inc(decay_exp, 1)
                for m in range(4):
                    silu(m)
                for m in range(5, CONV_T):
                    conv_first(m)
                    silu(m - 1)
                silu(CONV_T - 1)
                for t in range(TT):
                    act.wait_ge(*step_sem(L, S_Z + t))
                    A(hv[:, t, 0:DN_W], bank(step_bank(S_Z + t)), ACT.Silu).then_inc(z_gate, 1)
                nc.scalar.preload_act_table_set("natural_log_exp_and_others")

                def sb_copy(n):
                    kind, i = STEPS[n][0], STEPS[n][1]
                    act.wait_ge(*step_sem(L, n))
                    if kind == "sv":
                        dst, src = hv[:, i, DN_W:D], bank(step_bank(n))
                    else:
                        dst, src = (sq_v if kind == "sq" else sk_v)[:, i, :], bank(step_bank(n))[:, 0:T]
                    A(dst, src, ACT.Copy).then_inc(sb_copied, 1)

                if L:
                    act.wait_ge(x_ready, 4 * TT)
                for n in range(S_SB, S_FILL):
                    sb_copy(n)

                def m1_copy(l, g):
                    act.wait_ge(M1_ps, 2 * (LEVELS * L + l) + g + 1)
                    if l >= 2:
                        act.wait_ge(XTM_ps, 2 * (6 * L + l - 2) + g + 1)
                    A(M1[:, 4 * g:4 * g + 4, :], bank(g).rearrange("p (a b) -> p a b", a=4), ACT.Copy)\
                        .then_inc(M1_ready, 1)

                def sb_softplus_parts(h):
                    act.wait_ge(sbz_ready, SB_H * L + h + 1)
                    if h:
                        act.wait_ge(sb_softplus, SB_H * L + h)
                    n = 3 * (SB_H * L + h)
                    A(sbe[:, :], zm[:, h % 2, :], ACT.Abs).then_inc(sb_soft, 1)
                    act.wait_ge(sb_soft, n + 1)
                    A(sbe[:, :], sbe[:, :], ACT.Exp, scale=-1.0).then_inc(sb_soft, 1)
                    act.wait_ge(sb_soft, n + 2)
                    A(sbe[:, :], sbe[:, :], ACT.Ln, bias=1.0).then_inc(sb_soft, 1)

                def sb_weights(h):
                    act.wait_ge(sb_expo, SB_H * L + h + 1)
                    A(wT(h), zm[:, h % 2, :], ACT.Exp).then_inc(sb_weight, 1)

                for l in range(LEVELS):
                    sb_softplus_parts(l)
                    if l:
                        m1_copy(l, 0)
                        m1_copy(l, 1)
                    if l < LEVELS - 1:
                        sb_copy(S_FILL + l)
                    sb_weights(l)
                act.wait_ge(vnew_ps, 2 * L + 1)
                A(Vn[:, 0:4, :], bank(0).rearrange("p (a b) -> p a b", a=4), ACT.Copy).then_inc(vnew_ready, 1)
                sb_softplus_parts(SB_H - 1)
                act.wait_ge(state_ps, L + 1)
                A(S, bank(1).rearrange("p (a b) -> p a b", a=4), ACT.Copy).then_inc(state_ready, 1)
                sb_weights(SB_H - 1)
                sb_copy(N_STEPS - 1)
                act.wait_ge(vnew_ps, 2 * L + 2)
                A(Vn[:, 4:8, :], bank(0).rearrange("p (a b) -> p a b", a=4), ACT.Copy).then_inc(vnew_ready, 1)
                for t in range(TT):
                    act.wait_ge(sbo_ps, 2 * L + t + 1)
                    A((sbz, sbp)[t][:, 0:512], bank(6 + t), ACT.Square).then_inc(sb_sq, 1)
                for n, k, t, b in ((1, 4, 0, 4), (2, 4, 1, 6), (4, 0, 1, 3)):
                    act.wait_ge(mixT_ps, 4 * L + n)
                    col = CONV_ROWS + (R_SB if k else R_DN) + L
                    A(mixT[:, k:k + 4, t * P:(t + 1) * P], bank(b).rearrange("p (a b) -> p a b", a=4), ACT.Copy,
                      scale=prm[:, col:col + 1]).then_inc(mixT_act, 1)

                def through(eng, t):
                    eng.wait_ge(*((out_t0, L + 1) if t == 0 else (ring_used, FIRST_MIX[L] + N_MIX)))
                post_then_pre(2 * L, through, R_FFN + KD * L)

            def dense_ffn():
                for mt in range(D_FF // P):
                    act.wait_ge(gu_ps, mt + 1)
                    if mt >= 4:
                        act.wait_ge(hid_ready, mt - 3)
                    A(ffn_sg[:, mt % 4, :], bank(mt % 4)[:, 0:T], ACT.Silu).then_inc(sg_ready, 1)
                post_then_pre(1, ffn_through, R_MIX + KD)

            mixer(0)
            dense_ffn()
            mixer(1)

            def split(n, t):
                if n:
                    act.wait_ge(rest_ready, TT * (n - 1) + t + 1)
                else:
                    act.wait_ge(h_dve, TT * 3 + t + 1)
                    act.wait_ge(h_act, TT * 3 + t + 1)
                A(h_part[n][:, t, :], h_rest[:, t, :] if n else hv[:, t, :], ACT.Copy).then_inc(part_ready, 1)

            for n in range(2):
                for t in range(TT):
                    split(n, t)
            act.wait_ge(route_step, ROUTE_GD)
            A(ge, gd, ACT.Exp).then_inc(route_exp, 1)
            for t in range(TT):
                split(2, t)
            act.wait_ge(rounds_ready, 1)
            rounds = act.value_load(rounds_i[0:1, 0:1], min_val=1, max_val=3)

            def onehotT_copy(it, j):
                act.wait_ge(ohT_ps, it * 2 + (j + 1))
                A(onehotT[j], bank(6)[0:SLOTS, 0:T], ACT.Copy).then_inc(ohT_ready, 1)

            def y_copy(it, j):
                act.wait_ge(ring_used, it * (2 * MOE_CH) + (FIRST_MOE + (j + 1) * MOE_CH))
                A(y_tok[:, 0:512], bank(2)[0:SLOTS, :], ACT.Copy).then_inc(y_act, 1)

            def expert(it, j, tail, nxt):
                for c in range(MOE_CH):
                    act.wait_ge(mgu_ps, it * (2 * MOE_CH) + (j * MOE_CH + c + 1))
                    if c >= 2:
                        act.wait_ge(mhid_ready, it * (2 * MOE_CH) + (j * MOE_CH + c - 1))
                    A(moe_sg[c % 2], bank(c % 2)[:, 0:2 * SLOTS].rearrange("p (a b) -> p a b", a=2),
                      ACT.Silu).then_inc(msg_ready, 1)
                if nxt:
                    onehotT_copy(*nxt)
                y_copy(it, j)

            with act.Fori(0, rounds) as r:
                first = r * PAIRS
                onehotT_copy(first, 0)
                expert(first, 0, None, (first, 1))
                with act.Fori(0, PAIRS - 1) as pair:
                    it = r * PAIRS + pair
                    expert(it, 1, (it, 0), (it + 1, 0))
                    expert(it + 1, 0, (it, 1), (it + 1, 1))
                last = r * PAIRS + (PAIRS - 1)
                expert(last, 1, (last, 0), None)
            for t in range(TT):
                post_squares(3, lambda eng, t: eng.wait_ge(moe_acc[t], rounds * N_EXP),
                             lambda t, hf: moe_yv[:, t, half(hf)], t)

        @block.vector
        def _(dve):
            V = nc.vector

            def normalise(u, t):
                dve.wait_ge(rstd_ready, TT * u + t + 1)
                V.tensor_scalar(hv[:, t, half(0)], xv[:, t, half(0)], rsx[:, t:t + 1], None, ALU.mult)\
                    .then_inc(h_dve, 1)

            def hT_tiles(u, row, t):
                dve.wait_ge(hT_ps, 2 * (TT * u + t) + 1)
                V.tensor_tensor(hT[:, 0:4, t * P:(t + 1) * P], bank(2 * t).rearrange("p (a b) -> p a b", a=4),
                                bcl(prm[:, CONV_ROWS + row:CONV_ROWS + row + 4], P), ALU.mult).then_inc(hT_dve, 1)

            def post_weight(u, through, source, w, t):
                through(dve, t)
                for n, hf in enumerate((1, 0)):
                    if n and u < 3:
                        dve.wait_ge(post_ss, 2 * (TT * u + t) + 1)
                    V.tensor_tensor(post_tmp[t][:, half(hf)], source(t, hf), w[:, half(hf)], ALU.mult)\
                        .then_inc(post_w, 1)

            def residual(u, t):
                dve.wait_ge(post_rstd, TT * u + t + 1)
                dve.wait_ge(post_w, 2 * (TT * u + t + 1))
                for hf in range(2):
                    V.scalar_tensor_tensor(xv[:, t, half(hf)], post_tmp[t][:, half(hf)], rsx[:, t:t + 1],
                                           xv[:, t, half(hf)], ALU.mult, ALU.add).then_inc(x_ready, 1)

            def post_then_pre(u, through, w, row):
                for t in range(TT):
                    post_weight(u, through, bank_half, w, t)
                    residual(u, t)
                    normalise(u + 1, t)
                    hT_tiles(u + 1, row, t)

            def bank_half(t, hf):
                return bank(4 + 2 * t + hf)

            def conv_dst(m):
                return (qk[:, m, 1, :] if m < 4 else qk[:, m - 4, 0, :] if m < 8 else vT[:, m - 8, :])

            def mixer(L):
                if L == 0:
                    for t in range(TT):
                        normalise(0, t)
                    dve.wait_ge(params_ps, 1)
                    V.tensor_copy(prm[:, :], bank(7)[:, 0:CONV_ROWS + NORM_ROWS]).then_inc(params_ready, 1)
                    dve.wait_ge(params_ready, 1)
                    for t in range(TT):
                        hT_tiles(0, R_MIX, t)
                    dve.wait_ge(expA, 1)
                    V.tensor_scalar(negA, negA, -1.0, None, ALU.mult).then_inc(negA_ready, 1)
                    dve.wait_ge(negA_ready, 1)
                def taps(m):
                    dve.wait_ge(conv_base, CONV_T * L + m + 1)
                    for n, i in enumerate((2, 1, 0)):
                        s = 3 - i
                        if n:
                            dve.wait_ge(conv_taps, 3 * (CONV_T * L + m) + n)
                        w = L * CONV_K * CONV_T + i * CONV_T + m
                        V.scalar_tensor_tensor(conv_dst(m)[:, s:T], bank(step_bank(m + 1))[:, 0:T - s],
                                               prm[:, w:w + 1], conv_dst(m)[:, s:T], ALU.mult, ALU.add)\
                            .then_inc(conv_taps, 1)

                g0, c0 = 5 * L, 5 * L
                dve.wait_ge(*step_sem(L, 0))
                V.tensor_copy(ba, bank(4)[:, 0:16]).then_inc(ba_copied, 1)
                dve.wait_ge(ba_copied, L + 1)
                a_v = ba.rearrange("p (t c) -> p t c", t=TT)[:, :, 4:8]
                dtb = headp[:, (DEPTH + L) * DN_H:(DEPTH + L + 1) * DN_H]
                V.tensor_tensor(aa.rearrange("p (t c) -> p t c", t=TT), a_v, bcm(dtb, TT), ALU.add)\
                    .then_inc(gate_in, 1)
                dve.wait_ge(gate_in, L + 1)
                dve.wait_ge(gate_exp, 4 * (L + 1))
                V.scalar_tensor_tensor(spl, aa, 0.0, sabs, ALU.max, ALU.add).then_inc(gates_ready, 1)
                V.tensor_scalar(eb, eb, 1.0, None, ALU.add).then_inc(gates_ready, 1)
                dve.wait_ge(gates_ready, g0 + 2)
                V.reciprocal(beta, eb).then_inc(gates_ready, 1)
                V.tensor_tensor(g_log.rearrange("p (t c) -> p t c", t=TT), spl.rearrange("p (t c) -> p t c", t=TT),
                                bcm(negA[:, L * DN_H:(L + 1) * DN_H], TT), ALU.mult).then_inc(gates_ready, 1)
                taps(0)
                taps(1)
                dve.wait_ge(gcum_ps, L + 1)
                V.tensor_copy(gsum, bank(0)[:, 0:16]).then_inc(gcum_ready, 1)
                dve.wait_ge(gcum_ready, L + 1)
                V.tensor_tensor(gdiff, gsum[:, 8:12], gsum[:, 0:4], ALU.subtract).then_inc(coef_ready, 1)
                for m in range(2, 4):
                    taps(m)
                dve.wait_ge(bc_ps, 2 * L + 1)
                for pr in range(NPR):
                    V.tensor_scalar(DR[:, pr, :], bank(0, 2)[:, pr * P:(pr + 1) * P], gsum[:, pr:pr + 1], 0.0,
                                    ALU.subtract, ALU.min).then_inc(decay_in, 1)
                for m in range(4, 10):
                    taps(m)
                dve.wait_ge(norms_ps, L + 1)
                V.tensor_scalar(nsum, bank(2)[:, 0:16], EPS, None, ALU.add).then_inc(norms_sum, 1)
                taps(10)
                dve.wait_ge(gates_ready, g0 + 4)
                dve.wait_ge(norms_ready, L + 1)
                V.tensor_tensor(br, beta, rk, ALU.mult).then_inc(gates_ready, 1)
                V.tensor_scalar(coefq, rq, float(DN_D) ** -0.5, None, ALU.mult).then_inc(coef_ready, 1)
                dve.wait_ge(gexp_ready, 2 * (L + 1))
                dve.wait_ge(gates_ready, g0 + 5)
                V.tensor_tensor(scoef, eg[:, 4:8], br[:, 4:8], ALU.mult).then_inc(coef_ready, 1)
                dve.wait_ge(coef_ready, c0 + 3)
                V.tensor_scalar(scoef, scoef, -1.0, None, ALU.mult).then_inc(coef_ready, 1)
                V.tensor_tensor(kcoef, egl, rk[:, 0:4], ALU.mult).then_inc(coef_ready, 1)
                dve.wait_ge(coef_ready, c0 + 5)
                dve.wait_ge(kT_ps, L + 1)
                V.tensor_tensor(kend, bank(3).rearrange("p (a b) -> p a b", a=4), bcl(kcoef, P), ALU.mult)\
                    .then_inc(kend_ready, 1)
                taps(11)
                dve.wait_ge(bc_ps, 2 * L + 2)
                dve.wait_ge(decay_ready, 2 * (L + 1))
                for g in range(2):
                    V.tensor_tensor(DF[:, 4 * g:4 * g + 4, :], DR[:, 4 * g:4 * g + 4, :],
                                    bank(2 + g).rearrange("p (a b) -> p a b", a=4), ALU.mult)\
                        .then_inc(betadecay_ready, 1)
                for t in range(TT):
                    dve.wait_ge(v_ps, 2 * L + t + 1)
                    V.tensor_tensor(bv[:, 4 * t:4 * t + 4, :], bank(t).rearrange("p (a b) -> p a b", a=4),
                                    bcl(beta[:, 4 * t:4 * t + 4], P), ALU.mult).then_inc(bv_ready, 1)

                def sb_mask(h):
                    dve.wait_ge(sbz_ps, SB_H * L + h + 1)
                    if h >= 2:
                        dve.wait_ge(sb_weight, SB_H * L + h - 1)
                    V.scalar_tensor_tensor(zm[:, h % 2, :], bank(6)[:, 0:3 * P], SB_D ** -0.5, sbmask,
                                           ALU.mult, ALU.mult).then_inc(sbz_ready, 1)

                def sb_plus(h):
                    dve.wait_ge(sb_soft, 3 * (SB_H * L + h + 1))
                    if h >= 2:
                        dve.wait_ge(sbc_ps, SB_H * L + h - 1)
                    dve.wait_ge(sbz_ready, SB_H * L + h + 1)
                    V.scalar_tensor_tensor(sp[:, h % 2, :], zm[:, h % 2, :], 0.0, sbe[:, :], ALU.max, ALU.add)\
                        .then_inc(sb_softplus, 1)

                def sb_exponent(h):
                    dve.wait_ge(sbc_ps, SB_H * L + h + 1)
                    V.tensor_tensor(zm[:, h % 2, :], zm[:, h % 2, :], bank(6)[:, 0:3 * P], ALU.subtract)\
                        .then_inc(sb_expo, 1)

                dve.wait_ge(betadecay_ready, 2 * (L + 1))
                for g in range(2):
                    dve.wait_ge(kk_ps, 2 * L + g + 1)
                    two = ps[:, 2 * g:2 * g + 2, :].rearrange("p b (a k c) -> p (b a) k c", a=2, k=2)
                    V.tensor_tensor(LT[:, 4 * g:4 * g + 4, :], two[:, :, 0, :], DF[:, 4 * g:4 * g + 4, :],
                                    ALU.mult).then_inc(LT_ready, 1)
                    V.tensor_tensor(AT[:, 4 * g:4 * g + 4, :], two[:, :, 1, :], DR[:, 4 * g:4 * g + 4, :],
                                    ALU.mult).then_inc(AT_ready, 1)
                dve.wait_ge(LT_ready, 2 * (L + 1))
                for l in range(LEVELS):
                    sb_mask(l)
                    sb_plus(l)
                    if l:
                        sb_exponent(l)
                    for g in range(2):
                        s = slice(4 * g, 4 * g + 4)
                        if l == 0:
                            dve.wait_ge(M1_ps, 2 * LEVELS * L + g + 1)
                            V.tensor_tensor(X[:, s, :], bcm(ident, 4), bank(g).rearrange("p (a b) -> p a b", a=4),
                                            ALU.subtract).then_inc(X_ready, 1)
                            V.tensor_tensor(XT[:, s, :], bcm(ident, 4), BT[:, s, :], ALU.subtract)\
                                .then_inc(XT_ready, 1)
                            continue
                        if l < LEVELS - 1:
                            dve.wait_ge(XM_ps, 2 * (5 * L + l - 1) + g + 1)
                            dve.wait_ge(X_ready, 2 * (6 * L + l - 1) + g + 1)
                            V.tensor_tensor(X[:, s, :], X[:, s, :], bank(2 + g).rearrange("p (a b) -> p a b", a=4),
                                            ALU.subtract).then_inc(X_ready, 1)
                        dve.wait_ge(XTM_ps, 2 * (6 * L + l - 1) + g + 1)
                        dve.wait_ge(XT_ready, 2 * (LEVELS * L + l - 1) + g + 1)
                        V.tensor_tensor(XT[:, s, :], XT[:, s, :], bank(4 + g).rearrange("p (a b) -> p a b", a=4),
                                        ALU.subtract).then_inc(XT_ready, 1)
                    if l == 0:
                        sb_exponent(0)
                sb_mask(SB_H - 1)
                sb_plus(SB_H - 1)
                sb_exponent(SB_H - 1)
                dve.wait_ge(ks_ps, L + 1)
                V.tensor_tensor(RH1, bank(2).rearrange("p (a b) -> p a b", a=4), bcl(scoef, P), ALU.mult)\
                    .then_inc(rhs1_ready, 1)
                dve.wait_ge(rhs1_ready, 2 * L + 1)
                V.tensor_tensor(RH1, RH1, bv[:, 4:8, :], ALU.add).then_inc(rhs1_ready, 1)
                def head_sums(t):
                    dve.wait_ge(sb_sq, 2 * L + t + 1)
                    V.tensor_reduce(sss[:, 8 * t:8 * t + 8], v3((sbz, sbp)[t], SB_H, 0, 512), AX_X, ALU.add)\
                        .then_inc(sb_ss, 1)

                def head_scale(t):
                    dve.wait_ge(sb_rstd, 2 * L + t + 1)
                    dve.wait_ge(sbo_ps, 2 * (L + 1))
                    V.tensor_tensor(v3(h_sb, SB_H, t * D + DN_W, DN_W), bank(6 + t).rearrange("p (a b) -> p a b", a=SB_H),
                                    bcl(srs[:, 8 * t:8 * t + 8], SB_D), ALU.mult).then_inc(mixed_sb, 1)

                head_sums(0)
                head_scale(0)
                head_sums(1)
                dve.wait_ge(dno_ps, L + 1)
                c5 = 5 * L
                o0, o1 = v3(LT_sb, DN_H, 0, DN_W), v3(LT_sb, DN_H, DN_W, DN_W)
                V.tensor_tensor(o0, bank(1).rearrange("p (a b) -> p a b", a=4), bcl(coefq[:, 0:4], P), ALU.mult)\
                    .then_inc(dn_out, 1)
                V.tensor_tensor(o1, bank(3).rearrange("p (a b) -> p a b", a=4), bcl(eg[:, 4:8], P), ALU.mult)\
                    .then_inc(dn_out, 1)
                head_scale(1)
                dve.wait_ge(dn_out, c5 + 2)
                V.tensor_tensor(o1, o1, bank(2).rearrange("p (a b) -> p a b", a=4), ALU.add).then_inc(dn_out, 1)
                dve.wait_ge(dn_out, c5 + 3)
                V.tensor_tensor(o1, o1, bcl(coefq[:, 4:8], P), ALU.mult).then_inc(dn_out, 1)
                dve.wait_ge(dn_out, c5 + 4)
                V.tensor_tensor(AT_sb[:, :], LT_sb[:, :], LT_sb[:, :], ALU.mult).then_inc(dn_out, 1)
                dve.wait_ge(dn_out, c5 + 5)
                V.tensor_reduce(dss, v3(AT_sb, NPR), AX_X, ALU.add).then_inc(dn_rstd_in, 1)
                dve.wait_ge(dn_rstd, 2 * (L + 1))
                for t in range(TT):
                    V.tensor_tensor(v3(LT_sb, DN_H, t * DN_W, DN_W), v3(LT_sb, DN_H, t * DN_W, DN_W),
                                    bcl(drs[:, 4 * t:4 * t + 4], P), ALU.mult).then_inc(dn_rstd_in, 1)
                    dve.wait_ge(dn_rstd_in, 3 * L + t + 2)
                    V.tensor_tensor(hv[:, t, 0:DN_W], hv[:, t, 0:DN_W], LT_sb[:, t * DN_W:(t + 1) * DN_W],
                                    ALU.mult).then_inc(mixed_dn, 1)
                dve.wait_ge(mixT_ps, 4 * L + 3)
                col = CONV_ROWS + R_DN + L
                V.tensor_scalar(mixT[:, 0:4, 0:P], bank(0).rearrange("p (a b) -> p a b", a=4), prm[:, col:col + 1], None,
                                ALU.mult).then_inc(mixT_dve, 1)

                def through(eng, t):
                    eng.wait_ge(*((out_t0, L + 1) if t == 0 else (ring_used, FIRST_MIX[L] + N_MIX)))
                dve.wait_ge(wpost_landed, 16 * (L + 1))
                post_then_pre(2 * L, through, wpost, R_FFN + KD * L)

            def dense_ffn():
                for mt in range(D_FF // P):
                    dve.wait_ge(sg_ready, mt + 1)
                    if mt >= 4:
                        if mt % 2:
                            dve.wait_ge(ring_used, FIRST_FFN + (mt - 4) // 2 + 1)
                        else:
                            dve.wait_ge(down_done, (mt - 4) // 2 + 1)
                    V.tensor_tensor(ffn_hid[:, mt % 4, :], ffn_sg[:, mt % 4, :], bank(mt % 4)[:, T:2 * T], ALU.mult)\
                        .then_inc(hid_ready, 1)
                dve.wait_ge(wpostf_landed, 16)
                post_then_pre(1, ffn_through, wpost_ffn, R_MIX + KD)

            mixer(0)
            dense_ffn()
            mixer(1)

            n = [0]

            def step(*independent):
                for ins in independent:
                    n[0] += 1
                    ins.then_inc(route_step, 1)
                dve.wait_ge(route_step, n[0])

            def tv(ap):
                return ap.rearrange("p (t e) -> p t e", t=TT)

            def first_max(src, best, chosen):
                step(V.tensor_reduce(best, tv(src), AX_X, ALU.max))
                step(V.tensor_tensor(tv(cand), tv(src), bcl(best, N_EXP), ALU.is_equal))
                step(V.tensor_tensor(tv(cand), tv(cand), bcm(w8, TT), ALU.mult))
                step(V.tensor_reduce(mx, tv(cand), AX_X, ALU.max))
                step(V.tensor_tensor(tv(chosen), tv(cand), bcl(mx, N_EXP), ALU.is_equal))

            dve.wait_ge(router_ps, 1)
            step(V.tensor_copy(lg, bank(4)[:, 0:16]))
            step(V.tensor_reduce(m1, tv(lg), AX_X, ALU.max))
            first_max(lg, m1, sel1)
            step(V.scalar_tensor_tensor(lg2, sel1, -3.0e38, lg, ALU.mult, ALU.add))
            step(V.tensor_reduce(m2, tv(lg2), AX_X, ALU.max))
            first_max(lg2, m2, sel2)
            V.tensor_tensor(sel, sel1, sel2, ALU.add).then_inc(sel_ready, 1)
            step(V.tensor_tensor(gd, m2, m1, ALU.subtract))
            assert n[0] == ROUTE_GD
            dve.wait_ge(sel_ready, 1)
            dve.wait_ge(route_exp, 1)
            step(V.tensor_scalar(g1, ge, 1.0, None, ALU.add))
            step(V.reciprocal(g1, g1))
            step(V.tensor_tensor(g2, g1, ge, ALU.mult))
            step(V.tensor_tensor(tv(sel1), tv(sel1), bcl(g1, N_EXP), ALU.mult),
                 V.tensor_tensor(tv(sel2), tv(sel2), bcl(g2, N_EXP), ALU.mult))
            step(V.tensor_tensor(gate, sel1, sel2, ALU.add))
            dve.wait_ge(rank_ps, 1)
            step(V.tensor_reduce(cmax, bank(5)[:, 16:24], AX_X, ALU.max),
                 V.scalar_tensor_tensor(rank, bank(5)[:, 0:16], 1000.0, sel, ALU.add, ALU.mult))
            step(V.tensor_scalar(cgt, cmax, float(ROUND_LIMITS[0]), None, ALU.is_gt),
                 V.tensor_scalar(ctwo, cmax, float(ROUND_LIMITS[1]), 1.0, ALU.is_gt, ALU.add),
                 V.tensor_scalar(rank, rank, -1000.0, None, ALU.add))
            V.tensor_tensor(rounds_i[:, :], cgt, ctwo, ALU.add).then_inc(rounds_ready, 1)
            dve.wait_ge(rounds_ready, 1)
            dve.wait_ge(moe_zero, 1)
            rounds = dve.value_load(rounds_i[0:1, 0:1], min_val=1, max_val=3)
            wffn = prm[:, CONV_ROWS + R_FFN + KD:CONV_ROWS + R_FFN + 2 * KD]

            def choose(it, j, e):
                cr, cg = cur_rank[:, j * TT:(j + 1) * TT], cur_gate[:, j * TT:(j + 1) * TT]
                V.tensor_copy(cr, tv(rank)[:, :, bass.ds(e, 1)].rearrange("p t e -> p (t e)"))\
                    .then_inc(cur_ready, 1)
                V.tensor_copy(cg, tv(gate)[:, :, bass.ds(e, 1)].rearrange("p t e -> p (t e)"))\
                    .then_inc(cur_ready, 1)
                dve.wait_ge(cur_ready, it * 4 + 2 * (j + 1))
                for t in range(TT):
                    V.tensor_scalar(onehot[j][:, t, :], iota, cr[:, t:t + 1], None, ALU.is_equal)\
                        .then_inc(onehot_ready, 1)

            def gathered(it, j):
                for b in range(2):
                    dve.wait_ge(gather_ps, it * 4 + (2 * j + b + 1))
                    V.tensor_tensor(xgT[:, 4 * b:4 * b + 4, :],
                                    bank(4 + b)[:, 0:4 * SLOTS].rearrange("p (a b) -> p a b", a=4),
                                    bcl(wffn[:, 4 * b:4 * b + 4], SLOTS), ALU.mult).then_inc(xg_ready, 1)

            def y_copy(it, j):
                dve.wait_ge(ring_used, it * (2 * MOE_CH) + (FIRST_MOE + (j + 1) * MOE_CH))
                V.tensor_copy(y_tok[:, 512:D], bank(3)[0:SLOTS, :]).then_inc(y_dve, 1)

            def accumulate(it, j):
                for t in range(TT):
                    dve.wait_ge(scatter_ps, it * 4 + (2 * j + t + 1))
                    V.scalar_tensor_tensor(moe_yv[:, t, :], bank((6, 4)[t], 2),
                                           cur_gate[:, j * TT + t:j * TT + t + 1], moe_yv[:, t, :],
                                           ALU.mult, ALU.add).then_inc(moe_acc[t], 1)
                for t in range(TT):
                    dve.wait_ge(moe_acc[t], it * 2 + (j + 1))

            def expert(it, j, tail, nxt, nxt_e):
                for c in range(MOE_CH):
                    dve.wait_ge(msg_ready, it * (2 * MOE_CH) + (j * MOE_CH + c + 1))
                    if c >= 2:
                        dve.wait_ge(ring_used, it * (2 * MOE_CH) + (FIRST_MOE + j * MOE_CH + c - 1))
                    V.tensor_tensor(moe_hid[c % 2], moe_sg[c % 2],
                                    bank(c % 2)[:, 2 * SLOTS:4 * SLOTS].rearrange("p (a b) -> p a b", a=2),
                                    ALU.mult).then_inc(mhid_ready, 1)
                    if tail and c == 0:
                        accumulate(*tail)
                    if nxt and c == 2:
                        choose(*nxt, nxt_e)
                if nxt:
                    gathered(*nxt)
                y_copy(it, j)

            with dve.Fori(0, rounds) as r:
                first = r * PAIRS
                choose(first, 0, 0)
                gathered(first, 0)
                expert(first, 0, None, (first, 1), 1)
                with dve.Fori(0, PAIRS - 1) as pair:
                    it = r * PAIRS + pair
                    expert(it, 1, (it, 0), (it + 1, 0), pair * 2 + 2)
                    expert(it + 1, 0, (it, 1), (it + 1, 1), pair * 2 + 3)
                last = r * PAIRS + (PAIRS - 1)
                expert(last, 1, (last, 0), None, None)
                accumulate(last, 1)
                V.tensor_scalar(rank, rank, -float(SLOTS), None, ALU.add).then_inc(route_step, 1)
                dve.wait_ge(route_step, r + (n[0] + 1))
            dve.wait_ge(wpostf_landed, 32)
            for t in range(TT):
                post_weight(3, lambda eng, t: None, lambda t, hf: moe_yv[:, t, half(hf)], wpost_ffn, t)
                residual(3, t)

        @block.gpsimd
        def _(pool):
            G = nc.gpsimd
            pool.dma_start(headp[:, 0:8], dn_a_log.rearrange("l h -> (l h)").partition_broadcast(P))\
                .then_inc(heads_landed, 16)
            pool.dma_start(headp[:, 8:16], dn_dt_bias.rearrange("l h -> (l h)").partition_broadcast(P))\
                .then_inc(heads_landed, 16)
            G.memset(mhalf, -0.5).then_inc(half_ready, 1)
            pool.wait_ge(half_ready, 1)

            def rsqrt(dst, src, scale, mid, done, n_mid):
                G.tensor_scalar(src, src, scale, EPS, ALU.mult, ALU.add).then_inc(mid, 1)
                pool.wait_ge(mid, n_mid)
                G.tensor_tensor(dst, src, mhalf[:, 0:src.shape[1]], ALU.pow).then_inc(done, 1)

            def row_rstd(n, t, parts, mid, done):
                pool.wait_ge(parts, 2 * n - 1)
                G.tensor_scalar(ssum[:, t:t + 1], ssx[:, 2 * t:2 * t + 1], EPS, None, ALU.add).then_inc(mid, 1)
                pool.wait_ge(parts, 2 * n)
                pool.wait_ge(mid, 2 * n - 1)
                G.tensor_tensor(ssum[:, t:t + 1], ssum[:, t:t + 1], ssx[:, 2 * t + 1:2 * t + 2], ALU.add)\
                    .then_inc(mid, 1)
                pool.wait_ge(mid, 2 * n)
                G.tensor_tensor(rsx[:, t:t + 1], ssum[:, t:t + 1], mhalf[:, 0:1], ALU.pow).then_inc(done, 1)

            def pre_rstd(u, t):
                row_rstd(TT * u + t + 1, t, ss_ready, rstd_mean, rstd_ready)

            def post_rstd_of(u, t):
                row_rstd(TT * u + t + 1, t, post_ss, post_mean, post_rstd)

            def post_then_pre(u):
                for t in range(TT):
                    post_rstd_of(u, t)
                    pre_rstd(u + 1, t)

            def mixer(L):
                if L == 0:
                    for t in range(TT):
                        pre_rstd(0, t)
                    pool.dma_start(v3(routw, KD), router_w[0].rearrange("(k p) e -> p k e", p=P))\
                        .then_inc(router_landed, 16)
                pool.wait_ge(gcum_ready, L + 1)
                G.tensor_tensor(diag_g, bcm(ident, NPR), bcl(gsum[:, 0:8], P), ALU.mult).then_inc(diag_ready, 1)
                pool.wait_ge(decay_exp, L + 1)
                G.tensor_tensor(DR, DR, bcm(uinc, NPR), ALU.mult).then_inc(decay_ready, 1)
                for m in range(8):
                    pool.wait_ge(conv_silu, CONV_T * L + m + 1)
                    src = qk[:, m, 1, :] if m < 4 else qk[:, m - 4, 0, :]
                    if m == 0:
                        pool.wait_ge(params_ps, 1)
                    G.tensor_tensor(squares[:, m, :], src, src, ALU.mult).then_inc(qk_squares, 1)
                pool.wait_ge(norms_sum, L + 1)
                G.tensor_tensor(rn, nsum, mhalf, ALU.pow).then_inc(norms_ready, 1)
                pool.wait_ge(gates_ready, 5 * (L + 1))
                G.tensor_tensor(diag_b, bcm(ident, NPR), bcl(br, P), ALU.mult).then_inc(diag_ready, 1)
                pool.wait_ge(decay_ready, 2 * L + 1)
                pool.wait_ge(norms_ready, L + 1)
                G.tensor_tensor(DR, DR, bcl(rk, P), ALU.mult).then_inc(decay_ready, 1)

                def blocks(l, g):
                    s = slice(4 * g, 4 * g + 4)
                    pool.wait_ge(LT_ready, 2 * L + g + 1)
                    if l:
                        pool.wait_ge(M1_ps, 2 * (LEVELS * L + l - 1) + g + 1)
                        if l == 1:
                            pool.wait_ge(XT_ready, 2 * LEVELS * L + g + 1)
                    G.tensor_tensor(BT[:, s, :], LT[:, s, :], bcm(cst[:, C_LVL + l * P:C_LVL + (l + 1) * P], 4),
                                    ALU.mult).then_inc(BT_ready, 1)

                def sb_keep_mask(h):
                    pool.wait_ge(sb_softplus, SB_H * L + h + 1)
                    G.tensor_tensor(sp[:, h % 2, :], sp[:, h % 2, :], sbmask, ALU.mult).then_inc(sb_keep, 1)

                def sb_weight_mask(h):
                    pool.wait_ge(sb_weight, SB_H * L + h + 1)
                    G.tensor_tensor(wT(h), wT(h), sbmask, ALU.mult).then_inc(sb_wmask, 1)

                blocks(0, 0)
                blocks(0, 1)
                for l in range(LEVELS):
                    if l and l + 1 < LEVELS:
                        blocks(l + 1, 0)
                        blocks(l + 1, 1)
                    sb_keep_mask(l)
                    if l == 0:
                        blocks(1, 0)
                        blocks(1, 1)
                    sb_weight_mask(l)
                sb_keep_mask(SB_H - 1)
                sb_weight_mask(SB_H - 1)
                for t in range(TT):
                    pool.wait_ge(sb_ss, 2 * L + t + 1)
                    rsqrt(srs[:, 8 * t:8 * t + 8], sss[:, 8 * t:8 * t + 8], 1.0 / SB_D, sb_rstd_in, sb_rstd,
                          2 * L + t + 1)
                pool.wait_ge(sbo_ps, 2 * (L + 1))
                pool.dma_start(wpost[:, :], norm_mix_post[L].partition_broadcast(P)).then_inc(wpost_landed, 16)
                pool.wait_ge(dn_rstd_in, 3 * L + 1)
                G.tensor_scalar(dss, dss, 1.0 / DN_D, EPS, ALU.mult, ALU.add).then_inc(dn_rstd, 1)
                pool.wait_ge(dn_rstd, 2 * L + 1)
                G.tensor_tensor(drs, dss, mhalf[:, 0:8], ALU.pow).then_inc(dn_rstd, 1)
                pool.wait_ge(sbz_ps, SB_H * (L + 1))
                pool.dma_start(wpost_ffn, norm_ffn_post[L].partition_broadcast(P)).then_inc(wpostf_landed, 16)
                post_then_pre(2 * L)

            mixer(0)
            post_then_pre(1)
            mixer(1)
            G.memset(moe_y[:, :], 0.0).then_inc(moe_zero, 1)
            G.tensor_copy(ident_bf, ident).then_inc(ident_ready, 1)
            for n in range(2):
                for t in range(TT):
                    pool.wait_ge(part_ready, TT * n + t + 1)
                    if n:
                        pool.wait_ge(rest_ready, t + 1)
                    G.tensor_tensor(h_rest[:, t, :], h_rest[:, t, :] if n else hv[:, t, :], h_part[n][:, t, :],
                                    ALU.subtract).then_inc(rest_ready, 1)
            for t in range(TT):
                post_rstd_of(3, t)


_INS = ["x", "norm_mix_pre", "norm_mix_post", "norm_ffn_pre", "norm_ffn_post", "w_in", "conv_w", "dn_a_log",
        "dn_dt_bias", "dn_norm_w", "sb_norm_w", "w_out", "ffn_w_gate", "ffn_w_up", "ffn_w_down", "router_w",
        "moe_w_gate", "moe_w_up", "moe_w_down"]


def constants():
    c = np.zeros((P, C_ALL), np.float32)
    i, j = np.arange(P)[:, None], np.arange(P)[None, :]
    c[:, C_ID:C_ID + P] = i == j
    c[:, C_UINC:C_UINC + P] = i <= j
    c[:, C_TRI:C_TRI + P] = i >= j
    c[:, C_SB:C_SB + P] = i < j
    c[:, C_SB + P:C_SB + 2 * P] = 1.0
    c[:, C_SB + 2 * P:C_SB + 3 * P] = i < j
    for l in range(LEVELS):
        b = 1 << l
        c[:, C_LVL + l * P:C_LVL + (l + 1) * P] = (i // (2 * b) == j // (2 * b)) & (i % (2 * b) < b) & (j % (2 * b) >= b)
    c[:, C_IOTA:C_IOTA + SLOTS] = np.arange(SLOTS)
    c[:, C_W8:C_W8 + N_EXP] = N_EXP - np.arange(N_EXP)
    return c


def kernel(**inputs):
    import concourse.bacc as _bacc
    from concourse.bass_utils import run_bass_kernel_spmd as _run

    nc = _bacc.Bacc("TRN2", target_bir_lowering=False, num_devices=1)
    arrays, args = {}, []
    for name in _INS:
        a = np.ascontiguousarray(inputs[name])
        arrays[f"in_{name}"] = a
        args.append(nc.dram_tensor(f"in_{name}", a.shape, mybir.dt.from_np(a.dtype), kind="ExternalInput").ap())
    arrays["in_consts"] = constants()
    consts = nc.dram_tensor("in_consts", (P, C_ALL), F32, kind="ExternalInput").ap()
    out = nc.dram_tensor("out_x", (1, T, D), F32, kind="ExternalOutput").ap()
    build(nc, args[0], consts, *args[1:], out)
    r = _run(nc, [arrays], core_ids=[0])
    return r.results[0]["out_x"]
```
